# Optimizing a Trainium2 kernel written in Bass

```python
import functools
import jax, jax.numpy as jnp
from jax import lax
import numpy as np

D_MODEL = 1024
BATCH = 1
SEQ = 256
DEPTH = 1
DEC_BATCH = 1
DEC_SEQ = 4096
PAST_LEN = 512

GRID_W = 64
D_MIX = 1024
W_GRP = 256
HEAD_DIM = 64
N_HEADS_A = W_GRP // HEAD_DIM
WIN_H = 8
WIN_W = 16
CONV_W = 3
N_FOURIER = 4
N_HEADS_D = 4
DK = 64
DV = 64
GATE_RANK = 16
GLA_TAU = 16.0
CHUNK = 64
RMS_EPS = 1e-6
N_IN = 14 * W_GRP + 2 * GATE_RANK

kernel_name = 'hybrid_dit_na_conv_fnet_gla_step'

def rms_norm(x, g):
    xf = x.astype(jnp.float32)
    y = xf * lax.rsqrt(jnp.mean(xf * xf, axis=-1, keepdims=True) + RMS_EPS)
    return (y * g.astype(jnp.float32)).astype(x.dtype)

def to_heads(x, n):
    b, s, w = x.shape
    return x.reshape(b, s, n, w // n).transpose(0, 2, 1, 3)

def from_heads(x):
    b, n, s, d = x.shape
    return x.transpose(0, 2, 1, 3).reshape(b, s, n * d)

def adaln(cvec, w_mod_l, b_mod_l):
    m = jax.nn.silu(cvec) @ w_mod_l + b_mod_l
    shift, scale, gate = jnp.split(m, 3, axis=-1)
    return shift, scale, gate

def split_in(p):
    sizes = [W_GRP] * 14 + [GATE_RANK, GATE_RANK]
    idx = [int(i) for i in np.cumsum(sizes)[:-1]]
    return jnp.split(p, idx, axis=-1)

def attn_ctx(q, k, v):
    s = jnp.einsum('bhqd,bhkd->bhqk', q, k).astype(jnp.float32)
    p = jax.nn.softmax(s, axis=-1).astype(v.dtype)
    return jnp.einsum('bhqk,bhkd->bhqd', p, v)

def neighbourhood_attn(q, k, v, ck, cv, rpb_l):
    b, h, n, d = q.shape
    rows = n // GRID_W
    kh = min(WIN_H, rows)
    r = np.arange(rows)
    rs = np.clip(r - kh // 2, 0, rows - kh)
    row_idx = rs[:, None] + np.arange(kh)[None, :]
    dr = row_idx - r[:, None] + (WIN_H - 1)
    col = np.arange(GRID_W)
    cs = np.clip(col - WIN_W // 2, 0, GRID_W - WIN_W)
    col_ok = (col[None, :] >= cs[:, None]) & (col[None, :] < cs[:, None] + WIN_W)
    dc = np.clip(col[None, :] - col[:, None] + (WIN_W - 1), 0, 2 * WIN_W - 2)
    qg = q.reshape(b, h, rows, GRID_W, d)
    kg = k.reshape(b, h, rows, GRID_W, d)[:, :, row_idx]
    vg = v.reshape(b, h, rows, GRID_W, d)[:, :, row_idx]
    s_lat = jnp.einsum('bhrqd,bhrikd->bhrqik', qg, kg).astype(jnp.float32)
    bias = rpb_l[:, dr[:, None, :, None], dc[None, :, None, :]]
    s_lat = jnp.where(col_ok[:, None, :], s_lat + bias.astype(jnp.float32), -jnp.inf)
    s_ctx = jnp.einsum('bhrqd,bhcd->bhrqc', qg, ck).astype(jnp.float32)
    n_lat = kh * GRID_W
    s_all = jnp.concatenate([s_lat.reshape(b, h, rows, GRID_W, n_lat), s_ctx], axis=-1)
    p = jax.nn.softmax(s_all, axis=-1).astype(v.dtype)
    p_lat = p[..., :n_lat].reshape(b, h, rows, GRID_W, kh, GRID_W)
    o = (jnp.einsum('bhrqik,bhrikd->bhrqd', p_lat, vg)
         + jnp.einsum('bhrqc,bhcd->bhrqd', p[..., n_lat:], cv))
    return o.reshape(b, h, n, d)

def short_conv(bB, cB, hB, w):
    u = cB * hB
    up = jnp.pad(u, ((0, 0), (1, 1), (0, 0)))
    y = up[:, :-2] * w[0] + up[:, 1:-1] * w[1] + up[:, 2:] * w[2]
    return bB * y

def fourier_mix(u):
    b, s, w = u.shape
    ug = u.reshape(b, s, N_FOURIER, w // N_FOURIER).astype(jnp.float32)
    f = jnp.fft.fftn(ug, axes=(1, 3), norm='ortho').real
    return f.reshape(b, s, w).astype(u.dtype)

def gla_dir(q, k, v, log_a, s0):
    b, h, s, _ = q.shape
    nc = s // CHUNK
    rc = lambda t: t.reshape(b, h, nc, CHUNK, t.shape[-1])
    qc, kc, vc, gc = rc(q), rc(k), rc(v), rc(log_a)
    cum = jnp.cumsum(gc, axis=3)
    total = cum[:, :, :, -1:]
    q_dec = qc * jnp.exp(cum)
    k_inv = kc * jnp.exp(-cum)
    k_end = kc * jnp.exp(total - cum)
    causal = np.tril(np.ones((CHUNK, CHUNK), dtype=bool))
    att = jnp.where(causal, jnp.einsum('bhntk,bhnsk->bhnts', q_dec, k_inv), 0.0)
    o_intra = jnp.einsum('bhnts,bhnsv->bhntv', att, vc)
    upd = jnp.einsum('bhnsk,bhnsv->bhnkv', k_end, vc)
    decay = jnp.exp(total[:, :, :, 0])

    def step(state, inp):
        d_c, u_c = inp
        return d_c[..., None] * state + u_c, state

    s_fin, s_start = lax.scan(step, s0.astype(jnp.float32),
                              (jnp.moveaxis(decay, 2, 0), jnp.moveaxis(upd, 2, 0)))
    s_start = jnp.moveaxis(s_start, 0, 2)
    o_inter = jnp.einsum('bhntk,bhnkv->bhntv', q_dec, s_start)
    return (o_intra + o_inter).reshape(b, h, s, DV), s_fin

def gla_mixer(qD, kD, vD, aF, aB, up_f, b_f, up_b, b_b, s0_f, s0_b, gn):
    f32 = jnp.float32
    q = to_heads(qD, N_HEADS_D).astype(f32) * (DK ** -0.5)
    k = to_heads(kD, N_HEADS_D).astype(f32)
    v = to_heads(vD, N_HEADS_D).astype(f32)
    la_f = to_heads(jax.nn.log_sigmoid((aF @ up_f + b_f).astype(f32)) / GLA_TAU, N_HEADS_D)
    la_b = to_heads(jax.nn.log_sigmoid((aB @ up_b + b_b).astype(f32)) / GLA_TAU, N_HEADS_D)
    flip = lambda t: jnp.flip(t, axis=2)
    o_f, s_f = gla_dir(q, k, v, la_f, s0_f)
    o_b, s_b = gla_dir(flip(q), flip(k), flip(v), flip(la_b), s0_b)
    o = rms_norm(o_f + flip(o_b), gn)
    return from_heads(o).astype(qD.dtype), s_f, s_b

def trunk_layer(x, shift, scale, gate, attn_fn, s0_f, s0_b,
                norm_g_l, w_in_l, qn_l, kn_l, conv_l, up_f, b_f, up_b, b_b, gn_l, w_out_l):
    hN = rms_norm(x, norm_g_l) * (1.0 + scale) + shift
    p = hN @ w_in_l
    (qA, kA, vA, gA, bB, cB, hB, gB, uC, gC, qD, kD, vD, gD, aF, aB) = split_in(p)
    q = rms_norm(to_heads(qA, N_HEADS_A), qn_l) * (HEAD_DIM ** -0.5)
    k = rms_norm(to_heads(kA, N_HEADS_A), kn_l)
    v = to_heads(vA, N_HEADS_A)
    yA = from_heads(attn_fn(q, k, v)) * jax.nn.silu(gA)
    yB = short_conv(bB, cB, hB, conv_l) * jax.nn.silu(gB)
    yC = fourier_mix(uC) * jax.nn.silu(gC)
    oD, s_f, s_b = gla_mixer(qD, kD, vD, aF, aB, up_f, b_f, up_b, b_b, s0_f, s0_b, gn_l)
    yD = oD * jax.nn.silu(gD)
    y = jnp.concatenate([yA, yB, yC, yD], axis=-1) @ w_out_l
    return x + gate * y, k, v, s_f, s_b

def setup_inputs(seed: int = 0) -> dict:
    key = jax.random.key(seed)
    ks = jax.random.split(key, 24)
    nrm = lambda kk, shape, s: jax.random.normal(kk, shape, jnp.float32) * s
    return {
        'x_prompt': nrm(ks[0], (BATCH, SEQ, D_MODEL), 1.0),
        'x_sample': nrm(ks[1], (DEC_BATCH, DEC_SEQ, D_MODEL), 1.0),
        'cache_k': nrm(ks[2], (DEC_BATCH, DEPTH, N_HEADS_A, PAST_LEN, HEAD_DIM), 1.0),
        'cache_v': nrm(ks[3], (DEC_BATCH, DEPTH, N_HEADS_A, PAST_LEN, HEAD_DIM), 1.0),
        'state_gla': nrm(ks[4], (DEC_BATCH, DEPTH, 2, N_HEADS_D, DK, DV), 0.5),
        'c': nrm(ks[5], (DEC_BATCH, D_MODEL), 1.0),
        'c_ctx': nrm(ks[6], (D_MODEL,), 1.0),
        'norm_g': 1.0 + nrm(ks[7], (DEPTH, D_MODEL), 0.02),
        'w_mod': nrm(ks[8], (DEPTH, D_MODEL, 3 * D_MODEL), 0.5 * D_MODEL ** -0.5),
        'b_mod': nrm(ks[9], (DEPTH, 3 * D_MODEL), 0.02),
        'w_in': nrm(ks[10], (DEPTH, D_MODEL, N_IN), D_MODEL ** -0.5),
        'q_norm_g': 1.0 + nrm(ks[11], (DEPTH, HEAD_DIM), 0.02),
        'k_norm_g': 1.0 + nrm(ks[12], (DEPTH, HEAD_DIM), 0.02),
        'rpb': nrm(ks[13], (DEPTH, N_HEADS_A, 2 * WIN_H - 1, 2 * WIN_W - 1), 0.1),
        'conv_w': nrm(ks[14], (DEPTH, CONV_W, W_GRP), CONV_W ** -0.5),
        'gla_up_f': nrm(ks[15], (DEPTH, GATE_RANK, W_GRP), GATE_RANK ** -0.5),
        'gla_bias_f': nrm(ks[16], (DEPTH, W_GRP), 0.1),
        'gla_up_b': nrm(ks[17], (DEPTH, GATE_RANK, W_GRP), GATE_RANK ** -0.5),
        'gla_bias_b': nrm(ks[18], (DEPTH, W_GRP), 0.1),
        'gla_norm_g': 1.0 + nrm(ks[19], (DEPTH, DV), 0.02),
        'w_out': nrm(ks[20], (DEPTH, D_MIX, D_MODEL), D_MIX ** -0.5),
    }

def reference(x_prompt, x_sample, cache_k, cache_v, state_gla, c, c_ctx, norm_g, w_mod, b_mod,
              w_in, q_norm_g, k_norm_g, rpb, conv_w, gla_up_f, gla_bias_f, gla_up_b, gla_bias_b,
              gla_norm_g, w_out):
    def layer_params(l):
        return (norm_g[l], w_in[l], q_norm_g[l], k_norm_g[l], conv_w[l], gla_up_f[l],
                gla_bias_f[l], gla_up_b[l], gla_bias_b[l], gla_norm_g[l], w_out[l])

    x = x_prompt
    zero_state = jnp.zeros((x_prompt.shape[0], N_HEADS_D, DK, DV), jnp.float32)
    ks_, vs_, ss_ = [], [], []
    for l in range(DEPTH):
        shift, scale, gate = adaln(c_ctx, w_mod[l], b_mod[l])
        x, k, v, s_f, s_b = trunk_layer(x, shift, scale, gate, attn_ctx, zero_state, zero_state,
                                        *layer_params(l))
        ks_.append(k)
        vs_.append(v)
        ss_.append(jnp.stack([s_f, s_b], axis=1))
    y_prompt = x
    new_cache_k = jnp.stack(ks_, axis=1)
    new_cache_v = jnp.stack(vs_, axis=1)
    new_state_gla = jnp.stack(ss_, axis=1)

    xs = x_sample
    for l in range(DEPTH):
        shift, scale, gate = adaln(c, w_mod[l], b_mod[l])
        attn_fn = functools.partial(neighbourhood_attn, ck=cache_k[:, l], cv=cache_v[:, l],
                                    rpb_l=rpb[l])
        xs, _, _, _, _ = trunk_layer(xs, shift[:, None, :], scale[:, None, :], gate[:, None, :],
                                     attn_fn, state_gla[:, l, 0], state_gla[:, l, 1],
                                     *layer_params(l))
    y_sample = xs
    return (y_prompt, y_sample, new_cache_k, new_cache_v, new_state_gla)


_drawn_inputs = setup_inputs


def setup_inputs(seed=0):
    import zlib

    import numpy as np

    out = dict(_drawn_inputs(seed))
    spreads = {}
    factors = {'cache_k': 8.0,
     'cache_v': 8.0,
     'state_gla': 8.0,
     'q_norm_g': 8.0,
     'k_norm_g': 3.13,
     'rpb': 8.0,
     'gla_norm_g': 8.0}
    for name, (base, spread) in spreads.items():
        noise = np.random.default_rng([zlib.crc32(name.encode()), seed]).standard_normal(out[name].shape)
        drawn = base * np.exp(spread * noise) if base else spread * noise
        out[name] = __import__('jax').numpy.asarray(drawn.astype(out[name].dtype))
    for name, factor in factors.items():
        out[name] = (out[name] * factor).astype(out[name].dtype)
    return out
```

```python
from contextlib import ExitStack, contextmanager

import numpy as np

import concourse.bass as bass
from concourse import mybir

F32 = mybir.dt.float32
F32R = mybir.dt.float32r
ACT = mybir.ActivationFunctionType
ALU = mybir.AluOpType
AX = mybir.AxisListType

P = 128
DM = 1024
K8 = DM // P
N_PROMPT = 256
N_GRID = 4096
N_TOK = N_GRID + N_PROMPT
GRID_W = 64
ROWS = N_GRID // GRID_W
PAST = 512
W_GRP = 256
HD = 64
NH = 4
WIN_H = 8
WIN_W = 16
RANK = 16
TAU = 16.0
EPS = 1e-6
N_IN = 14 * W_GRP + 2 * RANK
TILES = 4
STEP = TILES * P
GRID_STEPS = N_GRID // STEP
NEG = -1e30

QA, KA, VA, GA, BB, CB, HB, GB, UC, GC, QD, KD, VD, GD, AF = (W_GRP * n for n in range(15))
P1_QK, P1_V, P1_G, P1_QKD, P1_VD, P1_GD, P1_A = 0, 512, 768, 1024, 1536, 1792, 2048
P1_W = P1_A + 2 * RANK


@contextmanager
def stage(nc):
    with ExitStack() as ctx:
        sems = []

        def sem(name):
            sems.append(nc.alloc_semaphore(name=name))
            return sems[-1]

        yield ctx, sem
        ctx.close()
        nc.clear_and_free_semaphores(sems)
        nc.all_engine_barrier()


def ahead(eng, *values):
    for v in values:
        if not isinstance(v, int):
            eng.compute_val(v)


def steps(eng):
    with eng.Fori(1, GRID_STEPS + 1) as n:
        yield n - 1, (n - 1) * STEP, TILES, 0
    yield GRID_STEPS, N_GRID, N_PROMPT // P, 1


def modulation_stage(nc, io, keep):
    with stage(nc) as (ctx, new_sem):
        sb = lambda name, shape, dt=F32: ctx.enter_context(nc.sbuf_tensor(name, shape, dt))
        sem = lambda name: new_sem(name)
        craw = sb("m_craw", [P, 2, K8])
        cact = sb("m_cact", [P, K8, 2])
        ng = sb("m_ng", [P, K8])
        bm = sb("m_bm", [P, 2, K8])
        wm = sb("m_wm", [P, 3, K8, DM])
        bg = sb("m_bg", [2, DM])
        grow = sb("m_grow", [2, DM])
        col = sb("m_col", [P, 2, K8, 2])
        ps_col = ctx.enter_context(nc.psum_tensor("m_pscol", [P, 2, K8, 2], F32))
        ps_row = ctx.enter_context(nc.psum_tensor("m_psrow", [2, 2, 512], F32))
        small_in, silu_c, cols_mm, rows_mm, cols_sb, rows_sb, out_done, idn = (
            sem(f"m_{n}") for n in ("small_in", "silu_c", "cols_mm", "rows_mm", "cols_sb", "rows_sb", "out", "idn"))
        w_in_sem = [sem(f"m_w{n}") for n in range(3)]
        block = ctx.enter_context(nc.Block())

        @block.sync
        def _(sp):
            sp.dma_start(craw[:, 0, :], io["c"].rearrange("a (p k) -> (a p) k", p=P)).then_inc(small_in, 16)
            sp.dma_start(craw[:, 1, :], io["c_ctx"].rearrange("(p k) -> p k", p=P)).then_inc(small_in, 16)
            wv = io["w_mod"].rearrange("a (p k) n -> (a p) k n", p=P)
            for n in range(3):
                sp.dma_start(wm[:, n], wv[:, :, n * DM:(n + 1) * DM]).then_inc(w_in_sem[n], 16)
            sp.wait_ge(rows_sb, 2)
            sp.dma_start(io["gates"], grow[:, :]).then_inc(out_done, 16)
            sp.wait_ge(out_done, 16)

        @block.gpsimd
        def _(pool):
            pool.memset(keep["ident"][:, :], 0.0).then_inc(idn, 1)
            pool.wait_ge(idn, 1)
            pool.affine_select(out=keep["ident"][:, :], in_=keep["ident"][:, :], compare_op=ALU.not_equal,
                               fill=1.0, base=0, pattern=[[-1, P]], channel_multiplier=1).then_inc(idn, 1)
            pool.wait_ge(idn, 2)

        @block.scalar
        def _(act):
            act.dma_start(ng[:, :], io["norm_g"].rearrange("a (p k) -> (a p) k", p=P)).then_inc(small_in, 16)
            for n in range(2):
                act.dma_start(bm[:, n, :], io["b_mod"][:, n * DM:(n + 1) * DM].rearrange("a (p k) -> (a p) k", p=P)).then_inc(small_in, 16)
            for n in range(2):
                act.dma_start(bg[n:n + 1, :], io["b_mod"][:, 2 * DM:3 * DM]).then_inc(small_in, 16)
            act.wait_ge(small_in, 7 * 16)
            act.activation(cact[:, :, :], craw[:, :, :].rearrange("p j k -> p k j"), ACT.Silu).then_inc(silu_c, 1)

        @block.tensor
        def _(pe):
            pe.wait_ge(silu_c, 1)
            for n in range(2):
                pe.wait_ge(w_in_sem[n], 16)
                for k in range(K8):
                    for kk in range(K8):
                        last = pe.matmul(ps_col[:, n, k, :], wm[:, n, kk, k::K8], cact[:, kk, :],
                                         start=(kk == 0), stop=(kk == K8 - 1))
            last.then_inc(cols_mm, 1)
            pe.wait_ge(w_in_sem[2], 16)
            for half in range(2):
                for kk in range(K8):
                    last = pe.matmul(ps_row[:, half, :], cact[:, kk, :], wm[:, 2, kk, half * 512:(half + 1) * 512],
                                     start=(kk == 0), stop=(kk == K8 - 1))
            last.then_inc(rows_mm, 1)

        @block.vector
        def _(dve):
            dve.wait_ge(small_in, 7 * 16)
            dve.wait_ge(cols_mm, 1)
            for n in range(2):
                for j in range(2):
                    dve.tensor_tensor(col[:, n, :, j], ps_col[:, n, :, j], bm[:, n, :], ALU.add).then_inc(cols_sb, 1)
            dve.wait_ge(cols_sb, 4)
            for j in range(2):
                dve.tensor_copy(keep["shift"][:, j, :], col[:, 0, :, j]).then_inc(cols_sb, 1)
                dve.scalar_tensor_tensor(keep["scale"][:, j, :], col[:, 1, :, j], 1.0, ng[:, :], ALU.add, ALU.mult).then_inc(cols_sb, 1)
            dve.wait_ge(cols_sb, 8)
            dve.tensor_scalar(keep["scale"][:, :, :], keep["scale"][:, :, :], DM ** 0.5, None, ALU.mult).then_inc(cols_sb, 1)
            dve.wait_ge(cols_sb, 9)
            dve.wait_ge(rows_mm, 1)
            for half in range(2):
                dve.tensor_tensor(grow[:, half * 512:(half + 1) * 512], ps_row[:, half, :],
                                  bg[:, half * 512:(half + 1) * 512], ALU.add).then_inc(rows_sb, 1)


def split_weights(nc, sp, act, dve, src, pieces, stage, w_hi, w_lo, loaded, hi_done, lo_done):
    for n, (k, c0, wd, a0) in enumerate(pieces):
        slot = stage[n % 2][:, 0:wd]
        if sp:
            if n >= 2:
                sp.wait_ge(lo_done, n - 1)
            sp.dma_start(slot, src[:, k, c0:c0 + wd]).then_inc(loaded[n % 2], 16)
        if act:
            act.wait_ge(loaded[n % 2], 16 * (n // 2 + 1))
            act.activation(w_hi[:, k, a0:a0 + wd], slot, ACT.Copy).then_inc(hi_done, 1)
        if dve:
            dve.wait_ge(hi_done, n + 1)
            dve.tensor_tensor(w_lo[:, k, a0:a0 + wd], slot, w_hi[:, k, a0:a0 + wd], ALU.subtract).then_inc(lo_done, 1)


def weight_pieces(blocks):
    out, at = [], 0
    for c0, n in blocks:
        out += [(k, c0, n, at) for k in range(K8)]
        at += n
    return out


def product(pe, out, left_hi, left_lo, right_hi, right_lo):
    for k in range(K8):
        pe.matmul(out, left_hi(k), right_hi(k), start=(k == 0), stop=False)
        pe.matmul(out, left_hi(k), right_lo(k), start=False, stop=False)
        last = pe.matmul(out, left_lo(k), right_hi(k), start=False, stop=(k == K8 - 1))
    return last


def projection_stage(nc, io, keep, which):
    pre = f"p{which}_"
    blocks = [(QA, 1024), (QD, 1024), (AF, 2 * RANK)] if which == 0 else [(BB, 1024), (UC, 512)]
    pieces = weight_pieces(blocks)
    width = sum(n for _, n in blocks)
    NB = 2
    GROUPS = 5 * TILES if which == 0 else 10 + TILES
    assert GROUPS % NB == 0
    PER_BANK = GROUPS // NB

    def freed(i, n):
        return i * PER_BANK + n // NB + 2

    with stage(nc) as (ctx, new_sem):
        sb = lambda name, shape, dt=F32: ctx.enter_context(nc.sbuf_tensor(pre + name, shape, dt))
        sem = lambda name: new_sem(pre + name)
        w_hi = sb("w_hi", [P, K8, width], F32R)
        w_lo = sb("w_lo", [P, K8, width], F32R)
        h_hi = sb("h_hi", [P, K8, STEP], F32R)
        h_lo = sb("h_lo", [P, K8, STEP], F32R)
        hf = sb("hf", [P, 2, STEP])
        xb = sb("xb", [P, TILES, DM])
        squares = hf[:, :, :].rearrange("p b t -> p (b t)")
        ss = sb("ss", [P, TILES])
        rstd = sb("rstd", [P, TILES])
        half_pow = sb("half_pow", [P, 8])
        eps = sb("eps", [P, 9])
        ps_t = [ctx.enter_context(nc.psum_tensor(pre + f"ps_t{b}", [P, 512], F32)) for b in range(2)]
        ps_m = [ctx.enter_context(nc.psum_tensor(pre + f"ps_m{b}", [P, 512], F32)) for b in range(NB)]
        stage_w = [xb[:, b, :] for b in range(2)]

        x_in = [sem(f"x_in{j}") for j in range(TILES)]
        w_ld = [sem(f"w_ld{j}") for j in range(2)]
        w_hi_done, w_lo_done = sem("w_hi_done"), sem("w_lo_done")
        small_in, pool_own, dve_own = sem("small_in"), sem("pool_own"), sem("dve_own")
        x_sq, x_rstd, x_normed, x_turned = sem("x_sq"), sem("x_rstd"), sem("x_normed"), sem("x_turned")
        h_done, h_hi_done, h_lo_done = sem("h_done"), sem("h_hi_done"), sem("h_lo_done")
        mm_done = sem("mm_done")
        bank_free = [sem(f"bank_free{b}") for b in range(NB)]
        if which == 0:
            rows = sb("rows", [P, 2, P1_W])
            qk_sq_sb = hf[:, 0, :]
            qss = sb("qss", [P, 8])
            qr = sb("qr", [P, 8])
            gqk = sb("gqk", [P, 2 * NH * HD])
            qkt = sb("qkt", [P, 2, 4, P])
            ps_q = ctx.enter_context(nc.psum_tensor(pre + "ps_q", [P, 4, P], F32))
            qk_sq, qk_ss, qk_r, qk_ready = sem("qk_sq"), sem("qk_ss"), sem("qk_r"), sem("qk_ready")
            qkt_mm, qkt_sb = sem("qkt_mm"), sem("qkt_sb")
            rows_sent = [sem(f"rows_sent{b}") for b in range(2)]
            qkt_sent = [sem(f"qkt_sent{b}") for b in range(2)]
        else:
            ft = sb("ft", [P, 4, STEP])
            ut = sb("ut", [P, 2, STEP])
            gst = sb("gst", [P, 2, 2, W_GRP])
            dft = sb("dft", [P, 2 * P])
            gcs = sb("gcs", [P, 2, W_GRP])
            ps_g = [ctx.enter_context(nc.psum_tensor(pre + f"ps_g{b}", [P, 2, 2, P], F32)) for b in range(2)]
            ft_sent = [sem(f"ft_sent{b}") for b in range(4)]
            dft_mm, dft_sb = sem("dft_mm"), sem("dft_sb")
            gate_sent = [sem(f"gate_sent{b}") for b in range(2)]
            dft_sent = [sem(f"dft_sent{b}") for b in range(2)]
        block = ctx.enter_context(nc.Block())

        @block.sync
        def _(sp):
            if which == 0:
                sp.dma_start(gqk[:, 0:HD], io["q_norm_g"].broadcast_to([P, HD])).then_inc(small_in, 16)
                sp.dma_start(gqk[:, 4 * HD:5 * HD], io["k_norm_g"].broadcast_to([P, HD])).then_inc(small_in, 16)
            else:
                sp.dma_start(dft[:, :], io["dft64"]).then_inc(small_in, 16)
            split_weights(nc, sp, None, None, io["w_in"].rearrange("a (p k) n -> (a p) k n", p=P), pieces, stage_w,
                          w_hi, w_lo, w_ld, w_hi_done, w_lo_done)
            sp.wait_ge(w_lo_done, len(pieces))
            for b in range(2):
                if which == 0:
                    sp.sem_inc(rows_sent[b], 16)
                    sp.sem_inc(qkt_sent[b], 16)
                else:
                    sp.sem_inc(gate_sent[b], 16)
                    sp.sem_inc(dft_sent[b], 16)
            if which == 1:
                for b in range(4):
                    sp.sem_inc(ft_sent[b], 16)
            for i, tok, nt, of in steps(sp):
                src = io["x_prompt" if of else "x_sample"].rearrange("a t d -> (a t) d")
                at = lambda j: tok + j * P
                if which == 0:
                    ahead(sp, *[v for j in range(nt) for v in (i * TILES + j + 2, i * TILES + j + 1,
                                                               freed(i, 5 * j + 3), freed(i, 5 * j + 4), at(j) * 4)])
                else:
                    ahead(sp, *[freed(i, n) for n in range(14)], *[i * TILES + j + 3 for j in range(nt)], tok * 4)
                sp.wait_ge(x_turned, i * K8 + 1)
                for j in range(nt):
                    sp.dma_start(xb[:, j, :], src[bass.ds(j * P if of else at(j), P), :]).then_inc(x_in[j], 16)
                if which == 0:
                    for j in range(nt):
                        sp.wait_ge(qkt_sb, i * TILES + j + 2)
                        sp.dma_start(io["qkt"][:, :, bass.ds(at(j), P)].rearrange("b p t -> p b t"),
                                     qkt[:, j % 2]).then_inc(qkt_sent[j % 2], 16)
                        sp.wait_ge(qk_ready, i * TILES + j + 1)
                        for n in (5 * j + 3, 5 * j + 4):
                            sp.wait_ge(bank_free[n % NB], freed(i, n))
                        sp.dma_start(io["p1"][bass.ds(at(j), P), :], rows[:, j % 2, :]).then_inc(rows_sent[j % 2], 16)
                else:
                    for f in range(8):
                        sp.wait_ge(bank_free[f % NB], freed(i, f))
                        sp.dma_start(io["bt"][f, :, bass.ds(tok, nt * P)], ft[:, f % 4, 0:nt * P]).then_inc(ft_sent[f % 4], 16)
                    for j in range(nt):
                        sp.wait_ge(bank_free[j % NB], freed(i, 10 + j))
                        sp.dma_start(io["gc"][bass.ds(at(j), P), :], gcs[:, j % 2, :]).then_inc(gate_sent[j % 2], 16)
                    for j in range(nt):
                        sp.wait_ge(dft_sb, i * TILES + j + 3)
                        sp.dma_start(io["g"][:, bass.ds(at(j), P), :].rearrange("r t c -> t r c"),
                                     gst[:, j % 2]).then_inc(dft_sent[j % 2], 16)
            per_slot = N_TOK // P // 2 + 1
            for b in range(2):
                if which == 0:
                    sp.wait_ge(rows_sent[b], 16 * per_slot)
                    sp.wait_ge(qkt_sent[b], 16 * per_slot)
                else:
                    sp.wait_ge(gate_sent[b], 16 * per_slot)
                    sp.wait_ge(dft_sent[b], 16 * per_slot)
            if which == 1:
                for b in range(4):
                    sp.wait_ge(ft_sent[b], 16 * (2 * (GRID_STEPS + 1) + 1))

        @block.gpsimd
        def _(pool):
            pool.memset(half_pow[:, :], -0.5).then_inc(pool_own, 1)
            pool.memset(eps[:, 0:1], DM * EPS).then_inc(pool_own, 1)
            pool.memset(eps[:, 1:9], HD * EPS).then_inc(pool_own, 1)
            pool.wait_ge(pool_own, 3)
            per = TILES * (2 if which == 0 else 1)
            for i, tok, nt, _ in steps(pool):
                for j in range(nt):
                    pool.wait_ge(x_sq, i * TILES + j + 1)
                    pool.tensor_tensor(rstd[:, j:j + 1], ss[:, j:j + 1], eps[:, 0:1], ALU.add).then_inc(pool_own, 1)
                    pool.wait_ge(pool_own, i * per + j + 4)
                    pool.tensor_tensor(rstd[:, j:j + 1], rstd[:, j:j + 1], half_pow[:, 0:1], ALU.pow).then_inc(x_rstd, 1)
                if which == 0:
                    for j in range(nt):
                        pool.wait_ge(qk_ss, i * TILES + j + 2)
                        pool.tensor_tensor(qss[:, :], qss[:, :], eps[:, 1:9], ALU.add).then_inc(pool_own, 1)
                        pool.wait_ge(pool_own, i * per + nt + j + 4)
                        pool.tensor_tensor(qr[:, :], qss[:, :], half_pow[:, :], ALU.pow).then_inc(qk_r, 1)

        @block.scalar
        def _(act):
            split_weights(nc, None, act, None, None, pieces, stage_w, w_hi, w_lo, w_ld, w_hi_done, w_lo_done)
            act.sem_inc(bank_free[0], 1)
            act.sem_inc(bank_free[1], 1)
            if which == 0:
                act.sem_inc(qkt_sb, 1)
            for i, tok, nt, _ in steps(act):
                mm = lambda n: act.wait_ge(mm_done, i * GROUPS + n + 1)
                for j in range(nt):
                    act.wait_ge(x_in[j], 16 * i + 16)
                    if j:
                        act.wait_ge(x_sq, i * TILES + j)
                    elif which == 0:
                        act.wait_ge(qk_ss, i * TILES + 1)
                    act.activation(squares, xb[:, j, :], ACT.Square, accum_out=ss[:, j:j + 1]).then_inc(x_sq, 1)
                for k in range(K8):
                    act.wait_ge(h_done, i * K8 + k + 1)
                    act.activation(h_hi[:, k, 0:nt * P], hf[:, k % 2, 0:nt * P], ACT.Copy).then_inc(h_hi_done, 1)
                if which == 0:
                    for j in range(nt):
                        n = 5 * j
                        mm(n)
                        act.wait_ge(qk_ss, i * TILES + j + 1)
                        act.activation(qk_sq_sb, ps_m[n % NB][:, :], ACT.Square).then_inc(qk_sq, 1)
                        mm(n + 1)
                        act.wait_ge(rows_sent[j % 2], 16 * (2 * i + j // 2) + 16)
                        act.activation(rows[:, j % 2, P1_V:P1_G], ps_m[(n + 1) % NB][:, 0:W_GRP], ACT.Copy)
                        act.activation(rows[:, j % 2, P1_G:P1_QKD], ps_m[(n + 1) % NB][:, W_GRP:512], ACT.Silu).then_inc(bank_free[(n + 1) % NB], 1)
                        mm(n + 3)
                        act.activation(rows[:, j % 2, P1_VD:P1_GD], ps_m[(n + 3) % NB][:, 0:W_GRP], ACT.Copy)
                        act.activation(rows[:, j % 2, P1_GD:P1_A], ps_m[(n + 3) % NB][:, W_GRP:512], ACT.Silu).then_inc(bank_free[(n + 3) % NB], 1)
                        act.wait_ge(qkt_mm, i * TILES + j + 1)
                        act.wait_ge(qkt_sent[j % 2], 16 * (2 * i + j // 2) + 16)
                        act.activation(qkt[:, j % 2], ps_q[:, :, :], ACT.Copy).then_inc(qkt_sb, 1)
                else:
                    for f in (1, 3, 5, 6, 7):
                        mm(f)
                        act.wait_ge(ft_sent[f % 4], 16 * (2 * i + f // 4) + 16)
                        act.activation(ft[:, f % 4, 0:nt * P], ps_m[f % NB][:, 0:nt * P],
                                       ACT.Silu if f >= 6 else ACT.Copy).then_inc(bank_free[f % NB], 1)
                    for j in range(nt):
                        mm(10 + j)
                        act.wait_ge(gate_sent[j % 2], 16 * (2 * i + j // 2) + 16)
                        act.activation(gcs[:, j % 2, :], ps_m[j % NB][:, 0:W_GRP], ACT.Silu).then_inc(bank_free[j % NB], 1)

        @block.tensor
        def _(pe):
            pe.sem_inc(x_turned, 1)
            pe.wait_ge(w_lo_done, len(pieces))
            if which == 1:
                pe.wait_ge(small_in, 16)
            for i, tok, nt, _ in steps(pe):
                for k in range(K8):
                    if k >= 2:
                        pe.wait_ge(h_done, i * K8 + k - 1)
                    for j in range(nt):
                        if k == 0:
                            pe.wait_ge(x_normed, i * TILES + j + 1)
                        last = pe.transpose(ps_t[k % 2][:, j * P:(j + 1) * P], xb[:, j, k::K8], keep["ident"][:, :])
                    last.then_inc(x_turned, 1)
                pe.wait_ge(h_lo_done, i * K8 + K8)

                def group(n, out, left, right):
                    pe.wait_ge(bank_free[n % NB], freed(i, n) - 1)
                    product(pe, out, lambda k: left[0](k), lambda k: left[1](k), lambda k: right[0](k),
                            lambda k: right[1](k)).then_inc(mm_done, 1)

                def h_part(a, b):
                    return [lambda k: h_hi[:, k, a:b], lambda k: h_lo[:, k, a:b]]

                def w_part(a, b):
                    return [lambda k: w_hi[:, k, a:b], lambda k: w_lo[:, k, a:b]]

                if which == 0:
                    for j in range(nt):
                        for g in range(5):
                            n = 5 * j + g
                            a, b = 512 * g, min(512 * g + 512, width)
                            group(n, ps_m[n % NB][:, 0:b - a], h_part(j * P, (j + 1) * P), w_part(a, b))
                        pe.wait_ge(qk_ready, i * TILES + j + 1)
                        pe.wait_ge(qkt_sb, i * TILES + j + 1)
                        for b in range(4):
                            last = pe.transpose(ps_q[:, b, :], rows[:, j % 2, b * P:(b + 1) * P], keep["ident"][:, :])
                        last.then_inc(qkt_mm, 1)
                else:
                    for f in range(10):
                        group(f, ps_m[f % NB][:, 0:nt * P], w_part(f * P, (f + 1) * P), h_part(0, nt * P))
                    for j in range(nt):
                        group(10 + j, ps_m[j % NB][:, 0:W_GRP], h_part(j * P, (j + 1) * P), w_part(1280, 1536))
                    for f in (8, 9):
                        pe.wait_ge(bank_free[f % NB], freed(i, f))
                    for j in range(nt):
                        pe.wait_ge(dft_sb, i * TILES + j + 1)
                        for f in range(2):
                            last = pe.matmul(ps_g[j % 2][:, f], ut[:, f, j * P:(j + 1) * P],
                                             dft[:, :].rearrange("p (r c) -> p r c", r=2), start=True, stop=True)
                        last.then_inc(dft_mm, 1)

        @block.vector
        def _(dve):
            split_weights(nc, None, None, dve, None, pieces, stage_w, w_hi, w_lo, w_ld, w_hi_done, w_lo_done)
            if which == 0:
                dve.wait_ge(small_in, 32)
                dve.tensor_scalar(gqk[:, NH * HD:(NH + 1) * HD], gqk[:, NH * HD:(NH + 1) * HD], HD ** 0.5, None,
                                  ALU.mult).then_inc(dve_own, 1)
                dve.wait_ge(dve_own, 1)
                for h in range(1, NH):
                    dve.tensor_copy(gqk[:, (NH + h) * HD:(NH + h + 1) * HD], gqk[:, NH * HD:(NH + 1) * HD]).then_inc(dve_own, 1)
                    dve.tensor_copy(gqk[:, h * HD:(h + 1) * HD], gqk[:, 0:HD]).then_inc(dve_own, 1)
                dve.wait_ge(dve_own, 2 * NH - 1)
                dve.sem_inc(qk_ss, 1)
            else:
                dve.sem_inc(dft_sb, 2)
            for i, tok, nt, of in steps(dve):
                mm = lambda n: dve.wait_ge(mm_done, i * GROUPS + n + 1)
                for j in range(nt):
                    dve.wait_ge(x_rstd, i * TILES + j + 1)
                    dve.tensor_scalar(xb[:, j, :], xb[:, j, :], rstd[:, j:j + 1], None, ALU.mult).then_inc(x_normed, 1)

                def low(k):
                    dve.wait_ge(h_hi_done, i * K8 + k + 1)
                    dve.tensor_tensor(h_lo[:, k, 0:nt * P], hf[:, k % 2, 0:nt * P], h_hi[:, k, 0:nt * P],
                                      ALU.subtract).then_inc(h_lo_done, 1)

                for k in range(K8):
                    dve.wait_ge(x_turned, i * K8 + k + 2)
                    if k >= 2:
                        dve.wait_ge(h_lo_done, i * K8 + k - 1)
                    dve.tensor_scalar(hf[:, k % 2, 0:nt * P], ps_t[k % 2][:, 0:nt * P], keep["scale"][:, of, k:k + 1],
                                      keep["shift"][:, of, k:k + 1], ALU.mult, ALU.add).then_inc(h_done, 1)
                    if k:
                        low(k - 1)
                low(K8 - 1)
                if which == 0:
                    for j in range(nt):
                        n = 5 * j
                        dve.wait_ge(qk_sq, i * TILES + j + 1)
                        dve.tensor_reduce(qss[:, :], qk_sq_sb.rearrange("t (h d) -> t h d", h=8), AX.X, ALU.add).then_inc(qk_ss, 1)
                        dve.wait_ge(rows_sent[j % 2], 16 * (2 * i + j // 2) + 16)
                        dve.wait_ge(qk_r, i * TILES + j + 1)
                        qk = rows[:, j % 2, 0:512]
                        dve.tensor_tensor(qk.rearrange("t (h d) -> t h d", h=8), ps_m[n % NB][:, :].rearrange("t (h d) -> t h d", h=8),
                                          qr[:, :].unsqueeze(2).broadcast_to([P, 8, HD]), ALU.mult).then_inc(bank_free[n % NB], 1)
                        dve.wait_ge(bank_free[n % NB], freed(i, n))
                        dve.tensor_tensor(qk, qk, gqk[:, :], ALU.mult).then_inc(qk_ready, 1)
                        mm(n + 2)
                        dve.tensor_copy(rows[:, j % 2, P1_QKD:P1_VD], ps_m[(n + 2) % NB][:, :]).then_inc(bank_free[(n + 2) % NB], 1)
                        mm(n + 4)
                        dve.tensor_copy(rows[:, j % 2, P1_A:P1_W], ps_m[(n + 4) % NB][:, 0:2 * RANK]).then_inc(bank_free[(n + 4) % NB], 1)
                else:
                    for f in (0, 2, 4):
                        mm(f)
                        dve.wait_ge(ft_sent[f % 4], 16 * (2 * i + f // 4) + 16)
                        dve.tensor_copy(ft[:, f % 4, 0:nt * P], ps_m[f % NB][:, 0:nt * P]).then_inc(bank_free[f % NB], 1)
                    for f in range(2):
                        mm(8 + f)
                        dve.tensor_copy(ut[:, f, 0:nt * P], ps_m[f % NB][:, 0:nt * P]).then_inc(bank_free[f % NB], 1)
                    for j in range(nt):
                        dve.wait_ge(dft_mm, i * TILES + j + 1)
                        dve.wait_ge(dft_sent[j % 2], 16 * (2 * i + j // 2) + 16)
                        dve.tensor_copy(gst[:, j % 2].rearrange("t r (f c) -> t f r c", f=2), ps_g[j % 2][:, :, :, :]).then_inc(dft_sb, 1)


def attention_rows(eng):
    start = lambda r: min(max(r - WIN_H // 2, 0), ROWS - WIN_H) if r < ROWS else None
    last = ROWS + N_PROMPT // GRID_W - 1
    lo, hi = WIN_H // 2, ROWS - WIN_H // 2
    for r in range(lo):
        yield r, start(r), r + 1, start(r + 1)
    with eng.Fori(lo, hi) as r:
        yield r, r - WIN_H // 2, r + 1, r + 1 - WIN_H // 2
    for r in range(hi, last + 1):
        yield r, start(r), r + 1 if r < last else None, start(r + 1)


def attention_stage(nc, io, keep):
    W = WIN_H * GRID_W
    CH = W // P
    CC = PAST // P
    NDR = 2 * WIN_H - 1
    with stage(nc) as (ctx, new_sem):
        sb = lambda name, shape, dt=F32: ctx.enter_context(nc.sbuf_tensor("a_" + name, shape, dt))
        sem = lambda name: new_sem("a_" + name)
        k_t = sb("k_t", [P, 2, N_GRID])
        v2 = sb("v2", [P, ROWS - 1, W_GRP])
        kp_t = sb("kp_t", [P, 2, N_PROMPT])
        vp = sb("vp", [P, N_PROMPT // P, W_GRP])
        ck = sb("ck", [P, CC, NH, HD])
        ck_t = sb("ck_t", [P, 2, PAST])
        cv = sb("cv", [P, CC, NH, HD])
        bias = sb("bias", [P, 2, NDR, GRID_W])
        q2 = sb("q2", [P, 2, P])
        s_sb = [sb(f"s_sb{p}", [P, W + PAST]) for p in range(2)]
        p_t = [sb(f"p_t{p}", [P, W + PAST]) for p in range(2)]
        o_sb = sb("o_sb", [P, 2, HD])
        max_c, max_w, neg_m, total, r_total = (sb(n, [P, 2]) for n in ("max_c", "max_w", "neg_m", "total", "r_total"))
        sums = sb("sums", [P, 2, 2])
        psum = lambda name, cols: ctx.enter_context(nc.psum_tensor("a_" + name, [P, cols], F32))
        ps_w = [psum(f"ps_w{p}", 512) for p in range(2)]
        ps_c = [psum(f"ps_c{p}", 512) for p in range(2)]
        ps_t = [psum(f"ps_t{h}", 512) for h in range(2)]
        ps_o = [psum(f"ps_o{p}", 512) for p in range(2)]
        (kv_in, c_in, toep, toep_in, toep_out, bias_in, bias_set, q_zero, ckt_mm, ckt_sb, s_done, maxc_done, w_done,
         max_done, exp_done, sum_done, rsum_done, t_done, t0_sb, t1_sb, pv_done, o_done, o_sent, cache_out) = (sem(n) for n in (
             "kv_in", "c_in", "toep", "toep_in", "toep_out", "bias_in", "bias_set", "q_zero", "ckt_mm", "ckt_sb", "s_done",
             "maxc_done", "w_done", "max_done", "exp_done", "sum_done", "rsum_done", "t_done", "t0_sb", "t1_sb", "pv_done",
             "o_done", "o_sent", "cache_out"))
        q_in = [sem(f"q_in{p}") for p in range(2)]
        pad = v2[0:GRID_W, :, :].rearrange("p a b -> p (a b)")[:, 0:NH * NDR * P].rearrange("q (n x) -> q n x", x=P)
        block = ctx.enter_context(nc.Block())

        @block.sync
        def _(sp):
            for p in range(2):
                sp.dma_start(k_t[:, p, :], io["qkt"][2 + p, :, 0:N_GRID]).then_inc(kv_in, 16)
                sp.dma_start(kp_t[:, p, :], io["qkt"][2 + p, :, N_GRID:N_TOK]).then_inc(kv_in, 16)
            sp.dma_start(vp[:, :, :], io["p1"][N_GRID:N_TOK, P1_V:P1_G].rearrange("(m p) c -> p m c", p=P)).then_inc(kv_in, 16)
            sp.wait_ge(toep, 1)
            sp.dma_start(pad[:, :, 48:48 + 2 * WIN_W - 1],
                         io["rpb"].rearrange("a h r x -> a (h r) x").broadcast_to([GRID_W, NH * NDR, 2 * WIN_W - 1])).then_inc(toep_in, 16)
            sp.wait_ge(toep_in, 16)
            sp.dma_start(io["toep"].rearrange("n q x -> q n x"), pad).then_inc(toep_out, 16)
            sp.wait_ge(toep_out, 16)
            flat = io["toep"].rearrange("n q x -> n (q x)")[:, GRID_W - 1:GRID_W - 1 + GRID_W * (P - 1)]
            skew = flat.rearrange("n (q x) -> q n x", x=P - 1)[:, :, 0:GRID_W]
            for h in range(NH):
                sp.dma_start(bias[(h % 2) * 64:(h % 2) * 64 + 64, h // 2], skew[:, h * NDR:(h + 1) * NDR, :]).then_inc(bias_in, 16)
            v_rows = io["p1"][0:N_GRID, P1_V:P1_G].rearrange("(j t) c -> t j c", t=GRID_W)
            for h in range(2):
                sp.dma_start(v2[h * GRID_W:(h + 1) * GRID_W, :, :], v_rows[:, h:h + ROWS - 1, :]).then_inc(kv_in, 16)
            for name, c0 in (("new_cache_k", W_GRP), ("new_cache_v", P1_V)):
                sp.dma_start(io[name].rearrange("a l h s d -> (a l h) s d"),
                             io["p1"][N_GRID:N_TOK, c0:c0 + W_GRP].rearrange("s (h d) -> h s d", h=NH)).then_inc(cache_out, 16)

            def load_q(r, p):
                for h in range(2):
                    sp.dma_start(q2[h * HD:(h + 1) * HD, p, h * HD:(h + 1) * HD],
                                 io["qkt"][p, h * HD:(h + 1) * HD, bass.ds(r * GRID_W, GRID_W)]).then_inc(q_in[p], 16)

            sp.wait_ge(q_zero, 1)
            for p in range(2):
                load_q(0, p)
            sp.sem_inc(o_sent, 16)
            for r, _, nxt, _ in attention_rows(sp):
                ahead(sp, 2 * r + 1, 2 * r + 2, (r + 1) * GRID_W * 4)
                if nxt is not None:
                    for p in range(2):
                        sp.wait_ge(s_done, 2 * r + p + 1)
                        load_q(r + 1, p)
                sp.wait_ge(o_done, 4 * r + 8)
                sp.dma_start(io["ya"][bass.ds(r, 1)].rearrange("a t p d -> (a t) p d"), o_sb[:, :, :]).then_inc(o_sent, 16)
            sp.wait_ge(o_sent, 16 * (N_TOK // GRID_W + 1))
            sp.wait_ge(cache_out, 32)

        @block.gpsimd
        def _(pool):
            pool.memset(pad, 0.0).then_inc(toep, 1)
            pool.memset(q2[:, :, :], 0.0).then_inc(q_zero, 1)
            for buf, name in ((ck, "cache_k"), (cv, "cache_v")):
                for m in range(CC):
                    pool.dma_start(buf[:, m, :, :], io[name][0, 0, :, m * P:(m + 1) * P, :].rearrange("h p d -> p h d")).then_inc(c_in, 16)
            pool.wait_ge(bias_in, 64)
            n = 0
            for h in range(2):
                for c0, c1, base, step, chan in ((0, GRID_W - WIN_W, WIN_W // 2, 1, -1), (WIN_W, GRID_W, WIN_W // 2 - 1 - WIN_W, -1, 1)):
                    part = bias[h * 64:(h + 1) * 64, :, :, c0:c1].rearrange("q p r x -> q (p r) x")
                    if n:
                        pool.wait_ge(bias_set, n)
                    pool.affine_select(out=part, in_=part, compare_op=ALU.is_ge, fill=NEG, base=base,
                                       pattern=[[0, 2 * NDR], [step, c1 - c0]], channel_multiplier=chan).then_inc(bias_set, 1)
                    n += 1

        @block.scalar
        def _(act):
            act.sem_inc(t1_sb, 1)

            def exps(r, rs, p):
                act.wait_ge(max_done, 2 * r + p + 1)
                if rs is None:
                    act.activation(s_sb[p][:, 0:N_PROMPT], ps_w[p][:, 0:N_PROMPT], ACT.Exp, bias=neg_m[:, p:p + 1],
                                   accum_out=total[:, p:p + 1]).then_inc(exp_done, 1)
                else:
                    act.activation(s_sb[p][:, 0:W], s_sb[p][:, 0:W], ACT.Exp, bias=neg_m[:, p:p + 1], accum_out=sums[:, p, 0:1])
                    act.activation(s_sb[p][:, W:], ps_c[p][:, :], ACT.Exp, bias=neg_m[:, p:p + 1],
                                   accum_out=sums[:, p, 1:2]).then_inc(exp_done, 1)

            for p in range(2):
                exps(0, 0, p)
            for r, rs, nxt, nrs in attention_rows(act):
                for p in range(2):
                    if rs is not None:
                        act.wait_ge(t_done, 4 * r + 2 * p + 2)
                        act.activation(p_t[p][:, W:], ps_t[1][:, :], ACT.Copy).then_inc(t1_sb, 1)
                    if nxt is not None:
                        exps(r + 1, nrs, p)

        @block.tensor
        def _(pe):
            pe.wait_ge(c_in, 2 * CC * 16)
            for p in range(2):
                for m in range(CC):
                    last = pe.transpose(ps_t[p][:, m * P:(m + 1) * P], ck[:, m, 2 * p:2 * p + 2, :].rearrange("k h d -> k (h d)"),
                                        keep["ident"][:, :])
            last.then_inc(ckt_mm, 1)
            pe.wait_ge(kv_in, 7 * 16)

            def scores(r, rs, p):
                pe.wait_ge(q_in[p], 32 * r + 32)
                if rs is None:
                    pe.matmul(ps_w[p][:, 0:N_PROMPT], q2[:, p, :], kp_t[:, p, :], start=True, stop=True).then_inc(s_done, 1)
                else:
                    pe.matmul(ps_w[p][:, :], q2[:, p, :], k_t[:, p, bass.ds(rs * GRID_W, W)], start=True, stop=True)
                    pe.matmul(ps_c[p][:, :], q2[:, p, :], ck_t[:, p, :], start=True, stop=True).then_inc(s_done, 1)

            pe.wait_ge(ckt_sb, 2)
            for p in range(2):
                scores(0, 0, p)
            for r, rs, nxt, nrs in attention_rows(pe):
                for p in range(2):
                    n_t = 2 if rs is None else 1
                    pe.wait_ge(exp_done, 2 * r + p + 1)
                    pe.wait_ge(t0_sb, 2 * r + p + 1)
                    chunks = N_PROMPT // P if rs is None else CH
                    for m in range(chunks):
                        last = pe.transpose(ps_t[0][:, m * P:(m + 1) * P], s_sb[p][:, m * P:(m + 1) * P], keep["ident"][:, :])
                    last.then_inc(t_done, n_t)
                    if rs is not None:
                        pe.wait_ge(t1_sb, 2 * r + p + 1)
                        for m in range(CC):
                            last = pe.transpose(ps_t[1][:, m * P:(m + 1) * P], s_sb[p][:, W + m * P:W + (m + 1) * P], keep["ident"][:, :])
                        last.then_inc(t_done, 1)
                    if nxt is not None:
                        scores(r + 1, nrs, p)
                    pe.wait_ge(t0_sb, 2 * r + p + 2)
                    pe.wait_ge(o_done, 4 * r + 2 * p + 2)
                    if rs is not None:
                        pe.wait_ge(t1_sb, 2 * r + p + 2)
                    todo = []
                    if rs is not None:
                        todo += [(CH + m, cv[:, m, :, :].rearrange("k h d -> k (h d)")) for m in range(CC)]
                        todo += [(m, v2[:, bass.ds(rs + 2 * m, 1), :].rearrange("k a c -> k (a c)")) for m in range(CH)]
                    else:
                        todo += [(m, vp[:, m, :]) for m in range(N_PROMPT // P)]
                    for n, (m, v) in enumerate(todo):
                        last = pe.matmul(ps_o[p][:, 0:P], p_t[p][:, m * P:(m + 1) * P], v[:, 2 * p * HD:2 * p * HD + P],
                                         start=(n == 0), stop=(n == len(todo) - 1))
                    last.then_inc(pv_done, 1)

        @block.vector
        def _(dve):
            dve.wait_ge(ckt_mm, 1)
            for p in range(2):
                dve.tensor_copy(ck_t[:, p, :], ps_t[p][:, :]).then_inc(ckt_sb, 1)
            dve.sem_inc(t0_sb, 1)
            dve.sem_inc(o_done, 4)
            dve.wait_ge(bias_set, 4)

            def maxima(r, rs, p):
                dve.wait_ge(s_done, 2 * r + p + 1)
                if rs is None:
                    dve.tensor_reduce(neg_m[:, p:p + 1], ps_w[p][:, 0:N_PROMPT], AX.X, ALU.max, negate=True).then_inc(max_done, 1)
                    return
                dve.tensor_reduce(max_c[:, p:p + 1], ps_c[p][:, :], AX.X, ALU.max).then_inc(maxc_done, 1)
                at = WIN_H // 2 - 1 if not isinstance(rs, int) else rs - r + WIN_H - 1
                dve.tensor_tensor_reduce(out=s_sb[p][:, 0:W].rearrange("k (r x) -> k r x", r=WIN_H), in0=ps_w[p][:, :].rearrange("k (r x) -> k r x", r=WIN_H), in1=bias[:, p, at:at + WIN_H, :],
                                         scale=1.0, scalar=NEG, op0=ALU.add, op1=ALU.max,
                                         accum_out=max_w[:, p:p + 1]).then_inc(w_done, 1)
                dve.wait_ge(maxc_done, 2 * r + p + 1)
                dve.wait_ge(w_done, 2 * r + p + 1)
                dve.tensor_scalar(neg_m[:, p:p + 1], max_w[:, p:p + 1], max_c[:, p:p + 1], -1.0, ALU.max, ALU.mult).then_inc(max_done, 1)

            for p in range(2):
                maxima(0, 0, p)
            for r, rs, nxt, nrs in attention_rows(dve):
                for p in range(2):
                    u = 2 * r + p
                    dve.wait_ge(exp_done, u + 1)
                    if rs is not None:
                        dve.tensor_tensor(total[:, p:p + 1], sums[:, p, 0:1], sums[:, p, 1:2], ALU.add).then_inc(sum_done, 1)
                        dve.wait_ge(sum_done, u + 1)
                    dve.reciprocal(r_total[:, p:p + 1], total[:, p:p + 1]).then_inc(rsum_done, 1)
                    dve.wait_ge(t_done, 2 * u + 1)
                    cols = N_PROMPT if rs is None else W
                    dve.tensor_copy(p_t[p][:, 0:cols], ps_t[0][:, 0:cols]).then_inc(t0_sb, 1)
                    if nxt is not None:
                        maxima(r + 1, nrs, p)
                    dve.wait_ge(pv_done, u + 1)
                    dve.wait_ge(rsum_done, u + 1)
                    dve.wait_ge(o_sent, 16 * r + 16)
                    for h in range(2):
                        dve.tensor_scalar(o_sb[h * 64:h * 64 + 64, p, :], ps_o[p][h * 64:h * 64 + 64, h * HD:(h + 1) * HD],
                                          r_total[h * 64:h * 64 + 64, p:p + 1], None, ALU.mult).then_inc(o_done, 1)


def gla_steps(eng):
    grid = N_GRID // P
    with eng.Fori(1, grid // 2 + 1) as n:
        for s in range(2):
            yield n * 2 - 2 + s, s, n * 2 - 2 + s, grid + 1 - s - n * 2
    for s in range(2):
        yield grid + s, s, grid + s, grid + 1 - s


def gla_stage(nc, io, keep):
    C = P // 2
    with stage(nc) as (ctx, new_sem):
        sb = lambda name, shape, dt=F32: ctx.enter_context(nc.sbuf_tensor("d_" + name, shape, dt))
        sem = lambda name: new_sem("d_" + name)
        both = lambda name, shape: [sb(f"{name}{d}", shape) for d in range(2)]
        tri = sb("tri", [P, 2, 2, P])
        mask = sb("mask", [P, 2, P])
        ind = sb("ind", [P, 2])
        up = sb("up", [33, 2, W_GRP])
        aug = both("aug", [33, P])
        qkv = [[sb(f"qkv{d}{s}", [P, 3 * W_GRP]) for s in range(2)] for d in range(2)]
        at = [[sb(f"a{d}{s}", [P, RANK]) for s in range(2)] for d in range(2)]
        low = both("low", [P, W_GRP])
        nab = both("nab", [P, W_GRP])
        ez = both("ez", [P, W_GRP])
        lz = both("lz", [P, W_GRP])
        la = both("la", [P, W_GRP])
        e_cum, e_neg = (both(n, [P, W_GRP]) for n in ("e_cum", "e_neg"))
        decay = both("decay", [P, 2, 2])
        q_d, k_i = (both(n, [P, W_GRP]) for n in ("q_d", "k_i"))
        e_rest = both("e_rest", [P, 2, W_GRP])
        k_e = both("k_e", [P, 2, W_GRP])
        q_t = both("q_t", [P, NH, P])
        k_t = both("k_t", [P, 2, P])
        att = both("att", [P, NH, P])
        s_at = [[sb(f"s_at{d}{s}", [P, 2, HD]) for s in range(2)] for d in range(2)]
        s_mid = [[sb(f"s_mid{d}{s}", [P, 2, HD]) for s in range(2)] for d in range(2)]
        o_sb = both("o_sb", [P, W_GRP])
        bank = lambda n: [ctx.enter_context(nc.psum_tensor(f"d_{n}{d}", [P, 512], F32)) for d in range(2)]
        ps_z, ps_c, ps_u, ps_a = bank("ps_z"), bank("ps_c"), bank("ps_u"), bank("ps_a")
        names = ("at_mm", "at_sb", "z_mm", "low_done", "nab_done", "ez_done", "lz_done", "la_done", "c_mm", "exps",
                 "qd_done", "ke_done", "turned", "turned_sb", "att_mm", "att_sb", "mid_done", "new_done", "o_mm", "o_done",
                 "o_sent", "st_out")
        S = [{n: sem(f"{n}{d}") for n in names} for d in range(2)]
        t_in = [[sem(f"t_in{d}{s}") for s in range(2)] for d in range(2)]
        consts, small_in, st_in = sem("consts"), sem("small_in"), sem("st_in")
        block = ctx.enter_context(nc.Block())
        n_steps = N_TOK // P
        DIRS = range(2)
        N_CONST = 32

        def loads(i, s):
            return (i - s) * 16 + 32

        @block.sync
        def _(sp):
            sp.wait_ge(consts, 1)
            for d, (w, b) in enumerate((("gla_up_f", "gla_bias_f"), ("gla_up_b", "gla_bias_b"))):
                sp.dma_start(up[0:RANK, d, :], io[w].rearrange("a r n -> (a r) n")).then_inc(small_in, 16)
                sp.dma_start(up[32:33, d, :], io[b]).then_inc(small_in, 16)
                sp.dma_start(s_at[d][0][:, :, :], io["state_gla"][0, 0, d].rearrange("(p h) k v -> (h k) p v", p=2)).then_inc(st_in, 16)
            for i, s, *tiles in gla_steps(sp):
                ahead(sp, i + 1, *(t * (P * 4 * P1_W) for t in tiles))
                for d in DIRS:
                    tok = tiles[d] * P
                    sp.wait_ge(S[d]["o_mm"], i + 1)
                    sp.dma_start(at[d][s][:, :], io["p1"][bass.ds(tok, P), P1_A + RANK * d:P1_A + RANK * (d + 1)]).then_inc(t_in[d][s], 16)
                    sp.dma_start(qkv[d][s][:, :], io["p1"][bass.ds(tok, P), P1_QKD:P1_GD]).then_inc(t_in[d][s], 16)

        @block.gpsimd
        def _(pool):
            n = 0

            def step(ins):
                nonlocal n
                ins.then_inc(consts, 1)
                n += 1

            step(pool.memset(up[:, :, :], 0.0))
            for d in DIRS:
                step(pool.memset(aug[d][:, :], 0.0))
                step(pool.memset(e_rest[d][:, :, :], 0.0))
                step(pool.memset(q_t[d][:, :, :], 0.0))
            step(pool.memset(tri[:, :, :, :], 1.0 / TAU))
            step(pool.memset(mask[:, :, :], 1.0))
            step(pool.memset(ind[:, :], 1.0 / TAU))
            pool.wait_ge(consts, n)
            for d in DIRS:
                step(pool.memset(aug[d][32:33, :], 1.0))
            cuts = []
            for d in DIRS:
                sign = 1 if d == 0 else -1
                cuts += [(tri[:, d, 0, :], 0, sign), (tri[:, d, 1, :], -1, -sign), (mask[:, d, :], 0, sign)]
            for view, base, sign in cuts:
                pool.wait_ge(consts, n)
                step(pool.affine_select(out=view, in_=view, compare_op=ALU.is_ge, fill=0.0, base=base,
                                        pattern=[[sign, P]], channel_multiplier=-sign))
                pool.wait_ge(consts, n)
                step(pool.memset(view[0:C, C:P], 0.0))
                step(pool.memset(view[C:P, 0:C], 0.0))
            pool.wait_ge(consts, n)
            step(pool.memset(ind[0:C, 1:2], 0.0))
            step(pool.memset(ind[C:P, 0:1], 0.0))
            assert n == N_CONST
            for i, s, *_ in gla_steps(pool):
                for d in DIRS:
                    k = qkv[d][s][:, W_GRP:2 * W_GRP]
                    pool.wait_ge(S[d]["exps"], i + 1)
                    pool.tensor_tensor(k_i[d][:, :], k, e_neg[d][:, :], ALU.mult)
                    pool.tensor_tensor(k_e[d][:, :, :], k.unsqueeze(1).broadcast_to([P, 2, W_GRP]), e_rest[d][:, :, :], ALU.mult).then_inc(S[d]["ke_done"], 1)

        @block.scalar
        def _(act):
            for d in DIRS:
                act.sem_inc(S[d]["o_done"], 1)
                act.sem_inc(S[d]["o_sent"], 16)
            for i, s, *tiles in gla_steps(act):
                for d in DIRS:
                    act.wait_ge(S[d]["nab_done"], i + 1)
                    act.activation(ez[d][:, :], nab[d][:, :], ACT.Exp).then_inc(S[d]["ez_done"], 1)
                    act.wait_ge(S[d]["ez_done"], i + 1)
                    act.activation(lz[d][:, :], ez[d][:, :], ACT.Ln, bias=1.0).then_inc(S[d]["lz_done"], 1)
                for d in DIRS:
                    act.wait_ge(S[d]["c_mm"], i + 1)
                    act.activation(e_cum[d][:, :], ps_c[d][:, 0:W_GRP], ACT.Exp)
                    act.activation(e_neg[d][:, :], ps_c[d][:, 0:W_GRP], ACT.Exp, scale=-1.0)
                    for c in range(2):
                        rows = slice(c * C, (c + 1) * C)
                        act.activation(e_rest[d][rows, c, :], ps_c[d][rows, W_GRP:], ACT.Exp)
                    act.activation(decay[d][:, :, :], ps_u[d][:, 0:4].rearrange("p (a b) -> p a b", a=2), ACT.Exp).then_inc(S[d]["exps"], 1)
                for d in DIRS:
                    act.wait_ge(S[d]["turned"], i + 1)
                    turned = ps_c[d][:, :].rearrange("p (a b) -> p a b", a=4)
                    act.activation(k_t[d][:, :, :], turned[:, 2:4, :], ACT.Copy)
                    for odd in range(2):
                        rows = slice(64 * odd, 64 * odd + 64)
                        last = act.activation(q_t[d][rows, odd::2, :], turned[rows, 0:2, :], ACT.Copy)
                    last.then_inc(S[d]["turned_sb"], 1)
                for d in DIRS:
                    act.wait_ge(S[d]["o_mm"], i + 3)
                    act.wait_ge(S[d]["o_sent"], i * 16 + 16)
                    act.activation(o_sb[d][:, :], ps_z[d][:, 0:W_GRP], ACT.Copy).then_inc(S[d]["o_done"], 1)
                for d in DIRS:
                    act.wait_ge(S[d]["o_done"], i + 2)
                    act.dma_start(io["od"][d, bass.ds(tiles[d] * P, P), :], o_sb[d][:, :]).then_inc(S[d]["o_sent"], 16)
            for d in DIRS:
                act.wait_ge(S[d]["o_sent"], 16 * (n_steps + 1))
                act.wait_ge(S[d]["new_done"], 2 * n_steps + 2)
                act.dma_start(io["new_state_gla"][0, 0, d].rearrange("(p h) k v -> (h k) p v", p=2),
                              s_at[d][n_steps % 2][:, :, :]).then_inc(S[d]["st_out"], 16)
            for d in DIRS:
                act.wait_ge(S[d]["st_out"], 16)

        @block.tensor
        def _(pe):
            for d in DIRS:
                pe.sem_inc(S[d]["o_mm"], 2)
            pe.wait_ge(consts, N_CONST)
            pe.wait_ge(small_in, 64)
            pe.wait_ge(st_in, 32)
            for i, s, *_ in gla_steps(pe):
                for d in DIRS:
                    pe.wait_ge(t_in[d][s], loads(i, s))
                    pe.wait_ge(S[d]["o_done"], i + 1)
                    pe.transpose(ps_z[d][0:RANK, 0:P], at[d][s][:, :], keep["ident"][:, :]).then_inc(S[d]["at_mm"], 1)
                for d in DIRS:
                    pe.wait_ge(S[d]["at_sb"], i + 1)
                    pe.matmul(ps_z[d][:, W_GRP:], aug[d][:, :], up[:, d, :], start=True, stop=True).then_inc(S[d]["z_mm"], 1)
                for d in DIRS:
                    pe.wait_ge(S[d]["la_done"], i + 1)
                    pe.matmul(ps_c[d][:, 0:W_GRP], tri[:, d, 0, :], la[d][:, :], start=True, stop=True)
                    pe.matmul(ps_c[d][:, W_GRP:], tri[:, d, 1, :], la[d][:, :], start=True, stop=True)
                    for p in range(2):
                        last = pe.matmul(ps_u[d][:, 2 * p:2 * p + 2], la[d][:, p * P:(p + 1) * P], ind[:, :], start=True, stop=True)
                    last.then_inc(S[d]["c_mm"], 1)
                for d in DIRS:
                    pe.wait_ge(S[d]["qd_done"], i + 1)
                    pe.wait_ge(S[d]["ke_done"], i + 1)
                    for n, src in enumerate((q_d[d], q_d[d], k_i[d], k_i[d])):
                        last = pe.transpose(ps_c[d][:, n * P:(n + 1) * P], src[:, (n % 2) * P:(n % 2) * P + P], keep["ident"][:, :])
                    last.then_inc(S[d]["turned"], 1)
                    for c in range(2):
                        for h in range(NH):
                            pe.matmul(ps_u[d][64 * (h % 2):64 * (h % 2) + 64, 256 + 128 * c + 64 * (h // 2):256 + 128 * c + 64 * (h // 2) + 64],
                                      k_e[d][:, c, h * HD:(h + 1) * HD],
                                      qkv[d][s][:, 2 * W_GRP + h * HD:2 * W_GRP + (h + 1) * HD], start=True, stop=True)
                for d in DIRS:
                    pe.wait_ge(S[d]["turned_sb"], i + 1)
                    for h in range(NH):
                        last = pe.matmul(ps_a[d][:, h * P:(h + 1) * P], k_t[d][:, h // 2, :], q_t[d][:, h, :], start=True, stop=True)
                    last.then_inc(S[d]["att_mm"], 1)
                for d in DIRS:
                    pe.wait_ge(S[d]["att_sb"], i + 1)
                    pe.wait_ge(S[d]["mid_done"], 2 * i + 2)
                    for h in range(NH):
                        for n in range(2):
                            c = n if d == 0 else 1 - n
                            pe.matmul(ps_z[d][c * C:(c + 1) * C, h * HD:(h + 1) * HD], q_t[d][:, h, c * C:(c + 1) * C],
                                      (s_mid if n else s_at)[d][s][:, h // 2, :], start=True, stop=False, skip_group_check=True)
                        last = pe.matmul(ps_z[d][:, h * HD:(h + 1) * HD], att[d][:, h, :],
                                         qkv[d][s][:, 2 * W_GRP + h * HD:2 * W_GRP + (h + 1) * HD],
                                         start=False, stop=True, skip_group_check=True)
                    last.then_inc(S[d]["o_mm"], 1)

        @block.vector
        def _(dve):
            dve.wait_ge(consts, N_CONST)
            dve.wait_ge(st_in, 32)
            for d in DIRS:
                dve.sem_inc(S[d]["new_done"], 2)
            for i, s, *_ in gla_steps(dve):
                if isinstance(i, int) and i == N_GRID // P:
                    for d in DIRS:
                        dve.wait_ge(S[d]["new_done"], 2 * i + 2)
                        dve.memset(s_at[d][s][:, :, :], 0.0).then_inc(st_in, 16)
                    dve.wait_ge(st_in, 64)
                for d in DIRS:
                    dve.wait_ge(S[d]["at_mm"], i + 1)
                    dve.tensor_copy(aug[d][0:RANK, :], ps_z[d][0:RANK, 0:P]).then_inc(S[d]["at_sb"], 1)
                for d in DIRS:
                    dve.wait_ge(S[d]["z_mm"], i + 1)
                    dve.tensor_scalar(low[d][:, :], ps_z[d][:, W_GRP:], 0.0, None, ALU.min).then_inc(S[d]["low_done"], 1)
                    dve.wait_ge(S[d]["low_done"], i + 1)
                    dve.scalar_tensor_tensor(nab[d][:, :], low[d][:, :], 2.0, ps_z[d][:, W_GRP:], ALU.mult, ALU.subtract).then_inc(S[d]["nab_done"], 1)
                for d in DIRS:
                    dve.wait_ge(S[d]["lz_done"], i + 1)
                    dve.tensor_tensor(la[d][:, :], low[d][:, :], lz[d][:, :], ALU.subtract).then_inc(S[d]["la_done"], 1)
                for d in DIRS:
                    dve.wait_ge(S[d]["exps"], i + 1)
                    dve.wait_ge(t_in[d][s], loads(i, s))
                    dve.scalar_tensor_tensor(q_d[d][:, :], qkv[d][s][:, 0:W_GRP], HD ** -0.5, e_cum[d][:, :], ALU.mult, ALU.mult).then_inc(S[d]["qd_done"], 1)
                for d in DIRS:
                    dve.wait_ge(S[d]["att_mm"], i + 1)
                    for n in range(2):
                        c = n if d == 0 else 1 - n
                        if n:
                            dve.wait_ge(S[d]["mid_done"], 2 * i + 2)
                        else:
                            dve.wait_ge(S[d]["new_done"], 2 * i + 2)
                        for p in range(2):
                            dst, src = (s_at[d][1 - s], s_mid[d][s]) if n else (s_mid[d][s], s_at[d][s])
                            dve.scalar_tensor_tensor(dst[:, p, :], src[:, p, :], decay[d][:, p, c:c + 1],
                                                     ps_u[d][:, 256 + 128 * c + 64 * p:256 + 128 * c + 64 * p + 64],
                                                     ALU.mult, ALU.add).then_inc(S[d]["new_done" if n else "mid_done"], 1)
                for d in DIRS:
                    dve.tensor_tensor(att[d][:, :, :], ps_a[d][:, :].rearrange("p (h t) -> p h t", h=NH),
                                      mask[:, d, :].unsqueeze(1).broadcast_to([P, NH, P]), ALU.mult).then_inc(S[d]["att_sb"], 1)


def fourier_groups(eng):
    with eng.Fori(1, 5) as n:
        for s in range(2):
            yield n * 2 - 2 + s, s


def mix_stage(nc, io, keep):
    GW = 8
    BANKS = GW // 2
    with stage(nc) as (ctx, new_sem):
        sb = lambda name, shape, dt=F32: ctx.enter_context(nc.sbuf_tensor("f_" + name, shape, dt))
        sem = lambda name: new_sem("f_" + name)
        first = sb("first", [P, P])
        second = [sb(f"second{s}", [P, GW, 64]) for s in range(2)]
        gx = [sb(f"gx{s}", [P, GW, W_GRP]) for s in range(2)]
        yx = [sb(f"yx{s}", [P, GW, W_GRP]) for s in range(2)]
        whole = sb("whole", [P, 2, 2, N_PROMPT])
        gp = sb("gp", [P, 2, 2, W_GRP])
        yp = sb("yp", [P, 2, W_GRP])
        cb, hb, bb, gb = (sb(n, [P, N_TOK]) for n in ("cb", "hb", "bb", "gb"))
        yb = sb("yb", [P, N_TOK])
        taps_raw = sb("taps_raw", [6, P])
        cw = sb("cw", [P, 3, 2])
        ps = [ctx.enter_context(nc.psum_tensor(f"f_ps{b}", [P, 2, W_GRP], F32)) for b in range(BANKS)]
        ps_p = ctx.enter_context(nc.psum_tensor("f_psp", [P, 2, W_GRP], F32))
        ps_w = ctx.enter_context(nc.psum_tensor("f_psw", [P, 6], F32))
        consts, gp_in, cw_in, cw_mm, cw_sb = (sem(n) for n in ("consts", "gp_in", "cw_in", "cw_mm", "cw_sb"))
        slot_in = [[sem(f"in{q}{s}") for s in range(2)] for q in range(2)]
        mm = [sem(f"mm{q}") for q in range(2)]
        by_act = [sem(f"by_act{q}") for q in range(2)]
        by_dve = [sem(f"by_dve{q}") for q in range(2)]
        sent = [[sem(f"sent{q}{s}") for s in range(2)] for q in range(2)]
        yp_mm, yp_sb, yp_sent = sem("yp_mm"), sem("yp_sb"), sem("yp_sent")
        conv_in, u_done, bg_done, taps, conv_done, ybt_sent = (
            sem(n) for n in ("conv_in", "u_done", "bg_done", "taps", "conv_done", "ybt_sent"))
        block = ctx.enter_context(nc.Block())

        @block.sync
        def _(sp):
            sp.dma_start(first[:, :], io["dft_first"]).then_inc(consts, 16)
            gv = io["g"][:, 0:N_GRID, :].rearrange("r (a b) c -> r a b c", b=64)
            for i, s in fourier_groups(sp):
                ahead(sp, i * BANKS + BANKS, i * (GW * W_GRP * 4))
                sp.wait_ge(mm[0], i * BANKS + BANKS)
                for r in range(2):
                    sp.dma_start(gx[s][64 * r:64 * r + 64, :, :], gv[r, :, bass.ds(i * GW, GW), :]).then_inc(slot_in[0][s], 16)
            for s in range(2):
                sp.wait_ge(sent[0][s], 80)
            yv = io["y1"].rearrange("(r k) b c -> r b k c", r=2)
            for i, s in fourier_groups(sp):
                ahead(sp, i * BANKS + BANKS, i * (GW * W_GRP * 4 * 64), i * (GW * 64 * 4))
                sp.wait_ge(mm[1], i * BANKS + BANKS)
                for r in range(2):
                    sp.dma_start(gx[s][64 * r:64 * r + 64, :, :], yv[r, :, bass.ds(i * GW, GW), :]).then_inc(slot_in[1][s], 16)
                sp.dma_start(second[s][:, :, :], io["dft_second"][:, bass.ds(i * GW, GW), :]).then_inc(slot_in[1][s], 16)

        @block.gpsimd
        def _(pool):
            pool.dma_start(taps_raw[:, :], io["conv_w"].rearrange("a t (f p) -> (a t f) p", p=P)).then_inc(cw_in, 16)
            for f in range(2):
                if f:
                    pool.wait_ge(conv_done, 1)
                for n, buf in enumerate((bb, cb, hb, gb)):
                    pool.dma_start(buf[:, :], io["bt"][2 * n + f]).then_inc(conv_in, 16)
                if f == 0:
                    for r in range(2):
                        pool.dma_start(gp[:, r, :, :], io["g"][r, N_GRID:N_TOK, :].rearrange("(j p) c -> p j c", p=P)).then_inc(gp_in, 16)
                        pool.dma_start(whole[:, r, :, :], io["dft_whole"][r].rearrange("(j p) k -> p j k", p=P)).then_inc(gp_in, 16)
                pool.wait_ge(conv_in, 64 * (f + 1))
                pool.tensor_tensor(cb[:, :], cb[:, :], hb[:, :], ALU.mult).then_inc(u_done, 1)
                pool.tensor_tensor(bb[:, :], bb[:, :], gb[:, :], ALU.mult).then_inc(bg_done, 1)
                pool.wait_ge(conv_done, f + 1)
                pool.dma_start(io["ybt"][f * P:(f + 1) * P, :], yb[:, :]).then_inc(ybt_sent, 16)
            pool.wait_ge(ybt_sent, 32)

        @block.tensor
        def _(pe):
            for q in range(2):
                pe.sem_inc(mm[q], 2 * BANKS)
            pe.wait_ge(cw_in, 16)
            pe.transpose(ps_w[:, :], taps_raw[:, :], keep["ident"][0:6, 0:6]).then_inc(cw_mm, 1)
            pe.wait_ge(consts, 16)
            for q in range(2):
                for i, s in fourier_groups(pe):
                    pe.wait_ge(slot_in[q][s], (i - s) * (8 * (2 + q)) + 16 * (2 + q))
                    for n in range(BANKS):
                        pe.wait_ge((by_act, by_dve)[n % 2][q], i * (BANKS // 2) + n // 2 + 1)
                        if q == 0:
                            last = pe.matmul(ps[n][:, :, :], first[:, :], gx[s][:, 2 * n:2 * n + 2, :], start=True, stop=True)
                        else:
                            for k in range(2):
                                last = pe.matmul(ps[n][0:64, k, :], second[s][:, 2 * n + k, :], gx[s][:, 2 * n + k, :], start=True, stop=True)
                        last.then_inc(mm[q], 1)
            pe.wait_ge(gp_in, 64)
            for kc in range(2):
                for r in range(2):
                    for j in range(2):
                        last = pe.matmul(ps_p[:, kc, :], whole[:, r, j, kc * P:(kc + 1) * P], gp[:, r, j, :],
                                         start=(r == 0 and j == 0), stop=(r == 1 and j == 1))
            last.then_inc(yp_mm, 1)

        @block.scalar
        def _(act):
            for q in range(2):
                act.sem_inc(by_act[q], BANKS // 2)
                for s in range(2):
                    act.sem_inc(sent[q][s], 16)
            for q in range(2):
                rows = slice(0, P if q == 0 else 64)
                for i, s in fourier_groups(act):
                    act.wait_ge(sent[q][s], (i - s) * 8 + 16)
                    for n in range(0, BANKS, 2):
                        act.wait_ge(mm[q], i * BANKS + n + 2 * BANKS + 1)
                        act.activation(yx[s][rows, 2 * n:2 * n + 2, :], ps[n][rows, :, :], ACT.Copy).then_inc(by_act[q], 1)
                    act.wait_ge(by_act[q], i * (BANKS // 2) + BANKS)
                    act.wait_ge(by_dve[q], i * (BANKS // 2) + BANKS)
                    if q == 0:
                        act.dma_start(io["y1"][:, bass.ds(i * GW, GW), :], yx[s][:, :, :]).then_inc(sent[q][s], 16)
                    else:
                        act.dma_start(io["yc"][0:N_GRID, :].rearrange("(k2 k1) c -> k2 k1 c", k1=64)[:, bass.ds(i * GW, GW), :],
                                      yx[s][rows, :, :]).then_inc(sent[q][s], 16)
            act.wait_ge(yp_mm, 1)
            act.activation(yp[:, :, :], ps_p[:, :, :], ACT.Copy).then_inc(yp_sb, 1)
            act.wait_ge(yp_sb, 1)
            act.dma_start(io["yc"][N_GRID:N_TOK, :].rearrange("(j p) c -> p j c", p=P), yp[:, :, :]).then_inc(yp_sent, 16)
            act.wait_ge(yp_sent, 16)
            for s in range(2):
                act.wait_ge(sent[1][s], 80)

        @block.vector
        def _(dve):
            for q in range(2):
                dve.sem_inc(by_dve[q], BANKS // 2)
            dve.wait_ge(cw_mm, 1)
            dve.tensor_copy(cw[:, :, :], ps_w[:, :].rearrange("p (t f) -> p t f", f=2)).then_inc(cw_sb, 1)
            for q in range(2):
                rows = slice(0, P if q == 0 else 64)
                for i, s in fourier_groups(dve):
                    dve.wait_ge(sent[q][s], (i - s) * 8 + 16)
                    for n in range(1, BANKS, 2):
                        dve.wait_ge(mm[q], i * BANKS + n + 2 * BANKS + 1)
                        dve.tensor_copy(yx[s][rows, 2 * n:2 * n + 2, :], ps[n][rows, :, :]).then_inc(by_dve[q], 1)
                f = q
                t = 0

                def tap(ins):
                    nonlocal t
                    ins.then_inc(taps, 1)
                    t += 1

                dve.wait_ge(cw_sb, 1)
                dve.wait_ge(u_done, f + 1)
                if f:
                    dve.wait_ge(ybt_sent, 16)
                tap(dve.tensor_scalar(yb[:, :], cb[:, :], cw[:, 1, f:f + 1], None, ALU.mult))
                for w, lag in ((0, 1), (2, -1)):
                    dve.wait_ge(taps, 5 * f + t)
                    for a, b in ((0, N_GRID), (N_GRID, N_TOK)):
                        dst = yb[:, a + max(lag, 0):b + min(lag, 0)]
                        tap(dve.scalar_tensor_tensor(dst, cb[:, a + max(-lag, 0):b + min(-lag, 0)], cw[:, w, f:f + 1], dst, ALU.mult, ALU.add))
                dve.wait_ge(taps, 5 * f + t)
                dve.wait_ge(bg_done, f + 1)
                dve.tensor_tensor(yb[:, :], yb[:, :], bb[:, :], ALU.mult).then_inc(conv_done, 1)


def output_tiles(eng):
    grid = N_GRID // P
    with eng.Fori(1, grid // 2 + 1) as n:
        for s in range(2):
            yield n * 2 - 2 + s, s, 0
    for s in range(2):
        yield grid + s, s, 1


def output_stage(nc, io, keep):
    CH = [(0, 128), (64, 192), (512, 576), (640, 704), (768, 832), (896, 960), (256, 320), (384, 448)]
    LAST = N_TOK // P - 1
    with stage(nc) as (ctx, new_sem):
        sb = lambda name, shape, dt=F32: ctx.enter_context(nc.sbuf_tensor("o_" + name, shape, dt))
        sem = lambda name: new_sem("o_" + name)
        two = lambda name, shape, dt=F32: [sb(f"{name}{s}", shape, dt) for s in range(2)]
        w_hi = sb("w_hi", [P, K8, DM], F32R)
        w_lo = sb("w_lo", [P, K8, DM], F32R)
        stage_w = two("stage_w", [P, DM])
        gate = sb("gate", [P, 2, DM])
        gn = sb("gn", [P, HD])
        gn8 = sb("gn8", [P, HD])
        half_pow = sb("half_pow", [P, NH])
        eps = sb("eps", [P, NH])
        x = two("x", [P, DM])
        ya = two("ya", [P, 2, 2, HD])
        g_ad = two("g_ad", [P, 2, W_GRP])
        gyc = two("gyc", [P, 2, W_GRP])
        od = two("od", [P, 2, W_GRP])
        yb = two("yb", [P, 2, P])
        o = sb("o", [P, W_GRP])
        o_sq = sb("o_sq", [P, W_GRP])
        ss = sb("ss", [P, NH])
        ve = sb("ve", [P, NH])
        r = sb("r", [P, NH])
        o_n = sb("o_n", [P, W_GRP])
        gg = sb("gg", [P, W_GRP])
        mix = two("mix", [P, 3, W_GRP])
        y_hi = two("y_hi", [P, K8, P], F32R)
        y_lo = two("y_lo", [P, K8, P], F32R)
        gx = two("gx", [P, DM])
        y = two("y", [P, DM])
        ps_t = [ctx.enter_context(nc.psum_tensor(f"o_ps_t{b}", [P, 4, P], F32)) for b in range(2)]
        ps_y = [[ctx.enter_context(nc.psum_tensor(f"o_ps_y{s}{h}", [P, 512], F32)) for h in range(2)] for s in range(2)]
        w_in = [sem(f"w_in{s}") for s in range(2)]
        w_hi_done, w_lo_done, small_in, gn_in, gn_done, pow_set = (
            sem(n) for n in ("w_hi_done", "w_lo_done", "small_in", "gn_in", "gn_done", "pow_set"))
        mix_in = [sem(f"mix_in{s}") for s in range(2)]
        x_in = [sem(f"x_in{s}") for s in range(2)]
        o_sum, sq_done, ss_done, ve_done, r_done, on_done, gg_done, mixed, turned, hi_done, lo_done = (
            sem(n) for n in ("o_sum", "sq_done", "ss_done", "ve_done", "r_done", "on_done", "gg_done", "mixed", "turned", "hi_done", "lo_done"))
        mm, gated, added = sem("mm"), sem("gated"), sem("added")
        sent = [sem(f"sent{s}") for s in range(2)]
        block = ctx.enter_context(nc.Block())

        @block.sync
        def _(sp):
            def load_mix(t, s):
                tok = t * P
                for a in range(2):
                    sp.dma_start(ya[s][64 * a:64 * a + 64, :, :, :].rearrange("q h p d -> q h (p d)"),
                                 io["ya"][bass.ds(t * 2 + a, 1)].rearrange("a (h q) p d -> (a q) h (p d)", h=2)).then_inc(mix_in[s], 16)
                sp.dma_start(g_ad[s][:, 0, :], io["p1"][bass.ds(tok, P), P1_G:P1_G + W_GRP]).then_inc(mix_in[s], 16)
                sp.dma_start(g_ad[s][:, 1, :], io["p1"][bass.ds(tok, P), P1_GD:P1_GD + W_GRP]).then_inc(mix_in[s], 16)
                sp.dma_start(gyc[s][:, 0, :], io["gc"][bass.ds(tok, P), :]).then_inc(mix_in[s], 16)
                sp.dma_start(gyc[s][:, 1, :], io["yc"][bass.ds(tok, P), :]).then_inc(mix_in[s], 16)
                sp.dma_start(od[s][:, :, :], io["od"][:, bass.ds(tok, P), :].rearrange("d t c -> t d c")).then_inc(mix_in[s], 16)
                sp.dma_start(yb[s][:, :, :], io["ybt"][:, bass.ds(tok, P)].rearrange("(f p) t -> p f t", p=P)).then_inc(mix_in[s], 16)

            sp.dma_start(gn[:, :], io["gla_norm_g"].broadcast_to([P, HD])).then_inc(gn_in, 16)
            load_mix(0, 0)
            load_mix(1, 1)
            for n in range(K8):
                if n >= 2:
                    sp.wait_ge(w_lo_done, n - 1)
                for a, row in enumerate(CH[n]):
                    sp.dma_start(stage_w[n % 2][64 * a:64 * a + 64, :], io["w_out"][0, row:row + 64, :]).then_inc(w_in[n % 2], 16)
            for j in range(2):
                sp.dma_start(gate[:, j, :], io["gates"][j:j + 1, :].broadcast_to([P, DM])).then_inc(small_in, 16)
            for t, s, j in output_tiles(sp):
                src, tok = ("x_prompt", (t - N_GRID // P) * P) if j else ("x_sample", t * P)
                if j == 0:
                    ahead(sp, t * 2 + 2, t * 3 + 6, tok * 4, tok * (4 * DM))
                    ahead(sp, *((t + 2) * (P * n) for n in (4, 4 * W_GRP, 4 * P1_W)), (t + 2) * (2 * GRID_W * W_GRP * 4))
                sp.wait_ge(added, t * 2 + 2)
                sp.dma_start(x[s][:, :], io[src][0, bass.ds(tok, P), :]).then_inc(x_in[s], 16)
                if j == 0:
                    sp.wait_ge(mixed, t * 3 + 6)
                    sp.wait_ge(lo_done, t * 3 + 6)
                    load_mix(t + 2, s)

        @block.gpsimd
        def _(pool):
            pool.memset(half_pow[:, :], -0.5).then_inc(pow_set, 1)
            pool.memset(eps[:, :], HD * EPS).then_inc(pow_set, 1)
            pool.wait_ge(pow_set, 2)
            pool.sem_inc(mixed, 3)
            pool.sem_inc(added, 4)
            pool.wait_ge(gn_done, 1)

            def join(t, s):
                gates = g_ad[s][:, 0, :].rearrange("t (p h d) -> t h p d", p=2, h=2)
                pool.wait_ge(mix_in[s], (t - s) * 64 + 128)
                pool.wait_ge(sq_done, t + 1)
                pool.wait_ge(on_done, t + 1)
                pool.tensor_tensor(o[:, :], od[s][:, 0, :], od[s][:, 1, :], ALU.add).then_inc(o_sum, 1)
                pool.wait_ge(turned, t + 1)
                for a in range(2):
                    for p in range(2):
                        last = pool.tensor_tensor(mix[s][:, 0, (2 * a + p) * HD:(2 * a + p + 1) * HD], ya[s][:, a, p, :], gates[:, a, p, :], ALU.mult)
                last.then_inc(mixed, 1)
                pool.tensor_tensor(mix[s][:, 1, :], gyc[s][:, 0, :], gyc[s][:, 1, :], ALU.mult).then_inc(mixed, 1)
                pool.wait_ge(mixed, t * 3 + 3)
                pool.tensor_tensor(gg[:, :].rearrange("t (h d) -> t h d", d=HD), g_ad[s][:, 1, :].rearrange("t (h d) -> t h d", d=HD),
                                   gn8[:, :].unsqueeze(1).broadcast_to([P, NH, HD]), ALU.mult).then_inc(gg_done, 1)
                pool.wait_ge(ss_done, t + 2)
                pool.tensor_tensor(ve[:, :], ss[:, :], eps[:, :], ALU.add).then_inc(ve_done, 1)
                pool.wait_ge(ve_done, t + 1)
                pool.tensor_tensor(r[:, :], ve[:, :], half_pow[:, :], ALU.pow).then_inc(r_done, 1)
                pool.wait_ge(on_done, t + 2)
                pool.wait_ge(gg_done, t + 1)
                pool.tensor_tensor(mix[s][:, 2, :], o_n[:, :], gg[:, :], ALU.mult).then_inc(mixed, 1)

            join(0, 0)
            for t, s, j in output_tiles(pool):
                if j == 0 or t < LAST:
                    join(t + 1, 1 - s)
                pool.wait_ge(x_in[s], (t - s) * 8 + 16)
                pool.wait_ge(sent[s], (t - s) * 8 + 16)
                for h in range(2):
                    pool.wait_ge(gated, t * 2 + h + 5)
                    cols = slice(h * 512, h * 512 + 512)
                    pool.tensor_tensor(y[s][:, cols], gx[s][:, cols], x[s][:, cols], ALU.add).then_inc(added, 1)

        @block.scalar
        def _(act):
            for s in range(2):
                act.sem_inc(sent[s], 16)
            for n in range(K8):
                act.wait_ge(w_in[n % 2], 32 * (n // 2 + 1))
                act.activation(w_hi[:, n, :], stage_w[n % 2][:, :], ACT.Copy).then_inc(w_hi_done, 1)
            act.sem_inc(sq_done, 1)
            act.wait_ge(gn_in, 16)
            act.activation(gn8[:, :], gn[:, :], ACT.Copy, scale=8.0).then_inc(gn_done, 1)

            def high(t, s):
                act.wait_ge(o_sum, t + 1)
                act.wait_ge(ss_done, t + 1)
                act.activation(o_sq[:, :], o[:, :], ACT.Square).then_inc(sq_done, 1)
                act.wait_ge(mix_in[s], (t - s) * 64 + 128)
                act.wait_ge(mm, t * 2 + 2)
                act.activation(y_hi[s][:, 6:8, :], yb[s][:, :, :], ACT.Copy).then_inc(hi_done, 1)
                act.wait_ge(turned, t + 3)
                act.activation(y_hi[s][:, 0:4, :], ps_t[0][:, :, :], ACT.Copy).then_inc(hi_done, 1)
                act.activation(y_hi[s][:, 4:6, :], ps_t[1][:, 0:2, :], ACT.Copy).then_inc(hi_done, 1)

            high(0, 0)
            for t, s, j in output_tiles(act):
                if j == 0 or t < LAST:
                    high(t + 1, 1 - s)
                dst, tok = ("y_prompt", (t - N_GRID // P) * P) if j else ("y_sample", t * P)
                act.wait_ge(added, t * 2 + 6)
                act.dma_start(io[dst][0, bass.ds(tok, P), :], y[s][:, :]).then_inc(sent[s], 16)
            for s in range(2):
                act.wait_ge(sent[s], 16 + 16 * (N_TOK // P // 2))

        @block.tensor
        def _(pe):
            pe.sem_inc(mm, 4)
            pe.sem_inc(turned, 2)

            def turn(t, s):
                pe.wait_ge(mixed, t * 3 + 6)
                pe.wait_ge(lo_done, t * 3 + 3)
                for n in range(6):
                    last = pe.transpose(ps_t[n // 4][:, n % 4, :], mix[s][:, n // 2, (n % 2) * P:(n % 2) * P + P], keep["ident"][:, :])
                last.then_inc(turned, 1)

            turn(0, 0)
            pe.wait_ge(w_lo_done, K8)
            for t, s, j in output_tiles(pe):
                pe.wait_ge(lo_done, t * 3 + 6)
                for h in range(2):
                    pe.wait_ge(gated, t * 2 + h + 1)
                    cols = slice(h * 512, h * 512 + 512)
                    product(pe, ps_y[s][h][:, :], lambda k: y_hi[s][:, k, :], lambda k: y_lo[s][:, k, :],
                            lambda k: w_hi[:, k, cols], lambda k: w_lo[:, k, cols]).then_inc(mm, 1)
                    if h == 0 and (j == 0 or t < LAST):
                        turn(t + 1, 1 - s)

        @block.vector
        def _(dve):
            dve.sem_inc(gated, 4)
            dve.sem_inc(on_done, 1)
            dve.sem_inc(ss_done, 1)
            dve.sem_inc(lo_done, 3)
            for n in range(K8):
                dve.wait_ge(w_hi_done, n + 1)
                dve.tensor_tensor(w_lo[:, n, :], stage_w[n % 2][:, :], w_hi[:, n, :], ALU.subtract).then_inc(w_lo_done, 1)

            def low(t, s):
                dve.wait_ge(sq_done, t + 2)
                dve.tensor_reduce(ss[:, :], o_sq[:, :].rearrange("t (h d) -> t h d", d=HD), AX.X, ALU.add).then_inc(ss_done, 1)
                dve.wait_ge(r_done, t + 1)
                dve.wait_ge(mixed, t * 3 + 3)
                dve.tensor_tensor(o_n[:, :].rearrange("t (h d) -> t h d", d=HD), o[:, :].rearrange("t (h d) -> t h d", d=HD),
                                  r[:, :].unsqueeze(2).broadcast_to([P, NH, HD]), ALU.mult).then_inc(on_done, 1)
                parts = (yb[s][:, :, :], 6, 8), (ps_t[0][:, :, :], 0, 4), (ps_t[1][:, 0:2, :], 4, 6)
                for n, (src, k0, k1) in enumerate(parts):
                    dve.wait_ge(hi_done, t * 3 + n + 1)
                    dve.tensor_tensor(y_lo[s][:, k0:k1, :], src, y_hi[s][:, k0:k1, :], ALU.subtract).then_inc(lo_done, 1)

            low(0, 0)
            dve.wait_ge(small_in, 32)
            for t, s, j in output_tiles(dve):
                if j == 0 or t < LAST:
                    low(t + 1, 1 - s)
                for h in range(2):
                    cols = slice(h * 512, h * 512 + 512)
                    dve.wait_ge(mm, t * 2 + h + 5)
                    dve.wait_ge(added, t * 2 + h + 1)
                    dve.tensor_tensor(gx[s][:, cols], ps_y[s][h][:, :], gate[:, j, cols], ALU.mult).then_inc(gated, 1)


def build(nc, io):
    with ExitStack() as ctx:
        sb = lambda name, shape: ctx.enter_context(nc.sbuf_tensor(name, shape, F32))
        keep = {"ident": sb("ident", [P, P]), "scale": sb("scale", [P, 2, K8]), "shift": sb("shift", [P, 2, K8])}
        modulation_stage(nc, io, keep)
        projection_stage(nc, io, keep, 0)
        projection_stage(nc, io, keep, 1)
        attention_stage(nc, io, keep)
        gla_stage(nc, io, keep)
        mix_stage(nc, io, keep)
        output_stage(nc, io, keep)


def dft_tables():
    wave = lambda a, b, n: 2 * np.pi * ((np.outer(a, b) % n) / n)
    r = np.arange(64)
    s64, sg = 64 ** -0.5, 8.0
    eye2 = np.eye(2)
    dft64 = np.concatenate([np.kron(eye2, np.cos(wave(r, r, 64)) / sg), np.kron(eye2, -np.sin(wave(r, r, 64)) / sg)], 1)
    c, s = np.cos(wave(r, r, 64)) * s64, np.sin(wave(r, r, 64)) * s64
    first = np.block([[c, -s], [s, c]])
    second = np.zeros((128, 64, 64))
    for k1 in range(64):
        ph = wave(r, k1 + 64 * r, N_GRID)
        second[:64, k1], second[64:, k1] = np.cos(ph) * s64, np.sin(ph) * s64
    n = np.arange(N_PROMPT)
    ph = wave(n, n, N_PROMPT)
    whole = np.stack([np.cos(ph), np.sin(ph)]) * N_PROMPT ** -0.5
    return {"dft64": dft64, "dft_first": first, "dft_second": second, "dft_whole": whole}


NAMES = ["x_prompt", "x_sample", "cache_k", "cache_v", "state_gla", "c", "c_ctx", "norm_g", "w_mod", "b_mod",
         "w_in", "q_norm_g", "k_norm_g", "rpb", "conv_w", "gla_up_f", "gla_bias_f", "gla_up_b", "gla_bias_b",
         "gla_norm_g", "w_out"]
OUTPUTS = [("y_prompt", (1, N_PROMPT, DM)), ("y_sample", (1, N_GRID, DM)), ("new_cache_k", (1, 1, NH, N_PROMPT, HD)),
           ("new_cache_v", (1, 1, NH, N_PROMPT, HD)), ("new_state_gla", (1, 1, 2, NH, HD, HD))]
SCRATCH = [("gates", (2, DM)), ("p1", (N_TOK, P1_W)), ("qkt", (4, P, N_TOK)), ("bt", (8, P, N_TOK)),
           ("gc", (N_TOK, W_GRP)), ("g", (2, N_TOK, W_GRP)), ("ya", (N_TOK // GRID_W, P, 2, HD)), ("toep", (NH * (2 * WIN_H - 1), GRID_W, P)), ("ybt", (W_GRP, N_TOK)),
           ("y1", (P, 64, W_GRP)), ("yc", (N_TOK, W_GRP)), ("od", (2, N_TOK, W_GRP))]


def kernel(**inputs):
    import concourse.bacc as bacc
    from concourse.bass_utils import run_bass_kernel_spmd

    nc = bacc.Bacc("TRN2", target_bir_lowering=False, num_devices=1)
    arrays, io = {}, {}
    for name in NAMES:
        arrays["in_" + name] = np.ascontiguousarray(inputs[name])
    for name, table in dft_tables().items():
        arrays["in_" + name] = np.ascontiguousarray(table.astype(np.float32))
    for name, a in arrays.items():
        io[name[3:]] = nc.dram_tensor(name, a.shape, F32, kind="ExternalInput").ap()
    for name, shape in OUTPUTS:
        io[name] = nc.dram_tensor("out_" + name, shape, F32, kind="ExternalOutput").ap()
    for name, shape in SCRATCH:
        io[name] = nc.dram_tensor("s_" + name, shape, F32, kind="Internal").ap()
    build(nc, io)
    got = run_bass_kernel_spmd(nc, [arrays], core_ids=[0]).results[0]
    return tuple(got["out_" + name] for name, _ in OUTPUTS)
```

```python
from contextlib import ExitStack, contextmanager

import numpy as np

import concourse.bass as bass
from concourse import mybir

F32 = mybir.dt.float32
F32R = mybir.dt.float32r
ACT = mybir.ActivationFunctionType
ALU = mybir.AluOpType
AX = mybir.AxisListType

P = 128
DM = 1024
K8 = DM // P
N_PROMPT = 256
N_GRID = 4096
N_TOK = N_GRID + N_PROMPT
GRID_W = 64
ROWS = N_GRID // GRID_W
PAST = 512
W_GRP = 256
HD = 64
NH = 4
WIN_H = 8
WIN_W = 16
RANK = 16
TAU = 16.0
EPS = 1e-6
N_IN = 14 * W_GRP + 2 * RANK
LAST = N_TOK // P - 1
NEG = -1e30

QA, KA, VA, GA, BB, CB, HB, GB, UC, GC, QD, KD, VD, GD, AF = (W_GRP * n for n in range(15))
P1_QK, P1_V, P1_G, P1_QKD, P1_VD, P1_GD, P1_A = 0, 512, 768, 1024, 1536, 1792, 2048
P1_W = P1_A + 2 * RANK
SKIP = (1, 2)


@contextmanager
def stage(nc):
    with ExitStack() as ctx:
        sems = []

        def sem(name):
            sems.append(nc.alloc_semaphore(name=name))
            return sems[-1]

        yield ctx, sem
        ctx.close()
        nc.clear_and_free_semaphores(sems)
        nc.all_engine_barrier()


def ahead(eng, *values):
    for v in values:
        if not isinstance(v, int):
            eng.compute_val(v)


def kind(t):
    return int(isinstance(t, int) and t >= N_GRID // P)


def tile_pairs(eng, apart=2):
    grid = N_GRID // P
    with eng.Fori(1, (grid - apart) // 2 + 1) as n:
        for s in range(2):
            yield n * 2 - 2 + s, s, 0
    for t in range(grid - apart, LAST + 1):
        yield t, t % 2, kind(t)


def token_rows(io, sample, prompt, t, j):
    return io[prompt][0, bass.ds((t - N_GRID // P) * P, P), :] if j else io[sample][0, bass.ds(t * P, P), :]


def prepare_next(prepare, t, s):
    if not (isinstance(t, int) and t == LAST):
        prepare(t + 1, 1 - s, kind(t + 1))


def prepare_second(prepare, t, s):
    if not (isinstance(t, int) and t + 2 > LAST):
        prepare(t + 2, s, kind(t + 2))


def modulation_stage(nc, io, keep):
    with stage(nc) as (ctx, new_sem):
        sb = lambda name, shape, dt=F32: ctx.enter_context(nc.sbuf_tensor("m_" + name, shape, dt))
        sem = lambda name: new_sem("m_" + name)
        SLOTS = 4
        craw = sb("craw", [2, DM])
        cact = sb("cact", [2, DM])
        c_t = sb("c_t", [P, K8, 2])
        wm = [sb(f"wm{s}", [P, 3 * DM]) for s in range(SLOTS)]
        bm = sb("bm", [2, 3 * DM])
        ng = sb("ng", [2, DM])
        m = sb("m", [2, 3 * DM])
        pad = sb("pad", [GRID_W, NH * (2 * WIN_H - 1), P])
        ps_c = ctx.enter_context(nc.psum_tensor("m_psc", [P, K8, 2], F32))
        ps_m = [ctx.enter_context(nc.psum_tensor(f"m_ps{n}", [2, 512], F32)) for n in range(6)]
        small_in, idn, silu_c, c_mm, c_sb, rows_mm, rows_sb, scaled, out_done = (
            sem(n) for n in ("small_in", "idn", "silu_c", "c_mm", "c_sb", "rows_mm", "rows_sb", "scaled", "out_done"))
        w_in = [sem(f"w_in{n}") for n in range(SLOTS)]
        chunk_mm, pad_zero, pad_in, toep_out = (sem(n) for n in ("chunk_mm", "pad_zero", "pad_in", "toep_out"))
        block = ctx.enter_context(nc.Block())

        @block.sync
        def _(sp):
            for n, name in enumerate(("c", "c_ctx")):
                src = io[name] if n == 0 else io[name].rearrange("(a n) -> a n", a=1)
                sp.dma_start(craw[n:n + 1, :], src).then_inc(small_in, 16)
            for k in range(K8):
                if k >= SLOTS:
                    sp.wait_ge(chunk_mm, k - SLOTS + 1)
                sp.dma_start(wm[k % SLOTS][:, :], io["w_mod"][0, k * P:(k + 1) * P, :]).then_inc(w_in[k % SLOTS], 16)
            sp.wait_ge(scaled, 2)
            sp.dma_start(io["mod"], m[:, :]).then_inc(out_done, 16)
            sp.wait_ge(out_done, 16)

        @block.gpsimd
        def _(pool):
            pool.memset(keep["ident"][:, :], 0.0).then_inc(idn, 1)
            pool.wait_ge(idn, 1)
            pool.affine_select(out=keep["ident"][:, :], in_=keep["ident"][:, :], compare_op=ALU.not_equal,
                               fill=1.0, base=0, pattern=[[-1, P]], channel_multiplier=1).then_inc(idn, 1)
            pool.wait_ge(idn, 2)
            pool.memset(pad[:, :, :], 0.0).then_inc(pad_zero, 1)
            pool.wait_ge(pad_zero, 1)
            pool.dma_start(pad[:, :, 48:48 + 2 * WIN_W - 1],
                           io["rpb"].rearrange("a h r x -> a (h r) x").broadcast_to([GRID_W, NH * (2 * WIN_H - 1), 2 * WIN_W - 1])).then_inc(pad_in, 16)
            pool.wait_ge(pad_in, 16)
            pool.dma_start(io["toep"].rearrange("n q x -> q n x"), pad[:, :, :]).then_inc(toep_out, 16)
            pool.wait_ge(toep_out, 16)

        @block.scalar
        def _(act):
            for n in range(2):
                act.dma_start(bm[n:n + 1, :], io["b_mod"]).then_inc(small_in, 16)
                act.dma_start(ng[n:n + 1, :], io["norm_g"]).then_inc(small_in, 16)
            act.wait_ge(small_in, 6 * 16)
            act.activation(cact[:, :], craw[:, :], ACT.Silu).then_inc(silu_c, 1)

        @block.tensor
        def _(pe):
            pe.wait_ge(idn, 2)
            pe.wait_ge(silu_c, 1)
            for k in range(K8):
                last = pe.transpose(ps_c[:, k, :], cact[:, k * P:(k + 1) * P], keep["ident"][0:2, 0:2])
            last.then_inc(c_mm, 1)
            pe.wait_ge(c_sb, 1)
            for k in range(K8):
                pe.wait_ge(w_in[k % SLOTS], 16 * (k // SLOTS + 1))
                for n in range(6):
                    last = pe.matmul(ps_m[n][:, :], c_t[:, k, :], wm[k % SLOTS][:, n * 512:(n + 1) * 512],
                                     start=(k == 0), stop=(k == K8 - 1))
                last.then_inc(chunk_mm, 1)

        @block.vector
        def _(dve):
            dve.wait_ge(c_mm, 1)
            dve.tensor_copy(c_t[:, :, :], ps_c[:, :, :]).then_inc(c_sb, 1)
            dve.wait_ge(small_in, 6 * 16)
            dve.wait_ge(chunk_mm, K8)
            for n in range(6):
                cols = slice(n * 512, n * 512 + 512)
                dve.tensor_tensor(m[:, cols], ps_m[n][:, :], bm[:, cols], ALU.add).then_inc(rows_sb, 1)
            dve.wait_ge(rows_sb, 6)
            s_cols = slice(DM, 2 * DM)
            dve.tensor_scalar(m[:, s_cols], m[:, s_cols], 1.0, DM ** 0.5, ALU.add, ALU.mult).then_inc(scaled, 1)
            dve.wait_ge(scaled, 1)
            dve.tensor_tensor(m[:, s_cols], m[:, s_cols], ng[:, :], ALU.mult).then_inc(scaled, 1)


def product(pe, out, left_hi, left_lo, right_hi, right_lo):
    for k in range(K8):
        pe.matmul(out, left_hi(k), right_hi(k), start=(k == 0), stop=False)
        pe.matmul(out, left_hi(k), right_lo(k), start=False, stop=False)
        last = pe.matmul(out, left_lo(k), right_hi(k), start=False, stop=(k == K8 - 1))
    return last


def weight_pieces(blocks):
    out, at, group = [], 0, 0
    for c0, n in blocks:
        for c in range(0, n, 512):
            wd = min(512, n - c)
            nk = min(K8, 2 * 512 // wd)
            out += [(k, nk, c0 + c, wd, at + c, group) for k in range(0, K8, nk)]
            group += 1
        at += n
    return out


def projection_stage(nc, io, keep, which):
    blocks = [(QA, 1024), (QD, 1024), (AF, 2 * RANK)] if which == 0 else [(UC, 512), (BB, 1024)]
    pieces = weight_pieces(blocks)
    width = sum(n for _, n in blocks)
    G = pieces[-1][5] + 1
    with stage(nc) as (ctx, new_sem):
        pre = f"p{which}_"
        sb = lambda name, shape, dt=F32: ctx.enter_context(nc.sbuf_tensor(pre + name, shape, dt))
        ps = lambda name, shape: ctx.enter_context(nc.psum_tensor(pre + name, shape, F32))
        sem = lambda name: new_sem(pre + name)
        w_hi = sb("w_hi", [P, K8, width], F32R)
        w_lo = sb("w_lo", [P, K8, width], F32R)
        w_raw = [sb(f"w_raw{s}", [P, 1024]) for s in range(2)]
        shift = sb("shift", [P, 2, DM])
        scale = sb("scale", [P, 2, DM])
        xb = [sb(f"xb{s}", [P, DM]) for s in range(2)]
        squares = sb("squares", [P, DM])
        h_hi = [sb(f"h_hi{s}", [P, K8, P], F32R) for s in range(2)]
        h_lo = [sb(f"h_lo{s}", [P, K8, P], F32R) for s in range(2)]
        ss, ve, rstd = ([sb(f"{n}{s}", [P, 1]) for s in range(2)] for n in ("ss", "ve", "rstd"))
        half_pow = sb("half_pow", [P, 8])
        eps = sb("eps", [P, 9])
        ps_t = [ps(f"ps_t{b}", [P, 4, P]) for b in range(2)]
        ps_m = [ps(f"ps_m{g}", [P, 512]) for g in range(G)]
        (w_hi_done, w_lo_done, small_in, consts, sq_done, ve_done, rstd_done, normed, shifted, turned, hi_done,
         lo_done, mm) = (sem(n) for n in (
             "w_hi_done", "w_lo_done", "small_in", "consts", "sq_done", "ve_done", "rstd_done", "normed", "shifted",
             "turned", "hi_done", "lo_done", "mm"))
        w_in = [sem(f"w_in{s}") for s in range(2)]
        mod_in = [sem(f"mod_in{j}") for j in range(2)]
        x_in = [sem(f"x_in{s}") for s in range(2)]
        bank_free = [sem(f"bank_free{g}") for g in range(G)]
        rows_sent = [sem(f"rows_sent{s}") for s in range(2)]
        t_sent = [sem(f"t_sent{s}") for s in range(2)]
        if which == 0:
            rows = [sb(f"rows{s}", [P, P1_W]) for s in range(2)]
            qss, qve, qr = (sb(n, [P, 8]) for n in ("qss", "qve", "qr"))
            gqk = sb("gqk", [P, 2 * NH * HD])
            qkt = [sb(f"qkt{s}", [P, 4, P]) for s in range(2)]
            ps_q = ps("ps_q", [P, 4, P])
            qk_sq, qk_ss, qk_ve, qk_r, qk_ready, qkt_mm, qkt_sb, gqk_set = (
                sem(n) for n in ("qk_sq", "qk_ss", "qk_ve", "qk_r", "qk_ready", "qkt_mm", "qkt_sb", "gqk_set"))
        else:
            rows = [sb(f"rows{s}", [P, 3, W_GRP]) for s in range(2)]
            zero = sb("zero", [1, W_GRP])
            silu_g = sb("silu_g", [P, W_GRP])
            h_b = sb("h_b", [P, W_GRP])
            u_tok = sb("u_tok", [P, W_GRP])
            u_t = sb("u_t", [P, 2, P])
            dft = sb("dft", [P, 2 * P])
            g_sb = [sb(f"g_sb{s}", [P, 2, W_GRP]) for s in range(2)]
            ps_u = ps("ps_u", [P, 2, P])
            ps_g = ps("ps_g", [P, 2, 2, P])
            u_done, u_mm, u_sb, dft_mm, dft_sb, hg_done, rows_done, zero_out = (
                sem(n) for n in ("u_done", "u_mm", "u_sb", "dft_mm", "dft_sb", "hg_done", "rows_done", "zero_out"))
        block = ctx.enter_context(nc.Block())

        def mm_at(t, n):
            return t * G + n + 1 + 2 * G

        @block.sync
        def _(sp):
            def load_x(t, s, j):
                sp.dma_start(xb[s][:, :], token_rows(io, "x_sample", "x_prompt", t, j)).then_inc(x_in[s], 16)

            for t in range(2):
                load_x(t, t, 0)
            for n, (k, nk, c0, wd, a0, _) in enumerate(pieces):
                if n >= 2:
                    sp.wait_ge(w_lo_done, n - 1)
                sp.dma_start(w_raw[n % 2][:, 0:nk * wd].rearrange("p (k n) -> p k n", k=nk),
                             io["w_in"][0, k * P:(k + nk) * P, c0:c0 + wd].rearrange("(k p) n -> p k n", p=P)).then_inc(w_in[n % 2], 16)
            for t, s, j in tile_pairs(sp):
                tok = t * P
                ahead(sp, t * 2 + 6, t + 1, t + 2, tok * 4, tok * (P1_W * 4), tok * (4 * W_GRP), (t + 2) * (P * DM * 4))
                if not (isinstance(t, int) and t + 2 > LAST):
                    sp.wait_ge(turned, t * 2 + 6)
                    load_x(t + 2, s, kind(t + 2))
                if which == 0:
                    sp.wait_ge(qkt_sb, t + 2)
                    sp.dma_start(io["qkt"][:, :, bass.ds(tok, P)].rearrange("b p t -> p b t"), qkt[s][:, :, :]).then_inc(t_sent[s], 16)
                    sp.wait_ge(qk_ready, t + 1)
                    for g in range(1, G):
                        sp.wait_ge(bank_free[g], t + 2)
                    sp.dma_start(io["p1"][bass.ds(tok, P), :], rows[s][:, :]).then_inc(rows_sent[s], 16)
                else:
                    sp.wait_ge(dft_sb, t + 2)
                    sp.dma_start(io["g"][:, bass.ds(tok, P), :].rearrange("r t c -> t r c"), g_sb[s][:, :, :]).then_inc(t_sent[s], 16)
                    sp.wait_ge(bank_free[0], t + 2)
                    sp.wait_ge(bank_free[1], t + 2)
                    sp.dma_start(io["conv_u"][bass.ds(tok + SKIP[j], P), :], rows[s][:, 0, :]).then_inc(rows_sent[s], 16)
                    sp.dma_start(io["gates_bc"][bass.ds(tok, P), :], rows[s][:, 1:3, :].rearrange("t a c -> t (a c)")).then_inc(rows_sent[s], 16)
            for s in range(2):
                sp.wait_ge(t_sent[s], 16 * (LAST // 2 + 2))
                sp.wait_ge(rows_sent[s], 16 + (1 + which) * 16 * (LAST // 2 + 1))
            if which == 1:
                sp.wait_ge(zero_out, 48)

        @block.gpsimd
        def _(pool):
            pool.memset(half_pow[:, :], -0.5).then_inc(consts, 1)
            pool.memset(eps[:, 0:1], DM * EPS).then_inc(consts, 1)
            pool.memset(eps[:, 1:9], HD * EPS).then_inc(consts, 1)
            pool.wait_ge(consts, 3)
            if which == 1:
                pool.memset(zero[:, :], 0.0).then_inc(consts, 1)
                pool.wait_ge(consts, 4)
                for row in (0, N_GRID + 1, N_TOK + 2):
                    pool.dma_start(io["conv_u"][row:row + 1, :], zero[:, :]).then_inc(zero_out, 16)

            def prepare(t, s, j):
                pool.wait_ge(sq_done, t + 1)
                pool.tensor_tensor(ve[s][:, :], ss[s][:, :], eps[:, 0:1], ALU.add).then_inc(ve_done, 1)
                pool.wait_ge(ve_done, t + 1)
                pool.tensor_tensor(rstd[s][:, :], ve[s][:, :], half_pow[:, 0:1], ALU.pow).then_inc(rstd_done, 1)
                if j:
                    pool.wait_ge(mod_in[1], 32)
                pool.wait_ge(normed, t + 1)
                pool.tensor_tensor(xb[s][:, :], xb[s][:, :], shift[:, j, :], ALU.add).then_inc(shifted, 1)

            pool.wait_ge(mod_in[0], 32)
            prepare(0, 0, 0)
            prepare(1, 1, 0)
            for t, s, j in tile_pairs(pool):
                prepare_second(prepare, t, s)
                if which == 0:
                    pool.wait_ge(qk_ss, t + 2)
                    pool.tensor_tensor(qve[:, :], qss[:, :], eps[:, 1:9], ALU.add).then_inc(qk_ve, 1)
                    pool.wait_ge(qk_ve, t + 1)
                    pool.tensor_tensor(qr[:, :], qve[:, :], half_pow[:, :], ALU.pow).then_inc(qk_r, 1)

        @block.scalar
        def _(act):
            def load_mod(j):
                for row, dst in ((1, scale), (0, shift)):
                    act.dma_start(dst[:, j, :], io["mod"][j:j + 1, row * DM:(row + 1) * DM].broadcast_to([P, DM])).then_inc(mod_in[j], 16)

            load_mod(0)
            if which == 0:
                act.dma_start(gqk[:, 0:HD], io["q_norm_g"].broadcast_to([P, HD])).then_inc(small_in, 16)
                act.dma_start(gqk[:, 4 * HD:5 * HD], io["k_norm_g"].broadcast_to([P, HD])).then_inc(small_in, 16)
            else:
                act.dma_start(dft[:, :], io["dft64"]).then_inc(small_in, 16)
            for g in range(G):
                act.sem_inc(bank_free[g], 1)
            if which == 0:
                act.sem_inc(qkt_sb, 1)
            else:
                act.sem_inc(dft_sb, 1)

            def square(t, s, j):
                act.wait_ge(x_in[s], (t - s) * 8 + 16)
                if not isinstance(t, int) or t:
                    act.wait_ge(sq_done, t)
                if which == 0 and (not isinstance(t, int) or t > 1):
                    act.wait_ge(qk_ss, t - 1)
                act.activation(squares[:, :], xb[s][:, :], ACT.Square, accum_out=ss[s][:, :]).then_inc(sq_done, 1)

            def high(t, s, j):
                act.wait_ge(mm, t * G + G)
                for b in range(2):
                    act.wait_ge(turned, t * 2 + b + 5)
                    act.activation(h_hi[s][:, 4 * b:4 * b + 4, :], ps_t[b][:, :, :], ACT.Copy).then_inc(hi_done, 1)

            square(0, 0, 0)
            square(1, 1, 0)
            load_mod(1)
            for n, (k, nk, c0, wd, a0, _) in enumerate(pieces):
                if n == 4:
                    high(0, 0, 0)
                act.wait_ge(w_in[n % 2], 16 * (n // 2 + 1))
                act.activation(w_hi[:, k:k + nk, a0:a0 + wd], w_raw[n % 2][:, 0:nk * wd].rearrange("p (k n) -> p k n", k=nk),
                               ACT.Copy).then_inc(w_hi_done, 1)
            for t, s, j in tile_pairs(act):
                prepare_second(square, t, s)
                done = (t - s) * 8 + 16
                if which == 0:
                    act.wait_ge(mm, mm_at(t, 0))
                    act.wait_ge(sq_done, min(t + 3, LAST + 1) if isinstance(t, int) else t + 3)
                    act.activation(squares[:, 0:512], ps_m[0][:, :], ACT.Square).then_inc(qk_sq, 1)
                    act.wait_ge(rows_sent[s], done)
                    act.wait_ge(mm, mm_at(t, 1))
                    act.activation(rows[s][:, P1_V:P1_G], ps_m[1][:, 0:W_GRP], ACT.Copy)
                    act.activation(rows[s][:, P1_G:P1_QKD], ps_m[1][:, W_GRP:512], ACT.Silu).then_inc(bank_free[1], 1)
                    prepare_next(high, t, s)
                    act.wait_ge(mm, mm_at(t, 3))
                    act.activation(rows[s][:, P1_VD:P1_GD], ps_m[3][:, 0:W_GRP], ACT.Copy)
                    act.activation(rows[s][:, P1_GD:P1_A], ps_m[3][:, W_GRP:512], ACT.Silu).then_inc(bank_free[3], 1)
                    act.wait_ge(qkt_mm, t + 1)
                    act.wait_ge(t_sent[s], done)
                    act.activation(qkt[s][:, :, :], ps_q[:, :, :], ACT.Copy).then_inc(qkt_sb, 1)
                else:
                    act.wait_ge(mm, mm_at(t, 0))
                    act.activation(u_tok[:, :], ps_m[0][:, 0:W_GRP], ACT.Copy).then_inc(u_done, 1)
                    act.wait_ge(rows_sent[s], (t - s) * 16 + 16)
                    act.activation(rows[s][:, 2, :], ps_m[0][:, W_GRP:512], ACT.Silu).then_inc(bank_free[0], 1)
                    prepare_next(high, t, s)
                    act.wait_ge(mm, mm_at(t, 2))
                    act.activation(h_b[:, :], ps_m[2][:, 0:W_GRP], ACT.Copy)
                    act.activation(silu_g[:, :], ps_m[2][:, W_GRP:512], ACT.Silu).then_inc(bank_free[2], 1)
                    act.wait_ge(dft_mm, t + 1)
                    act.wait_ge(t_sent[s], done)
                    act.activation(g_sb[s][:, :, :].rearrange("t r (f c) -> t f r c", f=2), ps_g[:, :, :, :], ACT.Copy).then_inc(dft_sb, 1)

        @block.tensor
        def _(pe):
            pe.sem_inc(mm, 2 * G)
            pe.sem_inc(turned, 4)

            def turn(t, s, j):
                pe.wait_ge(shifted, t + 1)
                pe.wait_ge(lo_done, t * 2 + 2)
                for b in range(2):
                    for n in range(4):
                        last = pe.transpose(ps_t[b][:, n, :], xb[s][:, (4 * b + n) * P:(4 * b + n + 1) * P], keep["ident"][:, :])
                    last.then_inc(turned, 1)

            turn(0, 0, 0)
            pe.wait_ge(small_in, 32 if which == 0 else 16)
            for t, s, j in tile_pairs(pe):
                pe.wait_ge(lo_done, t * 2 + 4)

                def group(g):
                    a, b = 512 * g, min(512 * g + 512, width)
                    pe.wait_ge(w_lo_done, sum(1 for p in pieces if p[5] <= g))
                    pe.wait_ge(bank_free[g], t + 1)
                    product(pe, ps_m[g][:, 0:b - a], lambda k: h_hi[s][:, k, :], lambda k: h_lo[s][:, k, :],
                            lambda k: w_hi[:, k, a:b], lambda k: w_lo[:, k, a:b]).then_inc(mm, 1)

                group(0)
                group(1)
                prepare_next(turn, t, s)
                if which == 0:
                    for g in range(2, G):
                        group(g)
                    pe.wait_ge(qk_ready, t + 1)
                    pe.wait_ge(qkt_sb, t + 1)
                    for b in range(4):
                        last = pe.transpose(ps_q[:, b, :], rows[s][:, b * P:(b + 1) * P], keep["ident"][:, :])
                    last.then_inc(qkt_mm, 1)
                else:
                    pe.wait_ge(u_done, t + 1)
                    for f in range(2):
                        last = pe.transpose(ps_u[:, f, :], u_tok[:, f * P:(f + 1) * P], keep["ident"][:, :])
                    last.then_inc(u_mm, 1)
                    group(2)
                    pe.wait_ge(u_sb, t + 1)
                    pe.wait_ge(dft_sb, t + 1)
                    for f in range(2):
                        last = pe.matmul(ps_g[:, f], u_t[:, f, :], dft[:, :].rearrange("p (r c) -> p r c", r=2), start=True, stop=True)
                    last.then_inc(dft_mm, 1)

        @block.vector
        def _(dve):
            dve.sem_inc(lo_done, 2)
            for s in range(2):
                dve.sem_inc(rows_sent[s], 16)
                dve.sem_inc(t_sent[s], 16)
            if which == 0:
                dve.sem_inc(qk_ss, 1)

            def norm(t, s, j):
                if j:
                    dve.wait_ge(mod_in[1], 32)
                dve.wait_ge(rstd_done, t + 1)
                dve.scalar_tensor_tensor(xb[s][:, :], xb[s][:, :], rstd[s][:, :], scale[:, j, :], ALU.mult, ALU.mult).then_inc(normed, 1)

            def low(t, s, j):
                for b in range(2):
                    dve.wait_ge(hi_done, t * 2 + b + 1)
                    dve.tensor_tensor(h_lo[s][:, 4 * b:4 * b + 4, :], ps_t[b][:, :, :], h_hi[s][:, 4 * b:4 * b + 4, :],
                                      ALU.subtract).then_inc(lo_done, 1)

            dve.wait_ge(mod_in[0], 32)
            norm(0, 0, 0)
            for n, (k, nk, c0, wd, a0, _) in enumerate(pieces):
                if n == 4:
                    norm(1, 1, 0)
                    low(0, 0, 0)
                dve.wait_ge(w_hi_done, n + 1)
                dve.tensor_tensor(w_lo[:, k:k + nk, a0:a0 + wd], w_raw[n % 2][:, 0:nk * wd].rearrange("p (k n) -> p k n", k=nk),
                                  w_hi[:, k:k + nk, a0:a0 + wd], ALU.subtract).then_inc(w_lo_done, 1)
            if which == 0:
                dve.wait_ge(small_in, 32)
                dve.tensor_scalar(gqk[:, NH * HD:(NH + 1) * HD], gqk[:, NH * HD:(NH + 1) * HD], HD ** 0.5, None,
                                  ALU.mult).then_inc(gqk_set, 1)
                dve.wait_ge(gqk_set, 1)
                for h in range(1, NH):
                    dve.tensor_copy(gqk[:, (NH + h) * HD:(NH + h + 1) * HD], gqk[:, NH * HD:(NH + 1) * HD]).then_inc(gqk_set, 1)
                    dve.tensor_copy(gqk[:, h * HD:(h + 1) * HD], gqk[:, 0:HD]).then_inc(gqk_set, 1)
                dve.wait_ge(gqk_set, 2 * NH - 1)
            for t, s, j in tile_pairs(dve):
                prepare_second(norm, t, s)
                if which == 0:
                    heads = lambda a: a.rearrange("t (h d) -> t h d", h=8)
                    dve.wait_ge(qk_sq, t + 1)
                    dve.tensor_reduce(qss[:, :], heads(squares[:, 0:512]), AX.X, ALU.add).then_inc(qk_ss, 1)
                    dve.wait_ge(rows_sent[s], (t - s) * 8 + 16)
                    dve.wait_ge(qk_r, t + 1)
                    qk = rows[s][:, 0:512]
                    dve.tensor_tensor(heads(qk), heads(ps_m[0][:, :]), qr[:, :].unsqueeze(2).broadcast_to([P, 8, HD]),
                                      ALU.mult).then_inc(bank_free[0], 1)
                    dve.wait_ge(bank_free[0], t + 2)
                    dve.tensor_tensor(qk, qk, gqk[:, :], ALU.mult).then_inc(qk_ready, 1)
                    prepare_next(low, t, s)
                    dve.wait_ge(mm, mm_at(t, 2))
                    dve.tensor_copy(rows[s][:, P1_QKD:P1_VD], ps_m[2][:, :]).then_inc(bank_free[2], 1)
                    dve.wait_ge(mm, mm_at(t, 4))
                    dve.tensor_copy(rows[s][:, P1_A:P1_W], ps_m[4][:, 0:2 * RANK]).then_inc(bank_free[4], 1)
                else:
                    prepare_next(low, t, s)
                    dve.wait_ge(u_mm, t + 1)
                    dve.tensor_copy(u_t[:, :, :], ps_u[:, :, :]).then_inc(u_sb, 1)
                    dve.wait_ge(rows_sent[s], (t - s) * 16 + 16)
                    dve.wait_ge(bank_free[2], t + 2)
                    dve.tensor_tensor(rows[s][:, 1, :], ps_m[1][:, 0:W_GRP], silu_g[:, :], ALU.mult)
                    dve.tensor_tensor(rows[s][:, 0, :], ps_m[1][:, W_GRP:512], h_b[:, :], ALU.mult).then_inc(bank_free[1], 1)


def attention_rows(eng):
    start = lambda r: min(max(r - WIN_H // 2, 0), ROWS - WIN_H) if r < ROWS else None
    last = ROWS + N_PROMPT // GRID_W - 1
    lo, hi = WIN_H // 2, ROWS - WIN_H // 2
    for r in range(lo):
        yield r, start(r), r + 1, start(r + 1), r % 2, r // 2
    with eng.Fori(lo // 2, hi // 2) as n:
        for d in range(2):
            r = n * 2 + d
            yield r, r - WIN_H // 2, r + 1, r + 1 - WIN_H // 2, d, n
    for r in range(hi, last + 1):
        yield r, start(r), r + 1 if r < last else None, start(r + 1), r % 2, r // 2


def attention_scan_stage(nc, io, keep):
    W = WIN_H * GRID_W
    CH = W // P
    CC = PAST // P
    NDR = 2 * WIN_H - 1
    C = P // 2
    DIRS = range(2)
    STEPS = N_TOK // P
    GRID_T = N_GRID // P
    KV0 = WIN_H + WIN_H // 2
    N_CONST = 32
    with stage(nc) as (ctx, new_sem):
        sb = lambda name, shape, dt=F32: ctx.enter_context(nc.sbuf_tensor("a_" + name, shape, dt))
        sem = lambda name: new_sem("a_" + name)
        k_t = sb("k_t", [P, 2, N_GRID])
        v2 = sb("v2", [P, ROWS - 1, W_GRP])
        kp_t = sb("kp_t", [P, 2, N_PROMPT])
        vp = sb("vp", [P, N_PROMPT // P, W_GRP])
        ck = sb("ck", [P, CC, NH, HD])
        ck_t = sb("ck_t", [P, 2, PAST])
        cv = sb("cv", [P, CC, NH, HD])
        bias = sb("bias", [P, 2, NDR, GRID_W])
        q2 = sb("q2", [P, 2, P])
        s_sb = [sb(f"s_sb{p}", [P, W + PAST]) for p in range(2)]
        p_t = [sb(f"p_t{p}", [P, W + PAST]) for p in range(2)]
        o_sb = sb("o_sb", [P, 2, HD])
        max_c, max_w, neg_m, total, r_total = (sb(n, [P, 2]) for n in ("max_c", "max_w", "neg_m", "total", "r_total"))
        sums = sb("sums", [P, 2, 2])
        psum = lambda name, cols: ctx.enter_context(nc.psum_tensor("a_" + name, [P, cols], F32))
        ps_w = psum("ps_w", 512)
        ps_c = [psum(f"ps_c{p}", 512) for p in range(2)]
        ps_t = [psum(f"ps_t{h}", 512) for h in range(2)]
        ps_ou = psum("ps_ou", 512)
        ps_o = [ps_ou[:, p * P:(p + 1) * P] for p in range(2)]
        ps_u = ps_ou[:, 2 * P:].rearrange("p (c a v) -> p c a v", c=2, a=2)
        ps_z = psum("ps_z", 512)
        ps_s = psum("ps_s", 512)
        (k0_in, v0_in, kv_in, ck_in, cv_in, bias_in, bias_set, q_zero, ckt_mm, ckt_sb, s_done, maxc_done, w_done,
         max_done, exp_done, sum_done, rsum_done, t_done, t0_sb, t1_sb, pv_done, o_done, o_sent, cache_out) = (sem(n) for n in (
             "k0_in", "v0_in", "kv_in", "ck_in", "cv_in", "bias_in", "bias_set", "q_zero", "ckt_mm", "ckt_sb", "s_done",
             "maxc_done", "w_done", "max_done", "exp_done", "sum_done", "rsum_done", "t_done", "t0_sb", "t1_sb", "pv_done",
             "o_done", "o_sent", "cache_out"))
        q_in = [sem(f"q_in{p}") for p in range(2)]
        both = lambda name, shape: [sb(f"{name}{d}", shape) for d in range(2)]
        tri = sb("tri", [P, 2, 2, P])
        mask = sb("mask", [P, 2, P])
        ind = sb("ind", [P, 2])
        up = sb("up", [33, 2, W_GRP])
        aug = both("aug", [33, P])
        qkv = both("qkv", [P, 3 * W_GRP])
        at = both("at", [P, RANK])
        low = both("low", [P, W_GRP])
        nab = both("nab", [P, W_GRP])
        ez = both("ez", [P, W_GRP])
        lz = both("lz", [P, W_GRP])
        la = both("la", [P, W_GRP])
        e_cum, e_neg = (both(n, [P, W_GRP]) for n in ("e_cum", "e_neg"))
        decay = both("decay", [P, 2, 2])
        q_d, k_i = (both(n, [P, W_GRP]) for n in ("q_d", "k_i"))
        e_rest = both("e_rest", [P, 2, W_GRP])
        k_e = both("k_e", [P, 2, W_GRP])
        qd_t = both("qd_t", [P, NH, P])
        kd_t = both("kd_t", [P, 2, P])
        att = both("att", [P, NH, P])
        s_at, s_mid = (both(n, [P, 2, HD]) for n in ("s_at", "s_mid"))
        od_sb = both("od_sb", [P, W_GRP])
        names = ("at_mm", "at_sb", "z_mm", "low_done", "nab_done", "ez_done", "lz_done", "la_done", "c_mm", "exps",
                 "qd_done", "ke_done", "turned", "turned_sb", "u_mm", "att_mm", "att_sb", "mid_done", "new_done", "o_mm", "o_done",
                 "o_sent", "st_out")
        S = [{n: sem(f"{n}{d}") for n in names} for d in DIRS]
        u_sb = sb("u_sb", [P, 2, HD])
        u_kept = sem("u_kept")
        t_in = [sem(f"t_in{d}") for d in DIRS]
        consts, small_in, st_in = sem("consts"), sem("small_in"), sem("st_in")
        block = ctx.enter_context(nc.Block())

        def before(d, i):
            return (0, i) if d else (1, i - 1)

        def tile_of(d, i):
            if isinstance(i, int) and i >= GRID_T:
                return i if d == 0 else GRID_T + STEPS - 1 - i
            return i if d == 0 else GRID_T - 1 - i

        @block.sync
        def _(sp):
            sp.wait_ge(consts, 1)
            for d, (w, b) in enumerate((("gla_up_f", "gla_bias_f"), ("gla_up_b", "gla_bias_b"))):
                sp.dma_start(up[0:RANK, d, :], io[w].rearrange("a r n -> (a r) n")).then_inc(small_in, 16)
                sp.dma_start(up[32:33, d, :], io[b]).then_inc(small_in, 16)
                sp.dma_start(s_at[d][:, :, :], io["state_gla"][0, 0, d].rearrange("(p h) k v -> (h k) p v", p=2)).then_inc(st_in, 16)

            def load_q(r, p):
                for h in range(2):
                    sp.dma_start(q2[h * HD:(h + 1) * HD, p, h * HD:(h + 1) * HD],
                                 io["qkt"][p, h * HD:(h + 1) * HD, bass.ds(r * GRID_W, GRID_W)]).then_inc(q_in[p], 16)

            def load_tile(d, i):
                tok = tile_of(d, i) * P
                sp.dma_start(at[d][:, :], io["p1"][bass.ds(tok, P), P1_A + RANK * d:P1_A + RANK * (d + 1)]).then_inc(t_in[d], 16)
                sp.dma_start(qkv[d][:, :], io["p1"][bass.ds(tok, P), P1_QKD:P1_GD]).then_inc(t_in[d], 16)

            sp.wait_ge(q_zero, 1)
            for p in range(2):
                sp.dma_start(k_t[:, p, 0:KV0 * GRID_W], io["qkt"][2 + p, :, 0:KV0 * GRID_W]).then_inc(k0_in, 16)
                load_q(0, p)
            flat = io["toep"].rearrange("n q x -> n (q x)")[:, GRID_W - 1:GRID_W - 1 + GRID_W * (P - 1)]
            skew = flat.rearrange("n (q x) -> q n x", x=P - 1)[:, :, 0:GRID_W]
            for h in range(NH):
                sp.dma_start(bias[(h % 2) * 64:(h % 2) * 64 + 64, h // 2], skew[:, h * NDR:(h + 1) * NDR, :]).then_inc(bias_in, 16)
            v_rows = io["p1"][0:N_GRID, P1_V:P1_G].rearrange("(j t) c -> t j c", t=GRID_W)
            for h in range(2):
                sp.dma_start(v2[h * GRID_W:(h + 1) * GRID_W, 0:KV0, :], v_rows[:, h:h + KV0, :]).then_inc(v0_in, 16)
            for d in DIRS:
                load_tile(d, 0)

            def load_keys(c):
                a, b = (KV0 + n * (ROWS - KV0) // 4 for n in (c, c + 1))
                for p in range(2):
                    sp.dma_start(k_t[:, p, a * GRID_W:b * GRID_W], io["qkt"][2 + p, :, a * GRID_W:b * GRID_W]).then_inc(kv_in, 16)

            def load_values(c):
                a, b = KV0 + c * (ROWS - KV0) // 4, min(KV0 + (c + 1) * (ROWS - KV0) // 4, ROWS - 1)
                for h in range(2):
                    sp.dma_start(v2[h * GRID_W:(h + 1) * GRID_W, a:b, :], v_rows[:, h + a:h + b, :]).then_inc(kv_in, 16)
                if c == 3:
                    for p in range(2):
                        sp.dma_start(kp_t[:, p, :], io["qkt"][2 + p, :, N_GRID:N_TOK]).then_inc(kv_in, 16)
                    sp.dma_start(vp[:, :, :], io["p1"][N_GRID:N_TOK, P1_V:P1_G].rearrange("(m p) c -> p m c", p=P)).then_inc(kv_in, 16)

            for p in range(2):
                sp.wait_ge(s_done, p + 1)
                load_q(1, p)
            sp.sem_inc(o_sent, 16)
            for r, _, nxt, _, d, i in attention_rows(sp):
                pd, pi = before(d, i)
                ahead(sp, 2 * r + 3, 2 * r + 4, (r + 2) * GRID_W * 4, r * GRID_W * 4, pi + 1, tile_of(pd, pi + 1) * (P * P1_W * 4))
                more = not isinstance(r, int) or r + 2 < N_TOK // GRID_W
                if more:
                    sp.wait_ge(s_done, 2 * r + 3)
                    load_q(r + 2, 0)
                if isinstance(r, int) and r < 4:
                    load_keys(r)
                if not isinstance(r, int) or 1 <= r <= 2 * STEPS - 2:
                    sp.wait_ge(S[pd]["o_mm"], pi + 1)
                    load_tile(pd, pi + 1)
                if more:
                    sp.wait_ge(s_done, 2 * r + 4)
                    load_q(r + 2, 1)
                if isinstance(r, int) and r < 4:
                    load_values(r)
                sp.wait_ge(o_done, 4 * r + 8)
                sp.dma_start(io["ya"][bass.ds(r, 1)].rearrange("a t p d -> (a t) p d"), o_sb[:, :, :]).then_inc(o_sent, 16)
            for name, c0 in (("new_cache_k", W_GRP), ("new_cache_v", P1_V)):
                sp.dma_start(io[name].rearrange("a l h s d -> (a l h) s d"),
                             io["p1"][N_GRID:N_TOK, c0:c0 + W_GRP].rearrange("s (h d) -> h s d", h=NH)).then_inc(cache_out, 16)

            sp.wait_ge(o_sent, 16 * (N_TOK // GRID_W + 1))
            sp.wait_ge(cache_out, 32)

        @block.gpsimd
        def _(pool):
            n = 0

            def step(ins):
                nonlocal n
                ins.then_inc(consts, 1)
                n += 1

            pool.memset(q2[:, :, :], 0.0).then_inc(q_zero, 1)
            step(pool.memset(up[:, :, :], 0.0))
            for d in DIRS:
                step(pool.memset(aug[d][:, :], 0.0))
                step(pool.memset(e_rest[d][:, :, :], 0.0))
                step(pool.memset(qd_t[d][:, :, :], 0.0))
            step(pool.memset(tri[:, :, :, :], 1.0 / TAU))
            step(pool.memset(mask[:, :, :], 1.0))
            step(pool.memset(ind[:, :], 1.0 / TAU))
            pool.wait_ge(consts, n)
            for d in DIRS:
                step(pool.memset(aug[d][32:33, :], 1.0))
            cuts = []
            for d in DIRS:
                sign = 1 if d == 0 else -1
                cuts += [(tri[:, d, 0, :], 0, sign), (tri[:, d, 1, :], -1, -sign), (mask[:, d, :], 0, sign)]
            for view, base, sign in cuts:
                pool.wait_ge(consts, n)
                step(pool.affine_select(out=view, in_=view, compare_op=ALU.is_ge, fill=0.0, base=base,
                                        pattern=[[sign, P]], channel_multiplier=-sign))
                pool.wait_ge(consts, n)
                step(pool.memset(view[0:C, C:P], 0.0))
                step(pool.memset(view[C:P, 0:C], 0.0))
            pool.wait_ge(consts, n)
            step(pool.memset(ind[0:C, 1:2], 0.0))
            step(pool.memset(ind[C:P, 0:1], 0.0))
            assert n == N_CONST
            pool.wait_ge(bias_in, 64)
            n = 0
            for h in range(2):
                for c0, c1, base, step, chan in ((0, GRID_W - WIN_W, WIN_W // 2, 1, -1), (WIN_W, GRID_W, WIN_W // 2 - 1 - WIN_W, -1, 1)):
                    part = bias[h * 64:(h + 1) * 64, :, :, c0:c1].rearrange("q p r x -> q (p r) x")
                    if n:
                        pool.wait_ge(bias_set, n)
                    pool.affine_select(out=part, in_=part, compare_op=ALU.is_ge, fill=NEG, base=base,
                                       pattern=[[0, 2 * NDR], [step, c1 - c0]], channel_multiplier=chan).then_inc(bias_set, 1)
                    n += 1
            for r, _, _, _, d, i in attention_rows(pool):
                k = qkv[d][:, W_GRP:2 * W_GRP]
                pool.wait_ge(S[d]["exps"], i + 1)
                pool.tensor_tensor(k_e[d][:, :, :], k.unsqueeze(1).broadcast_to([P, 2, W_GRP]), e_rest[d][:, :, :], ALU.mult).then_inc(S[d]["ke_done"], 1)

        @block.scalar
        def _(act):
            act.sem_inc(t1_sb, 1)
            for buf, name, landed in ((ck, "cache_k", ck_in), (cv, "cache_v", cv_in)):
                for m in range(CC):
                    act.dma_start(buf[:, m, :, :], io[name][0, 0, :, m * P:(m + 1) * P, :].rearrange("h p d -> p h d")).then_inc(landed, 16)
                act.wait_ge(k0_in, 32)
            for d in DIRS:
                act.sem_inc(S[d]["o_sent"], 16)

            def exps(r, rs, p):
                act.wait_ge(max_done, 2 * r + p + 1)
                if rs is None:
                    act.activation(s_sb[p][:, 0:N_PROMPT], ps_c[p][:, 0:N_PROMPT], ACT.Exp, bias=neg_m[:, p:p + 1],
                                   accum_out=total[:, p:p + 1]).then_inc(exp_done, 1)
                else:
                    act.activation(s_sb[p][:, 0:W], s_sb[p][:, 0:W], ACT.Exp, bias=neg_m[:, p:p + 1], accum_out=sums[:, p, 0:1])
                    act.activation(s_sb[p][:, W:], ps_c[p][:, :], ACT.Exp, bias=neg_m[:, p:p + 1],
                                   accum_out=sums[:, p, 1:2]).then_inc(exp_done, 1)

            for p in range(2):
                exps(0, 0, p)

            def log_decays(d, i):
                act.wait_ge(S[d]["nab_done"], i + 1)
                act.activation(ez[d][:, :], nab[d][:, :], ACT.Exp).then_inc(S[d]["ez_done"], 1)
                act.wait_ge(S[d]["ez_done"], i + 1)
                act.activation(lz[d][:, :], ez[d][:, :], ACT.Ln, bias=1.0).then_inc(S[d]["lz_done"], 1)

            def decays(d, i):
                act.wait_ge(S[d]["c_mm"], i + 1)
                act.activation(e_cum[d][:, :], ps_s[:, 0:W_GRP], ACT.Exp)
                act.activation(e_neg[d][:, :], ps_s[:, 0:W_GRP], ACT.Exp, scale=-1.0)
                for c in range(2):
                    rows = slice(c * C, (c + 1) * C)
                    act.activation(e_rest[d][rows, c, :], ps_s[rows, W_GRP:], ACT.Exp)
                act.activation(decay[d][:, :, :], ps_z[:, W_GRP:W_GRP + 4].rearrange("p (a b) -> p a b", a=2), ACT.Exp).then_inc(S[d]["exps"], 1)

            def keep_turned(d, i):
                act.wait_ge(S[d]["turned"], i + 1)
                turned = ps_s[:, :].rearrange("p (a b) -> p a b", a=4)
                act.activation(kd_t[d][:, :, :], turned[:, 2:4, :], ACT.Copy)
                for odd in range(2):
                    rows = slice(64 * odd, 64 * odd + 64)
                    last = act.activation(qd_t[d][rows, odd::2, :], turned[rows, 0:2, :], ACT.Copy)
                last.then_inc(S[d]["turned_sb"], 1)

            def store_out(d, i):
                act.wait_ge(S[d]["o_done"], i + 1)
                act.dma_start(io["od"][d, bass.ds(tile_of(d, i) * P, P), :], od_sb[d][:, :]).then_inc(S[d]["o_sent"], 16)

            for r, rs, nxt, nrs, d, i in attention_rows(act):
                prev = None if isinstance(r, int) and r == 0 else before(d, i)
                for p in range(2):
                    if rs is not None:
                        act.wait_ge(t_done, 4 * r + 2 * p + 2)
                        act.activation(p_t[p][:, W:], ps_t[1][:, :], ACT.Copy).then_inc(t1_sb, 1)
                    if p == 0 and prev:
                        keep_turned(*prev)
                    if p == 1:
                        decays(d, i)
                    if nxt is not None:
                        exps(r + 1, nrs, p)
                    if p == 0:
                        log_decays(d, i)
                if prev:
                    store_out(*prev)
            keep_turned(1, STEPS - 1)
            store_out(1, STEPS - 1)
            for d in DIRS:
                act.wait_ge(S[d]["o_sent"], 16 * (STEPS + 1))
                act.wait_ge(S[d]["new_done"], 2 * STEPS + 2)
                act.dma_start(io["new_state_gla"][0, 0, d].rearrange("(p h) k v -> (h k) p v", p=2),
                              s_at[d][:, :, :]).then_inc(S[d]["st_out"], 16)
            for d in DIRS:
                act.wait_ge(S[d]["st_out"], 16)

        @block.tensor
        def _(pe):
            pe.wait_ge(ck_in, CC * 16)
            for p in range(2):
                for m in range(CC):
                    last = pe.transpose(ps_t[p][:, m * P:(m + 1) * P], ck[:, m, 2 * p:2 * p + 2, :].rearrange("k h d -> k (h d)"),
                                        keep["ident"][:, :])
            last.then_inc(ckt_mm, 1)
            pe.wait_ge(k0_in, 2 * 16)

            def scores(r, rs, p):
                pe.wait_ge(q_in[p], 32 * r + 32)
                if not isinstance(r, int) or r or p:
                    pe.wait_ge(max_done, 2 * r + p)
                if rs is None:
                    pe.matmul(ps_c[p][:, 0:N_PROMPT], q2[:, p, :], kp_t[:, p, :], start=True, stop=True).then_inc(s_done, 1)
                else:
                    pe.matmul(ps_w[:, :], q2[:, p, :], k_t[:, p, bass.ds(rs * GRID_W, W)], start=True, stop=True)
                    pe.matmul(ps_c[p][:, :], q2[:, p, :], ck_t[:, p, :], start=True, stop=True).then_inc(s_done, 1)

            pe.wait_ge(ckt_sb, 2)
            for p in range(2):
                scores(0, 0, p)

            def turn(r, rs, p):
                pe.wait_ge(exp_done, 2 * r + p + 1)
                pe.wait_ge(t0_sb, 2 * r + p + 1)
                for m in range(N_PROMPT // P if rs is None else CH):
                    last = pe.transpose(ps_t[0][:, m * P:(m + 1) * P], s_sb[p][:, m * P:(m + 1) * P], keep["ident"][:, :])
                last.then_inc(t_done, 2 if rs is None else 1)
                if rs is not None:
                    pe.wait_ge(t1_sb, 2 * r + p + 1)
                    for m in range(CC):
                        last = pe.transpose(ps_t[1][:, m * P:(m + 1) * P], s_sb[p][:, W + m * P:W + (m + 1) * P], keep["ident"][:, :])
                    last.then_inc(t_done, 1)

            def values(r, rs, p, prev=None):
                pe.wait_ge(t0_sb, 2 * r + p + 2)
                pe.wait_ge(o_done, 4 * r + 2 * p + 4)
                if prev:
                    pe.wait_ge(S[prev[0]]["mid_done"], 2 * prev[1] + 2)
                if rs is not None:
                    pe.wait_ge(t1_sb, 2 * r + p + 2)
                    todo = [(CH + m, cv[:, m, :, :].rearrange("k h d -> k (h d)")) for m in range(CC)]
                    todo += [(m, v2[:, bass.ds(rs + 2 * m, 1), :].rearrange("k a c -> k (a c)")) for m in range(CH)]
                else:
                    todo = [(m, vp[:, m, :]) for m in range(N_PROMPT // P)]
                for n, (m, v) in enumerate(todo):
                    last = pe.matmul(ps_o[p], p_t[p][:, m * P:(m + 1) * P], v[:, 2 * p * HD:2 * p * HD + P],
                                     start=(n == 0), stop=(n == len(todo) - 1))
                last.then_inc(pv_done, 1)

            def d_gate(d, i):
                pe.wait_ge(t_in[d], 32 * i + 32)
                pe.transpose(ps_z[0:RANK, W_GRP:W_GRP + P], at[d][:, :], keep["ident"][:, :]).then_inc(S[d]["at_mm"], 1)

            def d_z(d, i):
                pe.wait_ge(S[d]["at_sb"], i + 1)
                pe.matmul(ps_z[:, W_GRP:], aug[d][:, :], up[:, d, :], start=True, stop=True).then_inc(S[d]["z_mm"], 1)

            def d_sums(d, i, prev):
                if prev:
                    pe.wait_ge(S[prev[0]]["o_done"], prev[1] + 1)
                pe.wait_ge(S[d]["la_done"], i + 1)
                pe.matmul(ps_s[:, 0:W_GRP], tri[:, d, 0, :], la[d][:, :], start=True, stop=True)
                pe.matmul(ps_s[:, W_GRP:], tri[:, d, 1, :], la[d][:, :], start=True, stop=True)
                for p in range(2):
                    last = pe.matmul(ps_z[:, W_GRP + 2 * p:W_GRP + 2 * p + 2], la[d][:, p * P:(p + 1) * P], ind[:, :], start=True, stop=True)
                last.then_inc(S[d]["c_mm"], 1)

            def d_turn(d, i, row):
                pe.wait_ge(S[d]["qd_done"], i + 1)
                pe.wait_ge(S[d]["ke_done"], i + 1)
                for n, src in enumerate((q_d[d], q_d[d], k_i[d], k_i[d])):
                    last = pe.transpose(ps_s[:, n * P:(n + 1) * P], src[:, (n % 2) * P:(n % 2) * P + P], keep["ident"][:, :])
                last.then_inc(S[d]["turned"], 1)
                pe.wait_ge(o_done, 4 * row + 4)
                for c in range(2):
                    for h in range(NH):
                        last = pe.matmul(ps_u[64 * (h % 2):64 * (h % 2) + 64, c, h // 2, :],
                                         k_e[d][:, c, h * HD:(h + 1) * HD],
                                         qkv[d][:, 2 * W_GRP + h * HD:2 * W_GRP + (h + 1) * HD], start=True, stop=True)
                last.then_inc(S[d]["u_mm"], 1)

            def d_scores(d, i):
                pe.wait_ge(S[d]["turned_sb"], i + 1)
                for h in range(NH):
                    last = pe.matmul(ps_s[:, h * P:(h + 1) * P], kd_t[d][:, h // 2, :], qd_t[d][:, h, :], start=True, stop=True)
                last.then_inc(S[d]["att_mm"], 1)

            def d_out(d, i):
                pe.wait_ge(S[d]["mid_done"], 2 * i + 2)
                pe.wait_ge(S[d]["att_sb"], i + 1)
                for h in range(NH):
                    for n in range(2):
                        c = n if d == 0 else 1 - n
                        pe.matmul(ps_z[c * C:(c + 1) * C, h * HD:(h + 1) * HD], qd_t[d][:, h, c * C:(c + 1) * C],
                                  (s_mid if n else s_at)[d][:, h // 2, :], start=True, stop=False, skip_group_check=True)
                    last = pe.matmul(ps_z[:, h * HD:(h + 1) * HD], att[d][:, h, :],
                                     qkv[d][:, 2 * W_GRP + h * HD:2 * W_GRP + (h + 1) * HD],
                                     start=False, stop=True, skip_group_check=True)
                last.then_inc(S[d]["o_mm"], 1)

            pe.wait_ge(consts, N_CONST)
            pe.wait_ge(small_in, 64)
            pe.wait_ge(st_in, 32)
            pe.wait_ge(v0_in, 2 * 16)
            pe.wait_ge(cv_in, CC * 16)
            for r, rs, nxt, nrs, d, i in attention_rows(pe):
                if not isinstance(r, int) or r == ROWS - WIN_H // 2:
                    pe.wait_ge(kv_in, 19 * 16)
                prev = None if isinstance(r, int) and r == 0 else before(d, i)
                turn(r, rs, 0)
                if prev:
                    d_turn(*prev, r)
                d_gate(d, i)
                if nxt is not None:
                    scores(r + 1, nrs, 0)
                if prev:
                    d_scores(*prev)
                d_z(d, i)
                values(r, rs, 0, prev)
                turn(r, rs, 1)
                if prev:
                    pe.wait_ge(S[d]["nab_done"], i + 1)
                    d_out(*prev)
                if nxt is not None:
                    scores(r + 1, nrs, 1)
                d_sums(d, i, prev)
                values(r, rs, 1)
            d_turn(1, STEPS - 1, 2 * STEPS)
            d_scores(1, STEPS - 1)
            d_out(1, STEPS - 1)

        @block.vector
        def _(dve):
            dve.wait_ge(ckt_mm, 1)
            for p in range(2):
                dve.tensor_copy(ck_t[:, p, :], ps_t[p][:, :]).then_inc(ckt_sb, 1)
            dve.sem_inc(t0_sb, 1)
            dve.sem_inc(o_done, 4)
            dve.wait_ge(bias_set, 4)
            dve.wait_ge(consts, N_CONST)
            dve.wait_ge(st_in, 32)
            for d in DIRS:
                dve.sem_inc(S[d]["new_done"], 2)

            def maxima(r, rs, p):
                dve.wait_ge(s_done, 2 * r + p + 1)
                if rs is None:
                    dve.tensor_reduce(neg_m[:, p:p + 1], ps_c[p][:, 0:N_PROMPT], AX.X, ALU.max, negate=True).then_inc(max_done, 1)
                    return
                dve.tensor_reduce(max_c[:, p:p + 1], ps_c[p][:, :], AX.X, ALU.max).then_inc(maxc_done, 1)
                at = WIN_H // 2 - 1 if not isinstance(rs, int) else rs - r + WIN_H - 1
                dve.tensor_tensor_reduce(out=s_sb[p][:, 0:W].rearrange("k (r x) -> k r x", r=WIN_H), in0=ps_w[:, :].rearrange("k (r x) -> k r x", r=WIN_H), in1=bias[:, p, at:at + WIN_H, :],
                                         scale=1.0, scalar=NEG, op0=ALU.add, op1=ALU.max,
                                         accum_out=max_w[:, p:p + 1]).then_inc(w_done, 1)
                dve.wait_ge(maxc_done, 2 * r + p + 1)
                dve.wait_ge(w_done, 2 * r + p + 1)
                dve.tensor_scalar(neg_m[:, p:p + 1], max_w[:, p:p + 1], max_c[:, p:p + 1], -1.0, ALU.max, ALU.mult).then_inc(max_done, 1)

            for p in range(2):
                maxima(0, 0, p)

            def state(d, i, n):
                c = n if d == 0 else 1 - n
                if n:
                    dve.wait_ge(S[d]["o_mm"], i + 1)
                    if isinstance(i, int) and i == GRID_T - 1:
                        for p in range(2):
                            dve.memset(s_at[d][:, p, :], 0.0).then_inc(S[d]["new_done"], 1)
                        return
                else:
                    dve.wait_ge(S[d]["u_mm"], i + 1)
                dve.wait_ge(S[d]["mid_done" if n else "new_done"], 2 * i + 2)
                dst, src = (s_at[d], s_mid[d]) if n else (s_mid[d], s_at[d])
                if n == 0:
                    dve.tensor_copy(u_sb[:, :, :], ps_u[:, 1 - c, :, :]).then_inc(u_kept, 1)
                else:
                    dve.wait_ge(u_kept, 2 * i + d + 1)
                for p in range(2):
                    dve.scalar_tensor_tensor(dst[:, p, :], src[:, p, :], decay[d][:, p, c:c + 1], u_sb[:, p, :] if n else ps_u[:, c, p, :],
                                             ALU.mult, ALU.add).then_inc(S[d]["new_done" if n else "mid_done"], 1)

            def mask_scores(d, i):
                dve.wait_ge(S[d]["att_mm"], i + 1)
                dve.tensor_tensor(att[d][:, :, :], ps_s[:, :].rearrange("p (h t) -> p h t", h=NH),
                                  mask[:, d, :].unsqueeze(1).broadcast_to([P, NH, P]), ALU.mult).then_inc(S[d]["att_sb"], 1)

            def copy_out(d, i):
                dve.wait_ge(S[d]["o_mm"], i + 1)
                dve.wait_ge(S[d]["o_sent"], i * 16 + 16)
                dve.tensor_copy(od_sb[d][:, :], ps_z[:, 0:W_GRP]).then_inc(S[d]["o_done"], 1)

            for r, rs, nxt, nrs, d, i in attention_rows(dve):
                prev = None if isinstance(r, int) and r == 0 else before(d, i)
                for p in range(2):
                    u = 2 * r + p
                    dve.wait_ge(exp_done, u + 1)
                    if rs is not None:
                        dve.tensor_tensor(total[:, p:p + 1], sums[:, p, 0:1], sums[:, p, 1:2], ALU.add).then_inc(sum_done, 1)
                        dve.wait_ge(sum_done, u + 1)
                    dve.reciprocal(r_total[:, p:p + 1], total[:, p:p + 1]).then_inc(rsum_done, 1)
                    if p:
                        dve.wait_ge(S[d]["lz_done"], i + 1)
                        dve.tensor_tensor(la[d][:, :], low[d][:, :], lz[d][:, :], ALU.subtract).then_inc(S[d]["la_done"], 1)
                    dve.wait_ge(t_done, 2 * u + 1)
                    cols = N_PROMPT if rs is None else W
                    dve.tensor_copy(p_t[p][:, 0:cols], ps_t[0][:, 0:cols]).then_inc(t0_sb, 1)
                    if p == 0:
                        if prev:
                            state(*prev, 0)
                        dve.wait_ge(S[d]["at_mm"], i + 1)
                        dve.tensor_copy(aug[d][0:RANK, :], ps_z[0:RANK, W_GRP:W_GRP + P]).then_inc(S[d]["at_sb"], 1)
                    elif prev:
                        copy_out(*prev)
                        state(*prev, 1)
                    if nxt is not None:
                        maxima(r + 1, nrs, p)
                    if p == 0:
                        if prev:
                            mask_scores(*prev)
                        dve.wait_ge(S[d]["z_mm"], i + 1)
                        dve.tensor_scalar(low[d][:, :], ps_z[:, W_GRP:], 0.0, None, ALU.min).then_inc(S[d]["low_done"], 1)
                        dve.wait_ge(S[d]["low_done"], i + 1)
                        dve.scalar_tensor_tensor(nab[d][:, :], low[d][:, :], 2.0, ps_z[:, W_GRP:], ALU.mult, ALU.subtract).then_inc(S[d]["nab_done"], 1)
                    else:
                        dve.wait_ge(S[d]["exps"], i + 1)
                        dve.wait_ge(t_in[d], 32 * i + 32)
                        dve.tensor_tensor(k_i[d][:, :], qkv[d][:, W_GRP:2 * W_GRP], e_neg[d][:, :], ALU.mult)
                        dve.scalar_tensor_tensor(q_d[d][:, :], qkv[d][:, 0:W_GRP], HD ** -0.5, e_cum[d][:, :], ALU.mult, ALU.mult).then_inc(S[d]["qd_done"], 1)
                    dve.wait_ge(pv_done, u + 1)
                    dve.wait_ge(rsum_done, u + 1)
                    dve.wait_ge(o_sent, 16 * r + 16)
                    for h in range(2):
                        dve.tensor_scalar(o_sb[h * 64:h * 64 + 64, p, :], ps_o[p][h * 64:h * 64 + 64, h * HD:(h + 1) * HD],
                                          r_total[h * 64:h * 64 + 64, p:p + 1], None, ALU.mult).then_inc(o_done, 1)
            last = (1, STEPS - 1)
            state(*last, 0)
            mask_scores(*last)
            copy_out(*last)
            state(*last, 1)


def fourier_groups(eng):
    with eng.Fori(1, 5) as n:
        for s in range(2):
            yield n * 2 - 2 + s, s


def fourier_stage(nc, io, keep):
    GW = 8
    BANKS = GW // 2
    with stage(nc) as (ctx, new_sem):
        sb = lambda name, shape, dt=F32: ctx.enter_context(nc.sbuf_tensor("f_" + name, shape, dt))
        sem = lambda name: new_sem("f_" + name)
        first = sb("first", [P, P])
        second = [sb(f"second{s}", [P, GW, 64]) for s in range(2)]
        gx = [sb(f"gx{s}", [P, GW, W_GRP]) for s in range(2)]
        yx = [sb(f"yx{s}", [P, GW, W_GRP]) for s in range(2)]
        whole = sb("whole", [P, 2, 2, N_PROMPT])
        gp = sb("gp", [P, 2, 2, W_GRP])
        yp = sb("yp", [P, 2, W_GRP])
        ps = [ctx.enter_context(nc.psum_tensor(f"f_ps{b}", [P, 2, W_GRP], F32)) for b in range(BANKS)]
        ps_p = ctx.enter_context(nc.psum_tensor("f_psp", [P, 2, W_GRP], F32))
        consts, gp_in = sem("consts"), sem("gp_in")
        slot_in = [[sem(f"in{q}{s}") for s in range(2)] for q in range(2)]
        mm = [sem(f"mm{q}") for q in range(2)]
        by_act = [sem(f"by_act{q}") for q in range(2)]
        by_dve = [sem(f"by_dve{q}") for q in range(2)]
        sent = [[sem(f"sent{q}{s}") for s in range(2)] for q in range(2)]
        yp_mm, yp_sb, yp_sent = sem("yp_mm"), sem("yp_sb"), sem("yp_sent")
        block = ctx.enter_context(nc.Block())

        @block.sync
        def _(sp):
            sp.dma_start(first[:, :], io["dft_first"]).then_inc(consts, 16)
            gv = io["g"][:, 0:N_GRID, :].rearrange("r (a b) c -> r a b c", b=64)
            for i, s in fourier_groups(sp):
                ahead(sp, i * BANKS + BANKS, i * (GW * W_GRP * 4))
                sp.wait_ge(mm[0], i * BANKS + BANKS)
                for r in range(2):
                    sp.dma_start(gx[s][64 * r:64 * r + 64, :, :], gv[r, :, bass.ds(i * GW, GW), :]).then_inc(slot_in[0][s], 16)
            for s in range(2):
                sp.wait_ge(sent[0][s], 80)
            yv = io["y1"].rearrange("(r k) b c -> r b k c", r=2)
            for i, s in fourier_groups(sp):
                ahead(sp, i * BANKS + BANKS, i * (GW * W_GRP * 4 * 64), i * (GW * 64 * 4))
                sp.wait_ge(mm[1], i * BANKS + BANKS)
                for r in range(2):
                    sp.dma_start(gx[s][64 * r:64 * r + 64, :, :], yv[r, :, bass.ds(i * GW, GW), :]).then_inc(slot_in[1][s], 16)
                sp.dma_start(second[s][:, :, :], io["dft_second"][:, bass.ds(i * GW, GW), :]).then_inc(slot_in[1][s], 16)

        @block.gpsimd
        def _(pool):
            for r in range(2):
                pool.dma_start(gp[:, r, :, :], io["g"][r, N_GRID:N_TOK, :].rearrange("(j p) c -> p j c", p=P)).then_inc(gp_in, 16)
                pool.dma_start(whole[:, r, :, :], io["dft_whole"][r].rearrange("(j p) k -> p j k", p=P)).then_inc(gp_in, 16)

        @block.tensor
        def _(pe):
            for q in range(2):
                pe.sem_inc(mm[q], 2 * BANKS)
            pe.wait_ge(consts, 16)
            for q in range(2):
                for i, s in fourier_groups(pe):
                    pe.wait_ge(slot_in[q][s], (i - s) * (8 * (2 + q)) + 16 * (2 + q))
                    for n in range(BANKS):
                        pe.wait_ge((by_act, by_dve)[n % 2][q], i * (BANKS // 2) + n // 2 + 1)
                        if q == 0:
                            last = pe.matmul(ps[n][:, :, :], first[:, :], gx[s][:, 2 * n:2 * n + 2, :], start=True, stop=True)
                        else:
                            for k in range(2):
                                last = pe.matmul(ps[n][0:64, k, :], second[s][:, 2 * n + k, :], gx[s][:, 2 * n + k, :], start=True, stop=True)
                        last.then_inc(mm[q], 1)
            pe.wait_ge(gp_in, 64)
            for kc in range(2):
                for r in range(2):
                    for j in range(2):
                        last = pe.matmul(ps_p[:, kc, :], whole[:, r, j, kc * P:(kc + 1) * P], gp[:, r, j, :],
                                         start=(r == 0 and j == 0), stop=(r == 1 and j == 1))
            last.then_inc(yp_mm, 1)

        @block.scalar
        def _(act):
            for q in range(2):
                act.sem_inc(by_act[q], BANKS // 2)
                for s in range(2):
                    act.sem_inc(sent[q][s], 16)
            for q in range(2):
                rows = slice(0, P if q == 0 else 64)
                for i, s in fourier_groups(act):
                    act.wait_ge(sent[q][s], (i - s) * 8 + 16)
                    for n in range(0, BANKS, 2):
                        act.wait_ge(mm[q], i * BANKS + n + 2 * BANKS + 1)
                        act.activation(yx[s][rows, 2 * n:2 * n + 2, :], ps[n][rows, :, :], ACT.Copy).then_inc(by_act[q], 1)
                    act.wait_ge(by_act[q], i * (BANKS // 2) + BANKS)
                    act.wait_ge(by_dve[q], i * (BANKS // 2) + BANKS)
                    if q == 0:
                        act.dma_start(io["y1"][:, bass.ds(i * GW, GW), :], yx[s][:, :, :]).then_inc(sent[q][s], 16)
                    else:
                        act.dma_start(io["yc"][0:N_GRID, :].rearrange("(k2 k1) c -> k2 k1 c", k1=64)[:, bass.ds(i * GW, GW), :],
                                      yx[s][rows, :, :]).then_inc(sent[q][s], 16)
            act.wait_ge(yp_mm, 1)
            act.activation(yp[:, :, :], ps_p[:, :, :], ACT.Copy).then_inc(yp_sb, 1)
            act.wait_ge(yp_sb, 1)
            act.dma_start(io["yc"][N_GRID:N_TOK, :].rearrange("(j p) c -> p j c", p=P), yp[:, :, :]).then_inc(yp_sent, 16)
            act.wait_ge(yp_sent, 16)
            for s in range(2):
                act.wait_ge(sent[1][s], 80)

        @block.vector
        def _(dve):
            for q in range(2):
                dve.sem_inc(by_dve[q], BANKS // 2)
            for q in range(2):
                rows = slice(0, P if q == 0 else 64)
                for i, s in fourier_groups(dve):
                    dve.wait_ge(sent[q][s], (i - s) * 8 + 16)
                    for n in range(1, BANKS, 2):
                        dve.wait_ge(mm[q], i * BANKS + n + 2 * BANKS + 1)
                        dve.tensor_copy(yx[s][rows, 2 * n:2 * n + 2, :], ps[n][rows, :, :]).then_inc(by_dve[q], 1)


def output_stage(nc, io, keep):
    CH = [(0, 128), (64, 192)] + [(n * P, n * P + 64) for n in range(2, K8)]
    PIECES = [(h, m) for h in range(2) for m in range(K8 // 2)]
    LOADS = 11
    with stage(nc) as (ctx, new_sem):
        sb = lambda name, shape, dt=F32: ctx.enter_context(nc.sbuf_tensor("o_" + name, shape, dt))
        sem = lambda name: new_sem("o_" + name)
        two = lambda name, shape, dt=F32: [sb(f"{name}{s}", shape, dt) for s in range(2)]
        w_hi = sb("w_hi", [P, K8, DM], F32R)
        w_lo = sb("w_lo", [P, K8, DM], F32R)
        stage_w = two("stage_w", [P, 2, 512])
        gate = sb("gate", [P, 2, DM])
        gn = sb("gn", [P, HD])
        gn8 = sb("gn8", [P, HD])
        taps = sb("taps", [P, 3, W_GRP])
        half_pow = sb("half_pow", [P, NH])
        eps = sb("eps", [P, NH])
        x = two("x", [P, DM])
        ya = two("ya", [P, 2, 2, HD])
        g_ad = two("g_ad", [P, 2, W_GRP])
        gbc = two("gbc", [P, 2, W_GRP])
        yc = two("yc", [P, W_GRP])
        od = two("od", [P, 2, W_GRP])
        u = two("u", [P, 3, W_GRP])
        u_w = sb("u_w", [P, 3, W_GRP])
        conv = sb("conv", [P, W_GRP])
        o = sb("o", [P, W_GRP])
        o_sq = sb("o_sq", [P, W_GRP])
        ss = sb("ss", [P, NH])
        ve = sb("ve", [P, NH])
        r = sb("r", [P, NH])
        o_n = sb("o_n", [P, W_GRP])
        gg = sb("gg", [P, W_GRP])
        mix = two("mix", [P, 4, W_GRP])
        y_hi = two("y_hi", [P, K8, P], F32R)
        y_lo = two("y_lo", [P, K8, P], F32R)
        gx = two("gx", [P, DM])
        y = two("y", [P, DM])
        ps_t = [ctx.enter_context(nc.psum_tensor(f"o_ps_t{b}", [P, 4, P], F32)) for b in range(2)]
        ps_y = [[ctx.enter_context(nc.psum_tensor(f"o_ps_y{s}{h}", [P, 512], F32)) for h in range(2)] for s in range(2)]
        w_in = [sem(f"w_in{s}") for s in range(2)]
        w_hi_done, w_lo_done, small_in, taps_in, gn_in, gn_done, pow_set = (
            sem(n) for n in ("w_hi_done", "w_lo_done", "small_in", "taps_in", "gn_in", "gn_done", "pow_set"))
        mix_in = [sem(f"mix_in{s}") for s in range(2)]
        x_in = [sem(f"x_in{s}") for s in range(2)]
        o_sum, sq_done, ss_done, ve_done, r_done, on_done, gg_done, mixed, turned, hi_done, lo_done = (
            sem(n) for n in ("o_sum", "sq_done", "ss_done", "ve_done", "r_done", "on_done", "gg_done", "mixed", "turned", "hi_done", "lo_done"))
        uw_done, conv_done = sem("uw_done"), sem("conv_done")
        mm, gated, added = sem("mm"), sem("gated"), sem("added")
        sent = [sem(f"sent{s}") for s in range(2)]
        block = ctx.enter_context(nc.Block())

        @block.sync
        def _(sp):
            def load_mix(t, s):
                j = kind(t)
                tok = t * P
                for a in range(2):
                    sp.dma_start(ya[s][64 * a:64 * a + 64, :, :, :].rearrange("q h p d -> q h (p d)"),
                                 io["ya"][bass.ds(t * 2 + a, 1)].rearrange("a (h q) p d -> (a q) h (p d)", h=2)).then_inc(mix_in[s], 16)
                sp.dma_start(g_ad[s][:, 0, :], io["p1"][bass.ds(tok, P), P1_G:P1_G + W_GRP]).then_inc(mix_in[s], 16)
                sp.dma_start(g_ad[s][:, 1, :], io["p1"][bass.ds(tok, P), P1_GD:P1_GD + W_GRP]).then_inc(mix_in[s], 16)
                sp.dma_start(gbc[s][:, :, :], io["gates_bc"][bass.ds(tok, P), :].rearrange("t (a c) -> t a c", a=2)).then_inc(mix_in[s], 16)
                sp.dma_start(yc[s][:, :], io["yc"][bass.ds(tok, P), :]).then_inc(mix_in[s], 16)
                for d in range(2):
                    sp.dma_start(od[s][:, d, :], io["od"][d, bass.ds(tok, P), :]).then_inc(mix_in[s], 16)
                for a in range(3):
                    sp.dma_start(u[s][:, a, :], io["conv_u"][bass.ds(tok + (SKIP[j] - 1 + a), P), :]).then_inc(mix_in[s], 16)

            sp.dma_start(gn[:, :], io["gla_norm_g"].broadcast_to([P, HD])).then_inc(gn_in, 16)
            load_mix(0, 0)
            load_mix(1, 1)
            sp.dma_start(taps[:, :, :].rearrange("p a c -> p (a c)"),
                         io["conv_w"].rearrange("a t c -> a (t c)").broadcast_to([P, 3 * W_GRP])).then_inc(taps_in, 16)
            for n, (h, m) in enumerate(PIECES):
                if n >= 2:
                    sp.wait_ge(w_lo_done, n - 1)
                for b in range(2):
                    for a, row in enumerate(CH[2 * m + b]):
                        sp.dma_start(stage_w[n % 2][64 * a:64 * a + 64, b, :],
                                     io["w_out"][0, row:row + 64, 512 * h:512 * h + 512]).then_inc(w_in[n % 2], 16)
            for j in range(2):
                sp.dma_start(gate[:, j, :], io["mod"][j:j + 1, 2 * DM:3 * DM].broadcast_to([P, DM])).then_inc(small_in, 16)
            sp.wait_ge(mixed, 2)
            load_mix(2, 0)
            for t, s, j in tile_pairs(sp, 4):
                ahead(sp, t * 2 + 2, t + 3, t * (P * DM * 4), *((t + 3) * (P * n) for n in (4, 4 * W_GRP, 8 * W_GRP, 4 * P1_W)),
                      (t + 3) * (2 * GRID_W * W_GRP * 4))
                sp.wait_ge(added, t * 2 + 2)
                sp.dma_start(x[s][:, :], token_rows(io, "x_sample", "x_prompt", t, j)).then_inc(x_in[s], 16)
                if not (isinstance(t, int) and t + 3 > LAST):
                    sp.wait_ge(mixed, t + 3)
                    load_mix(t + 3, 1 - s)

        @block.gpsimd
        def _(pool):
            pool.memset(half_pow[:, :], -0.5).then_inc(pow_set, 1)
            pool.memset(eps[:, :], HD * EPS).then_inc(pow_set, 1)
            pool.wait_ge(pow_set, 2)
            pool.sem_inc(mixed, 1)
            pool.wait_ge(gn_done, 1)
            heads = lambda a: a.rearrange("t (h d) -> t h d", d=HD)

            def join(t, s):
                pool.wait_ge(mix_in[s], (t - s) * (LOADS * 8) + LOADS * 16)
                pool.wait_ge(turned, t * 2 + 2)
                pool.tensor_tensor(mix[s][:, 0, :].rearrange("t (h p d) -> t h p d", p=2, h=2), ya[s][:, :, :, :],
                                   g_ad[s][:, 0, :].rearrange("t (p h d) -> t h p d", p=2, h=2), ALU.mult)
                pool.tensor_tensor(mix[s][:, 2, :], gbc[s][:, 1, :], yc[s][:, :], ALU.mult)
                pool.wait_ge(mixed, t + 1)
                pool.tensor_tensor(heads(gg[:, :]), heads(g_ad[s][:, 1, :]), gn8[:, :].unsqueeze(1).broadcast_to([P, NH, HD]),
                                   ALU.mult).then_inc(gg_done, 1)
                pool.wait_ge(ss_done, t + 2)
                pool.tensor_tensor(ve[:, :], ss[:, :], eps[:, :], ALU.add).then_inc(ve_done, 1)
                pool.wait_ge(ve_done, t + 1)
                pool.tensor_tensor(r[:, :], ve[:, :], half_pow[:, :], ALU.pow).then_inc(r_done, 1)
                pool.wait_ge(conv_done, t + 2)
                pool.tensor_tensor(mix[s][:, 1, :], conv[:, :], gbc[s][:, 0, :], ALU.mult)
                pool.wait_ge(on_done, t + 2)
                pool.wait_ge(gg_done, t + 1)
                pool.tensor_tensor(mix[s][:, 3, :], o_n[:, :], gg[:, :], ALU.mult).then_inc(mixed, 1)

            for t in range(2):
                join(t, t)
            for t, s, j in tile_pairs(pool):
                if not (isinstance(t, int) and t + 2 > LAST):
                    join(t + 2, s)

        @block.scalar
        def _(act):
            for s in range(2):
                act.sem_inc(sent[s], 16)
            act.sem_inc(sq_done, 1)
            act.wait_ge(gn_in, 16)
            act.activation(gn8[:, :], gn[:, :], ACT.Copy, scale=8.0).then_inc(gn_done, 1)

            def square(t, s):
                act.wait_ge(o_sum, t + 1)
                act.wait_ge(ss_done, t + 1)
                act.activation(o_sq[:, :], o[:, :], ACT.Square).then_inc(sq_done, 1)

            def high(t, s, _):
                act.wait_ge(mm, t * 2 + 2)
                for b in range(2):
                    act.wait_ge(turned, t * 2 + b + 5)
                    act.activation(y_hi[s][:, 4 * b:4 * b + 4, :], ps_t[b][:, :, :], ACT.Copy).then_inc(hi_done, 1)

            square(0, 0)
            square(1, 1)
            for n, (h, m) in enumerate(PIECES):
                if n == len(PIECES) // 2:
                    high(0, 0, 0)
                act.wait_ge(w_in[n % 2], 64 * (n // 2 + 1))
                act.activation(w_hi[:, 2 * m:2 * m + 2, 512 * h:512 * h + 512], stage_w[n % 2][:, :, :], ACT.Copy).then_inc(w_hi_done, 1)
            for t, s, j in tile_pairs(act):
                prepare_next(high, t, s)
                if not (isinstance(t, int) and t + 2 > LAST):
                    square(t + 2, s)
                act.wait_ge(added, t * 2 + 6)
                act.dma_start(token_rows(io, "y_sample", "y_prompt", t, j), y[s][:, :]).then_inc(sent[s], 16)
            for s in range(2):
                act.wait_ge(sent[s], 16 + 16 * (N_TOK // P // 2))

        @block.tensor
        def _(pe):
            pe.sem_inc(mm, 4)
            pe.sem_inc(turned, 4)

            def turn(t, s, _):
                pe.wait_ge(mixed, t + 2)
                pe.wait_ge(lo_done, t * 2 + 2)
                for b in range(2):
                    for n in range(4):
                        c = 4 * b + n
                        last = pe.transpose(ps_t[b][:, n, :], mix[s][:, c // 2, (c % 2) * P:(c % 2) * P + P], keep["ident"][:, :])
                    last.then_inc(turned, 1)

            turn(0, 0, 0)
            for t, s, j in tile_pairs(pe):
                pe.wait_ge(lo_done, t * 2 + 4)
                for h in range(2):
                    pe.wait_ge(gated, t * 2 + h + 1)
                    pe.wait_ge(w_lo_done, (h + 1) * len(PIECES) // 2)
                    cols = slice(h * 512, h * 512 + 512)
                    product(pe, ps_y[s][h][:, :], lambda k: y_hi[s][:, k, :], lambda k: y_lo[s][:, k, :],
                            lambda k: w_hi[:, k, cols], lambda k: w_lo[:, k, cols]).then_inc(mm, 1)
                    if h == 0:
                        prepare_next(turn, t, s)

        @block.vector
        def _(dve):
            dve.sem_inc(gated, 4)
            dve.sem_inc(on_done, 1)
            dve.sem_inc(ss_done, 1)
            dve.sem_inc(lo_done, 2)
            dve.sem_inc(conv_done, 1)
            dve.sem_inc(added, 4)

            def combine(t, s):
                heads = lambda a: a.rearrange("t (h d) -> t h d", d=HD)
                dve.wait_ge(mix_in[s], (t - s) * (LOADS * 8) + LOADS * 16)
                dve.wait_ge(sq_done, t + 1)
                dve.wait_ge(on_done, t + 1)
                dve.tensor_tensor(o[:, :], od[s][:, 0, :], od[s][:, 1, :], ALU.add).then_inc(o_sum, 1)
                dve.wait_ge(conv_done, t + 1)
                dve.tensor_tensor(u_w[:, :, :], u[s][:, :, :], taps[:, :, :], ALU.mult).then_inc(uw_done, 1)
                dve.wait_ge(sq_done, t + 2)
                dve.tensor_reduce(ss[:, :], heads(o_sq[:, :]), AX.X, ALU.add).then_inc(ss_done, 1)
                dve.wait_ge(mixed, t + 1)
                dve.wait_ge(uw_done, t + 1)
                dve.tensor_reduce(conv[:, :], u_w[:, :, :].rearrange("p a c -> p c a"), AX.X, ALU.add).then_inc(conv_done, 1)
                dve.wait_ge(r_done, t + 1)
                dve.tensor_tensor(heads(o_n[:, :]), heads(o[:, :]), r[:, :].unsqueeze(2).broadcast_to([P, NH, HD]),
                                  ALU.mult).then_inc(on_done, 1)

            def low(t, s, _):
                for b in range(2):
                    dve.wait_ge(hi_done, t * 2 + b + 1)
                    dve.tensor_tensor(y_lo[s][:, 4 * b:4 * b + 4, :], ps_t[b][:, :, :], y_hi[s][:, 4 * b:4 * b + 4, :],
                                      ALU.subtract).then_inc(lo_done, 1)

            dve.wait_ge(taps_in, 16)
            combine(0, 0)
            combine(1, 1)
            for n, (h, m) in enumerate(PIECES):
                if n == len(PIECES) // 2:
                    low(0, 0, 0)
                part = slice(2 * m, 2 * m + 2), slice(512 * h, 512 * h + 512)
                dve.wait_ge(w_hi_done, n + 1)
                dve.tensor_tensor(w_lo[:, part[0], part[1]], stage_w[n % 2][:, :, :], w_hi[:, part[0], part[1]],
                                  ALU.subtract).then_inc(w_lo_done, 1)
            dve.wait_ge(small_in, 32)
            for t, s, j in tile_pairs(dve):
                prepare_next(low, t, s)
                dve.wait_ge(x_in[s], (t - s) * 8 + 16)
                for h in range(2):
                    if h and not (isinstance(t, int) and t + 2 > LAST):
                        combine(t + 2, s)
                    cols = slice(h * 512, h * 512 + 512)
                    dve.wait_ge(mm, t * 2 + h + 5)
                    dve.wait_ge(added, t * 2 + h + 1)
                    dve.tensor_tensor(gx[s][:, cols], ps_y[s][h][:, :], gate[:, j, cols], ALU.mult).then_inc(gated, 1)
                    dve.wait_ge(gated, t * 2 + h + 5)
                    dve.wait_ge(sent[s], (t - s) * 8 + 16)
                    dve.tensor_tensor(y[s][:, cols], gx[s][:, cols], x[s][:, cols], ALU.add).then_inc(added, 1)


def build(nc, io):
    with ExitStack() as ctx:
        sb = lambda name, shape: ctx.enter_context(nc.sbuf_tensor(name, shape, F32))
        keep = {"ident": sb("ident", [P, P])}
        modulation_stage(nc, io, keep)
        projection_stage(nc, io, keep, 0)
        projection_stage(nc, io, keep, 1)
        attention_scan_stage(nc, io, keep)
        fourier_stage(nc, io, keep)
        output_stage(nc, io, keep)


def dft_tables():
    wave = lambda a, b, n: 2 * np.pi * ((np.outer(a, b) % n) / n)
    r = np.arange(64)
    s64, sg = 64 ** -0.5, 8.0
    eye2 = np.eye(2)
    dft64 = np.concatenate([np.kron(eye2, np.cos(wave(r, r, 64)) / sg), np.kron(eye2, -np.sin(wave(r, r, 64)) / sg)], 1)
    c, s = np.cos(wave(r, r, 64)) * s64, np.sin(wave(r, r, 64)) * s64
    first = np.block([[c, -s], [s, c]])
    second = np.zeros((128, 64, 64))
    for k1 in range(64):
        ph = wave(r, k1 + 64 * r, N_GRID)
        second[:64, k1], second[64:, k1] = np.cos(ph) * s64, np.sin(ph) * s64
    n = np.arange(N_PROMPT)
    ph = wave(n, n, N_PROMPT)
    whole = np.stack([np.cos(ph), np.sin(ph)]) * N_PROMPT ** -0.5
    return {"dft64": dft64, "dft_first": first, "dft_second": second, "dft_whole": whole}


NAMES = ["x_prompt", "x_sample", "cache_k", "cache_v", "state_gla", "c", "c_ctx", "norm_g", "w_mod", "b_mod",
         "w_in", "q_norm_g", "k_norm_g", "rpb", "conv_w", "gla_up_f", "gla_bias_f", "gla_up_b", "gla_bias_b",
         "gla_norm_g", "w_out"]
OUTPUTS = [("y_prompt", (1, N_PROMPT, DM)), ("y_sample", (1, N_GRID, DM)), ("new_cache_k", (1, 1, NH, N_PROMPT, HD)),
           ("new_cache_v", (1, 1, NH, N_PROMPT, HD)), ("new_state_gla", (1, 1, 2, NH, HD, HD))]
SCRATCH = [("mod", (2, 3 * DM)), ("p1", (N_TOK, P1_W)), ("qkt", (4, P, N_TOK)), ("conv_u", (N_TOK + 3, W_GRP)),
           ("gates_bc", (N_TOK, 2 * W_GRP)), ("g", (2, N_TOK, W_GRP)), ("ya", (N_TOK // GRID_W, P, 2, HD)), ("toep", (NH * (2 * WIN_H - 1), GRID_W, P)),
           ("y1", (P, 64, W_GRP)), ("yc", (N_TOK, W_GRP)), ("od", (2, N_TOK, W_GRP))]


def kernel(**inputs):
    import concourse.bacc as bacc
    from concourse.bass_utils import run_bass_kernel_spmd

    nc = bacc.Bacc("TRN2", target_bir_lowering=False, num_devices=1)
    arrays, io = {}, {}
    for name in NAMES:
        arrays["in_" + name] = np.ascontiguousarray(inputs[name])
    for name, table in dft_tables().items():
        arrays["in_" + name] = np.ascontiguousarray(table.astype(np.float32))
    for name, a in arrays.items():
        io[name[3:]] = nc.dram_tensor(name, a.shape, F32, kind="ExternalInput").ap()
    for name, shape in OUTPUTS:
        io[name] = nc.dram_tensor("out_" + name, shape, F32, kind="ExternalOutput").ap()
    for name, shape in SCRATCH:
        io[name] = nc.dram_tensor("s_" + name, shape, F32, kind="Internal").ap()
    build(nc, io)
    got = run_bass_kernel_spmd(nc, [arrays], core_ids=[0]).results[0]
    return tuple(got["out_" + name] for name, _ in OUTPUTS)
```

```python
from contextlib import ExitStack, contextmanager

import numpy as np

import concourse.bass as bass
from concourse import mybir

F32 = mybir.dt.float32
F32R = mybir.dt.float32r
ACT = mybir.ActivationFunctionType
ALU = mybir.AluOpType
AX = mybir.AxisListType

P = 128
DM = 1024
K8 = DM // P
N_PROMPT = 256
N_GRID = 4096
N_TOK = N_GRID + N_PROMPT
GRID_W = 64
ROWS = N_GRID // GRID_W
PAST = 512
W_GRP = 256
HD = 64
NH = 4
WIN_H = 8
WIN_W = 16
RANK = 16
TAU = 16.0
EPS = 1e-6
LAST = N_TOK // P - 1
NEG = -1e30

QA, KA, VA, GA, BB, CB, HB, GB, UC, GC, QD, KD, VD, GD, AF = (W_GRP * n for n in range(15))
P1_V, P1_G, P1_QKD, P1_VD, P1_GD, P1_W = 512, 768, 1024, 1536, 1792, 2048
SKIP = (1, 2)


@contextmanager
def stage(nc):
    with ExitStack() as ctx:
        sems = []

        def sem(name):
            sems.append(nc.alloc_semaphore(name=name))
            return sems[-1]

        yield ctx, sem
        ctx.close()
        nc.clear_and_free_semaphores(sems)
        nc.all_engine_barrier()


def ahead(eng, *values):
    for v in values:
        if not isinstance(v, int):
            eng.compute_val(v)


def kind(t):
    return int(isinstance(t, int) and t >= N_GRID // P)


def tile_pairs(eng, apart=2):
    grid = N_GRID // P
    with eng.Fori(1, (grid - apart) // 2 + 1) as n:
        for s in range(2):
            yield n * 2 - 2 + s, s, 0
    for t in range(grid - apart, LAST + 1):
        yield t, t % 2, kind(t)


def token_rows(io, sample, prompt, t, j):
    return io[prompt][0, bass.ds((t - N_GRID // P) * P, P), :] if j else io[sample][0, bass.ds(t * P, P), :]


def prepare_next(prepare, t, s):
    if not (isinstance(t, int) and t == LAST):
        prepare(t + 1, 1 - s, kind(t + 1))


def prepare_second(prepare, t, s):
    if not (isinstance(t, int) and t + 2 > LAST):
        prepare(t + 2, s, kind(t + 2))


def modulation_stage(nc, io, keep):
    with stage(nc) as (ctx, new_sem):
        sb = lambda name, shape, dt=F32: ctx.enter_context(nc.sbuf_tensor("m_" + name, shape, dt))
        sem = lambda name: new_sem("m_" + name)
        SLOTS = 4
        BLOCKS = 3 * DM // 512
        SCALE = (2, 3)
        tile_rows = lambda n: slice(32 * (n % 4), 32 * (n % 4) + 2)
        craw = sb("craw", [2, DM])
        cact = sb("cact", [2, DM])
        c_t = sb("c_t", [P, K8, 2])
        wm = [sb(f"wm{s}", [P, 3 * DM]) for s in range(SLOTS)]
        bm = sb("bm", [P, BLOCKS, 512])
        ng = sb("ng", [P, BLOCKS, 512])
        m = sb("m", [P, BLOCKS, 512])
        pad = sb("pad", [GRID_W, NH * (2 * WIN_H - 1), P])
        ps_c = ctx.enter_context(nc.psum_tensor("m_psc", [P, K8, 2], F32))
        ps_m = [ctx.enter_context(nc.psum_tensor(f"m_ps{n}", [P, 512], F32)) for n in range(BLOCKS)]
        small_in, idn, silu_c, c_mm, c_sb, rows_mm, rows_sb, scaled, out_done = (
            sem(n) for n in ("small_in", "idn", "silu_c", "c_mm", "c_sb", "rows_mm", "rows_sb", "scaled", "out_done"))
        w_in = [sem(f"w_in{n}") for n in range(SLOTS)]
        rows_in = sem("rows_in")
        chunk_mm, pad_zero, pad_in, toep_out = (sem(n) for n in ("chunk_mm", "pad_zero", "pad_in", "toep_out"))
        block = ctx.enter_context(nc.Block())

        @block.sync
        def _(sp):
            for n, name in enumerate(("c", "c_ctx")):
                src = io[name] if n == 0 else io[name].rearrange("(a n) -> a n", a=1)
                sp.dma_start(craw[n:n + 1, :], src).then_inc(small_in, 16)
            for k in range(K8):
                if k >= SLOTS:
                    sp.wait_ge(chunk_mm, k - SLOTS + 1)
                sp.dma_start(wm[k % SLOTS][:, :], io["w_mod"][0, k * P:(k + 1) * P, :]).then_inc(w_in[k % SLOTS], 16)
            sp.wait_ge(rows_sb, BLOCKS)
            sp.wait_ge(scaled, 4)
            for n in range(BLOCKS):
                sp.dma_start(io["mod"][:, n * 512:(n + 1) * 512], m[tile_rows(n), n, :]).then_inc(out_done, 16)
            sp.wait_ge(out_done, 16 * BLOCKS)

        @block.gpsimd
        def _(pool):
            pool.memset(keep["ident"][:, :], 0.0).then_inc(idn, 1)
            pool.wait_ge(idn, 1)
            pool.affine_select(out=keep["ident"][:, :], in_=keep["ident"][:, :], compare_op=ALU.not_equal,
                               fill=1.0, base=0, pattern=[[-1, P]], channel_multiplier=1).then_inc(idn, 1)
            pool.wait_ge(idn, 2)
            pool.memset(pad[:, :, :], 0.0).then_inc(pad_zero, 1)
            pool.wait_ge(pad_zero, 1)
            pool.dma_start(pad[:, :, 48:48 + 2 * WIN_W - 1],
                           io["rpb"].rearrange("a h r x -> a (h r) x").broadcast_to([GRID_W, NH * (2 * WIN_H - 1), 2 * WIN_W - 1])).then_inc(pad_in, 16)
            pool.wait_ge(pad_in, 16)
            pool.dma_start(io["toep"].rearrange("n q x -> q n x"), pad[:, :, :]).then_inc(toep_out, 16)
            pool.wait_ge(toep_out, 16)

        @block.scalar
        def _(act):
            act.wait_ge(small_in, 2 * 16)
            act.activation(cact[:, :], craw[:, :], ACT.Silu).then_inc(silu_c, 1)
            for n in range(BLOCKS):
                act.dma_start(bm[tile_rows(n), n, :], io["b_mod"][:, n * 512:(n + 1) * 512].broadcast_to([2, 512])).then_inc(rows_in, 16)
            for i, n in enumerate(SCALE):
                act.dma_start(ng[tile_rows(n), n, :], io["norm_g"][:, i * 512:(i + 1) * 512].broadcast_to([2, 512])).then_inc(rows_in, 16)

        @block.tensor
        def _(pe):
            pe.wait_ge(idn, 2)
            pe.wait_ge(silu_c, 1)
            for k in range(K8):
                last = pe.transpose(ps_c[:, k, :], cact[:, k * P:(k + 1) * P], keep["ident"][0:2, 0:2])
            last.then_inc(c_mm, 1)
            pe.wait_ge(c_sb, 1)
            for k in range(K8):
                pe.wait_ge(w_in[k % SLOTS], 16 * (k // SLOTS + 1))
                for n in range(BLOCKS):
                    last = pe.matmul(ps_m[n][tile_rows(n), :], c_t[:, k, :], wm[k % SLOTS][:, n * 512:(n + 1) * 512],
                                     start=(k == 0), stop=(k == K8 - 1))
                last.then_inc(chunk_mm, 1)

        @block.vector
        def _(dve):
            dve.wait_ge(c_mm, 1)
            dve.tensor_copy(c_t[:, :, :], ps_c[:, :, :]).then_inc(c_sb, 1)
            dve.wait_ge(rows_in, 16 * (BLOCKS + 2))
            dve.wait_ge(chunk_mm, K8)
            for n in (*SCALE, 0, 1, 4, 5):
                a = tile_rows(n)
                dve.tensor_tensor(m[a, n, :], ps_m[n][a, :], bm[a, n, :], ALU.add).then_inc(rows_sb, 1)
            for i, n in enumerate(SCALE):
                a = tile_rows(n)
                dve.wait_ge(rows_sb, i + 1)
                dve.tensor_scalar(m[a, n, :], m[a, n, :], 1.0, DM ** 0.5, ALU.add, ALU.mult).then_inc(scaled, 1)
            for i, n in enumerate(SCALE):
                a = tile_rows(n)
                dve.wait_ge(scaled, i + 1)
                dve.tensor_tensor(m[a, n, :], m[a, n, :], ng[a, n, :], ALU.mult).then_inc(scaled, 1)


def product(pe, out, left_hi, left_lo, right_hi, right_lo):
    for k in range(K8):
        pe.matmul(out, left_hi(k), right_hi(k), start=(k == 0), stop=False)
        pe.matmul(out, left_hi(k), right_lo(k), start=False, stop=False)
        last = pe.matmul(out, left_lo(k), right_hi(k), start=False, stop=(k == K8 - 1))
    return last


def weight_pieces(blocks):
    out, at, group = [], 0, 0
    for c0, n in blocks:
        for c in range(0, n, 512):
            wd = min(512, n - c)
            nk = min(K8, 2 * 512 // wd)
            out += [(k, nk, c0 + c, wd, at + c, group) for k in range(0, K8, nk)]
            group += 1
        at += n
    return out


def projection_stage(nc, io, keep, which):
    blocks = [(QA, 1024), (QD, 1024), (AF, 2 * RANK)] if which == 0 else [(UC, 512), (BB, 1024)]
    pieces = weight_pieces(blocks)
    width = sum(n for _, n in blocks)
    G = pieces[-1][5] + 1
    with stage(nc) as (ctx, new_sem):
        pre = f"p{which}_"
        sb = lambda name, shape, dt=F32: ctx.enter_context(nc.sbuf_tensor(pre + name, shape, dt))
        ps = lambda name, shape: ctx.enter_context(nc.psum_tensor(pre + name, shape, F32))
        sem = lambda name: new_sem(pre + name)
        w_hi = sb("w_hi", [P, K8, width], F32R)
        w_lo = sb("w_lo", [P, K8, width], F32R)
        w_raw = [sb(f"w_raw{s}", [P, 1024]) for s in range(2 + 2 * which)]
        shift = sb("shift", [P, 2, DM])
        scale = sb("scale", [P, 2, DM])
        xb = [sb(f"xb{s}", [P, DM]) for s in range(2)]
        squares = sb("squares", [P, DM])
        h_hi = [sb(f"h_hi{s}", [P, K8, P], F32R) for s in range(2)]
        h_lo = [sb(f"h_lo{s}", [P, K8, P], F32R) for s in range(2)]
        ss, ve, rstd = ([sb(f"{n}{s}", [P, 1]) for s in range(2)] for n in ("ss", "ve", "rstd"))
        half_pow = sb("half_pow", [P, 8])
        eps = sb("eps", [P, 9])
        ps_t = [ps(f"ps_t{b}", [P, 4, P]) for b in range(2)]
        ps_m = [ps(f"ps_m{g}", [P, 512]) for g in range(G)]
        (w_hi_done, w_lo_done, small_in, consts, sq_done, ve_done, rstd_done, normed, shifted, turned, hi_done,
         lo_done, mm) = (sem(n) for n in (
             "w_hi_done", "w_lo_done", "small_in", "consts", "sq_done", "ve_done", "rstd_done", "normed", "shifted",
             "turned", "hi_done", "lo_done", "mm"))
        w_in = [sem(f"w_in{s}") for s in range(4)]
        mod_in = [sem(f"mod_in{j}") for j in range(2)]
        x_in = [sem(f"x_in{s}") for s in range(2)]
        bank_free = [sem(f"bank_free{g}") for g in range(G)]
        rows_sent = [sem(f"rows_sent{s}") for s in range(2)]
        t_sent = [sem(f"t_sent{s}") for s in range(2)]
        if which == 0:
            rows = [sb(f"rows{s}", [P, P1_W]) for s in range(2)]
            w_raw += [rows[s][:, 0:1024] for s in range(2)]
            a_t = [sb(f"a_t{s}", [2 * RANK, P]) for s in range(2)]
            qss, qve, qr = (sb(n, [P, 8]) for n in ("qss", "qve", "qr"))
            gqk = sb("gqk", [P, 2 * NH * HD])
            qkt = [sb(f"qkt{s}", [P, 4, P]) for s in range(2)]
            ps_q = ps("ps_q", [P, 4, P])
            qk_sq, qk_ss, qk_ve, qk_r, qk_ready, qkt_mm, qkt_sb, gqk_set = (
                sem(n) for n in ("qk_sq", "qk_ss", "qk_ve", "qk_r", "qk_ready", "qkt_mm", "qkt_sb", "gqk_set"))
        else:
            rows = [sb(f"rows{s}", [P, 3, W_GRP]) for s in range(2)]
            zero = sb("zero", [1, W_GRP])
            silu_g = sb("silu_g", [P, W_GRP])
            h_b = sb("h_b", [P, W_GRP])
            u_tok = sb("u_tok", [P, W_GRP])
            u_t = sb("u_t", [P, 2, P])
            dft = sb("dft", [P, 2 * P])
            g_sb = [sb(f"g_sb{s}", [P, 2, W_GRP]) for s in range(2)]
            ps_u = ps("ps_u", [P, 2, P])
            ps_g = ps("ps_g", [P, 2, 2, P])
            u_done, u_mm, u_sb, dft_mm, dft_sb, hg_done, rows_done, zero_out = (
                sem(n) for n in ("u_done", "u_mm", "u_sb", "dft_mm", "dft_sb", "hg_done", "rows_done", "zero_out"))
        block = ctx.enter_context(nc.Block())

        def mm_at(t, n):
            return t * G + n + 1 + 2 * G

        @block.sync
        def _(sp):
            def load_x(t, s, j):
                sp.dma_start(xb[s][:, :], token_rows(io, "x_sample", "x_prompt", t, j)).then_inc(x_in[s], 16)

            for t in range(2):
                load_x(t, t, 0)
            for n, (k, nk, c0, wd, a0, _) in enumerate(pieces):
                if n >= 4:
                    sp.wait_ge(w_lo_done, n - 3)
                sp.dma_start(w_raw[n % 4][:, 0:nk * wd].rearrange("p (k n) -> p k n", k=nk),
                             io["w_in"][0, k * P:(k + nk) * P, c0:c0 + wd].rearrange("(k p) n -> p k n", p=P)).then_inc(w_in[n % 4], 16)
            for t, s, j in tile_pairs(sp):
                tok = t * P
                ahead(sp, t * 2 + 6, t + 1, t + 2, tok * 4, tok * (P1_W * 4), tok * (4 * W_GRP), (t + 2) * (P * DM * 4))
                if not (isinstance(t, int) and t + 2 > LAST):
                    sp.wait_ge(turned, t * 2 + 6)
                    load_x(t + 2, s, kind(t + 2))
                if which == 0:
                    sp.wait_ge(qkt_sb, t + 2)
                    sp.dma_start(io["qkt"][:, :, bass.ds(tok, P)].rearrange("b p t -> p b t"), qkt[s][:, :, :]).then_inc(t_sent[s], 16)
                    sp.wait_ge(qk_ready, t + 1)
                    for g in range(1, G):
                        sp.wait_ge(bank_free[g], t + 2)
                    sp.dma_start(io["p1"][bass.ds(tok, P), :], rows[s][:, :]).then_inc(rows_sent[s], 16)
                    sp.dma_start(io["a_t"][:, bass.ds(tok, P)], a_t[s][:, :]).then_inc(rows_sent[s], 16)
                else:
                    sp.wait_ge(dft_sb, t + 2)
                    sp.dma_start(io["g"][:, bass.ds(tok, P), :].rearrange("r t c -> t r c"), g_sb[s][:, :, :]).then_inc(t_sent[s], 16)
                    sp.wait_ge(bank_free[0], t + 2)
                    sp.wait_ge(bank_free[1], t + 2)
                    sp.dma_start(io["conv_u"][bass.ds(tok + SKIP[j], P), :], rows[s][:, 0, :]).then_inc(rows_sent[s], 16)
                    sp.dma_start(io["gates_bc"][bass.ds(tok, P), :], rows[s][:, 1:3, :].rearrange("t a c -> t (a c)")).then_inc(rows_sent[s], 16)
            for s in range(2):
                sp.wait_ge(t_sent[s], 16 * (LAST // 2 + 2))
                sp.wait_ge(rows_sent[s], 16 + 32 * (LAST // 2 + 1))
            if which == 1:
                sp.wait_ge(zero_out, 48)

        @block.gpsimd
        def _(pool):
            pool.memset(half_pow[:, :], -0.5).then_inc(consts, 1)
            pool.memset(eps[:, 0:1], DM * EPS).then_inc(consts, 1)
            pool.memset(eps[:, 1:9], HD * EPS).then_inc(consts, 1)
            pool.wait_ge(consts, 3)
            if which == 1:
                pool.memset(zero[:, :], 0.0).then_inc(consts, 1)
                pool.wait_ge(consts, 4)
                for row in (0, N_GRID + 1, N_TOK + 2):
                    pool.dma_start(io["conv_u"][row:row + 1, :], zero[:, :]).then_inc(zero_out, 16)

            def prepare(t, s, j):
                pool.wait_ge(sq_done, t + 1)
                pool.tensor_tensor(ve[s][:, :], ss[s][:, :], eps[:, 0:1], ALU.add).then_inc(ve_done, 1)
                pool.wait_ge(ve_done, t + 1)
                pool.tensor_tensor(rstd[s][:, :], ve[s][:, :], half_pow[:, 0:1], ALU.pow).then_inc(rstd_done, 1)
                if j:
                    pool.wait_ge(mod_in[1], 32)
                pool.wait_ge(normed, t + 1)
                pool.tensor_tensor(xb[s][:, :], xb[s][:, :], shift[:, j, :], ALU.add).then_inc(shifted, 1)

            pool.wait_ge(mod_in[0], 32)
            prepare(0, 0, 0)
            prepare(1, 1, 0)
            for t, s, j in tile_pairs(pool):
                prepare_second(prepare, t, s)
                if which == 0:
                    pool.wait_ge(qk_ss, t + 2)
                    pool.tensor_tensor(qve[:, :], qss[:, :], eps[:, 1:9], ALU.add).then_inc(qk_ve, 1)
                    pool.wait_ge(qk_ve, t + 1)
                    pool.tensor_tensor(qr[:, :], qve[:, :], half_pow[:, :], ALU.pow).then_inc(qk_r, 1)

        @block.scalar
        def _(act):
            def load_mod(j):
                for row, dst in ((1, scale), (0, shift)):
                    act.dma_start(dst[:, j, :], io["mod"][j:j + 1, row * DM:(row + 1) * DM].broadcast_to([P, DM])).then_inc(mod_in[j], 16)

            load_mod(0)
            if which == 0:
                act.dma_start(gqk[:, 0:HD], io["q_norm_g"].broadcast_to([P, HD])).then_inc(small_in, 16)
                act.dma_start(gqk[:, 4 * HD:5 * HD], io["k_norm_g"].broadcast_to([P, HD])).then_inc(small_in, 16)
            else:
                act.dma_start(dft[:, :], io["dft64"]).then_inc(small_in, 16)
            for g in range(G):
                act.sem_inc(bank_free[g], 1)
            if which == 0:
                act.sem_inc(qkt_sb, 1)
            else:
                act.sem_inc(dft_sb, 1)

            def square(t, s, j):
                act.wait_ge(x_in[s], (t - s) * 8 + 16)
                if not isinstance(t, int) or t:
                    act.wait_ge(sq_done, t)
                if which == 0 and (not isinstance(t, int) or t > 1):
                    act.wait_ge(qk_ss, t - 1)
                act.activation(squares[:, :], xb[s][:, :], ACT.Square, accum_out=ss[s][:, :]).then_inc(sq_done, 1)

            def high(t, s, j):
                act.wait_ge(mm, t * G + G)
                for b in range(2):
                    act.wait_ge(turned, t * 2 + b + 5)
                    act.activation(h_hi[s][:, 4 * b:4 * b + 4, :], ps_t[b][:, :, :], ACT.Copy).then_inc(hi_done, 1)

            square(0, 0, 0)
            square(1, 1, 0)
            load_mod(1)
            for n, (k, nk, c0, wd, a0, _) in enumerate(pieces):
                if n == 4:
                    high(0, 0, 0)
                act.wait_ge(w_in[n % 4], 16 * (n // 4 + 1))
                act.activation(w_hi[:, k:k + nk, a0:a0 + wd], w_raw[n % 4][:, 0:nk * wd].rearrange("p (k n) -> p k n", k=nk),
                               ACT.Copy).then_inc(w_hi_done, 1)
            act.wait_ge(w_lo_done, len(pieces))
            for t, s, j in tile_pairs(act):
                prepare_second(square, t, s)
                done, stored = (t - s) * 8 + 16, (t - s) * 16 + 16
                if which == 0:
                    act.wait_ge(mm, mm_at(t, 0))
                    act.wait_ge(sq_done, min(t + 3, LAST + 1) if isinstance(t, int) else t + 3)
                    act.activation(squares[:, 0:512], ps_m[0][:, :], ACT.Square).then_inc(qk_sq, 1)
                    act.wait_ge(rows_sent[s], stored)
                    act.wait_ge(mm, mm_at(t, 1))
                    act.activation(rows[s][:, P1_V:P1_G], ps_m[1][:, 0:W_GRP], ACT.Copy)
                    act.activation(rows[s][:, P1_G:P1_QKD], ps_m[1][:, W_GRP:512], ACT.Silu).then_inc(bank_free[1], 1)
                    prepare_next(high, t, s)
                    act.wait_ge(mm, mm_at(t, 3))
                    act.activation(rows[s][:, P1_VD:P1_GD], ps_m[3][:, 0:W_GRP], ACT.Copy)
                    act.activation(rows[s][:, P1_GD:P1_W], ps_m[3][:, W_GRP:512], ACT.Silu).then_inc(bank_free[3], 1)
                    act.wait_ge(qkt_mm, t + 1)
                    act.wait_ge(t_sent[s], done)
                    act.activation(qkt[s][:, :, :], ps_q[:, :, :], ACT.Copy).then_inc(qkt_sb, 1)
                else:
                    act.wait_ge(mm, mm_at(t, 0))
                    act.activation(u_tok[:, :], ps_m[0][:, 0:W_GRP], ACT.Copy).then_inc(u_done, 1)
                    act.wait_ge(rows_sent[s], stored)
                    act.activation(rows[s][:, 2, :], ps_m[0][:, W_GRP:512], ACT.Silu).then_inc(bank_free[0], 1)
                    prepare_next(high, t, s)
                    act.wait_ge(mm, mm_at(t, 2))
                    act.activation(h_b[:, :], ps_m[2][:, 0:W_GRP], ACT.Copy)
                    act.activation(silu_g[:, :], ps_m[2][:, W_GRP:512], ACT.Silu).then_inc(bank_free[2], 1)
                    act.wait_ge(dft_mm, t + 1)
                    act.wait_ge(t_sent[s], done)
                    act.activation(g_sb[s][:, :, :].rearrange("t r (f c) -> t f r c", f=2), ps_g[:, :, :, :], ACT.Copy).then_inc(dft_sb, 1)

        @block.tensor
        def _(pe):
            pe.sem_inc(mm, 2 * G)
            pe.sem_inc(turned, 4)

            def turn(t, s, j):
                pe.wait_ge(shifted, t + 1)
                pe.wait_ge(lo_done, t * 2 + 2)
                for b in range(2):
                    for n in range(4):
                        last = pe.transpose(ps_t[b][:, n, :], xb[s][:, (4 * b + n) * P:(4 * b + n + 1) * P], keep["ident"][:, :])
                    last.then_inc(turned, 1)

            turn(0, 0, 0)
            pe.wait_ge(small_in, 32 if which == 0 else 16)
            for t, s, j in tile_pairs(pe):
                pe.wait_ge(lo_done, t * 2 + 4)

                def group(g):
                    a, b = 512 * g, min(512 * g + 512, width)
                    pe.wait_ge(w_lo_done, sum(1 for p in pieces if p[5] <= g))
                    pe.wait_ge(bank_free[g], t + 1)
                    if b - a < P:
                        product(pe, ps_m[g][0:b - a, 0:P], lambda k: w_hi[:, k, a:b], lambda k: w_lo[:, k, a:b],
                                lambda k: h_hi[s][:, k, :], lambda k: h_lo[s][:, k, :]).then_inc(mm, 1)
                        return
                    product(pe, ps_m[g][:, 0:b - a], lambda k: h_hi[s][:, k, :], lambda k: h_lo[s][:, k, :],
                            lambda k: w_hi[:, k, a:b], lambda k: w_lo[:, k, a:b]).then_inc(mm, 1)

                group(0)
                group(1)
                prepare_next(turn, t, s)
                if which == 0:
                    for g in range(2, G):
                        group(g)
                    pe.wait_ge(qk_ready, t + 1)
                    pe.wait_ge(qkt_sb, t + 1)
                    for b in range(4):
                        last = pe.transpose(ps_q[:, b, :], rows[s][:, b * P:(b + 1) * P], keep["ident"][:, :])
                    last.then_inc(qkt_mm, 1)
                else:
                    pe.wait_ge(u_done, t + 1)
                    for f in range(2):
                        last = pe.transpose(ps_u[:, f, :], u_tok[:, f * P:(f + 1) * P], keep["ident"][:, :])
                    last.then_inc(u_mm, 1)
                    group(2)
                    pe.wait_ge(u_sb, t + 1)
                    pe.wait_ge(dft_sb, t + 1)
                    for f in range(2):
                        last = pe.matmul(ps_g[:, f], u_t[:, f, :], dft[:, :].rearrange("p (r c) -> p r c", r=2), start=True, stop=True)
                    last.then_inc(dft_mm, 1)

        @block.vector
        def _(dve):
            dve.sem_inc(lo_done, 2)
            for s in range(2):
                dve.sem_inc(rows_sent[s], 16)
                dve.sem_inc(t_sent[s], 16)
            if which == 0:
                dve.sem_inc(qk_ss, 1)

            def norm(t, s, j):
                if j:
                    dve.wait_ge(mod_in[1], 32)
                dve.wait_ge(rstd_done, t + 1)
                dve.scalar_tensor_tensor(xb[s][:, :], xb[s][:, :], rstd[s][:, :], scale[:, j, :], ALU.mult, ALU.mult).then_inc(normed, 1)

            def low(t, s, j):
                for b in range(2):
                    dve.wait_ge(hi_done, t * 2 + b + 1)
                    dve.tensor_tensor(h_lo[s][:, 4 * b:4 * b + 4, :], ps_t[b][:, :, :], h_hi[s][:, 4 * b:4 * b + 4, :],
                                      ALU.subtract).then_inc(lo_done, 1)

            dve.wait_ge(mod_in[0], 32)
            norm(0, 0, 0)
            for n, (k, nk, c0, wd, a0, _) in enumerate(pieces):
                if n == 4:
                    norm(1, 1, 0)
                    low(0, 0, 0)
                dve.wait_ge(w_hi_done, n + 1)
                dve.tensor_tensor(w_lo[:, k:k + nk, a0:a0 + wd], w_raw[n % 4][:, 0:nk * wd].rearrange("p (k n) -> p k n", k=nk),
                                  w_hi[:, k:k + nk, a0:a0 + wd], ALU.subtract).then_inc(w_lo_done, 1)
            if which == 0:
                dve.wait_ge(small_in, 32)
                dve.tensor_scalar(gqk[:, NH * HD:(NH + 1) * HD], gqk[:, NH * HD:(NH + 1) * HD], HD ** 0.5, None,
                                  ALU.mult).then_inc(gqk_set, 1)
                dve.wait_ge(gqk_set, 1)
                for h in range(1, NH):
                    dve.tensor_copy(gqk[:, (NH + h) * HD:(NH + h + 1) * HD], gqk[:, NH * HD:(NH + 1) * HD]).then_inc(gqk_set, 1)
                    dve.tensor_copy(gqk[:, h * HD:(h + 1) * HD], gqk[:, 0:HD]).then_inc(gqk_set, 1)
                dve.wait_ge(gqk_set, 2 * NH - 1)
            for t, s, j in tile_pairs(dve):
                prepare_second(norm, t, s)
                if which == 0:
                    heads = lambda a: a.rearrange("t (h d) -> t h d", h=8)
                    dve.wait_ge(qk_sq, t + 1)
                    dve.tensor_reduce(qss[:, :], heads(squares[:, 0:512]), AX.X, ALU.add).then_inc(qk_ss, 1)
                    dve.wait_ge(rows_sent[s], (t - s) * 16 + 16)
                    dve.wait_ge(qk_r, t + 1)
                    qk = rows[s][:, 0:512]
                    dve.tensor_tensor(heads(qk), heads(ps_m[0][:, :]), qr[:, :].unsqueeze(2).broadcast_to([P, 8, HD]),
                                      ALU.mult).then_inc(bank_free[0], 1)
                    dve.wait_ge(bank_free[0], t + 2)
                    dve.tensor_tensor(qk, qk, gqk[:, :], ALU.mult).then_inc(qk_ready, 1)
                    prepare_next(low, t, s)
                    dve.wait_ge(mm, mm_at(t, 2))
                    dve.tensor_copy(rows[s][:, P1_QKD:P1_VD], ps_m[2][:, :]).then_inc(bank_free[2], 1)
                    dve.wait_ge(mm, mm_at(t, 4))
                    dve.tensor_copy(a_t[s][:, :], ps_m[4][0:2 * RANK, 0:P]).then_inc(bank_free[4], 1)
                else:
                    prepare_next(low, t, s)
                    dve.wait_ge(u_mm, t + 1)
                    dve.tensor_copy(u_t[:, :, :], ps_u[:, :, :]).then_inc(u_sb, 1)
                    dve.wait_ge(rows_sent[s], (t - s) * 16 + 16)
                    dve.wait_ge(bank_free[2], t + 2)
                    dve.tensor_tensor(rows[s][:, 1, :], ps_m[1][:, 0:W_GRP], silu_g[:, :], ALU.mult)
                    dve.tensor_tensor(rows[s][:, 0, :], ps_m[1][:, W_GRP:512], h_b[:, :], ALU.mult).then_inc(bank_free[1], 1)


def attention_rows(eng):
    start = lambda r: min(max(r - WIN_H // 2, 0), ROWS - WIN_H) if r < ROWS else None
    last = ROWS + N_PROMPT // GRID_W - 1
    lo, hi = WIN_H // 2, ROWS - WIN_H // 2 - 2
    for r in range(lo):
        yield r, start(r), r + 1, start(r + 1), r % 2, r // 2
    with eng.Fori(lo // 2, hi // 2) as n:
        for d in range(2):
            r = n * 2 + d
            yield r, r - WIN_H // 2, r + 1, r + 1 - WIN_H // 2, d, n
    for r in range(hi, last + 1):
        yield r, start(r), r + 1 if r < last else None, start(r + 1), r % 2, r // 2


def attention_scan_stage(nc, io, keep):
    W = WIN_H * GRID_W
    CH = W // P
    CC = PAST // P
    NDR = 2 * WIN_H - 1
    C = P // 2
    DIRS = range(2)
    STEPS = N_TOK // P
    GRID_T = N_GRID // P
    PIECE = N_GRID // 4
    N_CONST = 32
    with stage(nc) as (ctx, new_sem):
        sb = lambda name, shape, dt=F32: ctx.enter_context(nc.sbuf_tensor("a_" + name, shape, dt))
        sem = lambda name: new_sem("a_" + name)
        k_raw = [sb(f"k_raw{p}", [P, PIECE]) for p in range(2)]
        k_hi, k_lo = (sb(n, [P, 2, N_TOK], F32R) for n in ("k_hi", "k_lo"))
        v_win = [sb(f"v_win{s}", [P, CH, W_GRP]) for s in range(2)]
        vp = sb("vp", [P, N_PROMPT // P, W_GRP])
        ck = sb("ck", [P, CC, NH, HD])
        ck_hi, ck_lo = (sb(n, [P, 2, PAST], F32R) for n in ("ck_hi", "ck_lo"))
        cv = sb("cv", [P, CC, NH, HD])
        bias = sb("bias", [P, 2, NDR, GRID_W])
        q2 = sb("q2", [P, 2, P])
        q_hi, q_lo = (sb(n, [P, 2, P], F32R) for n in ("q_hi", "q_lo"))
        s_sb = [sb(f"s_sb{p}", [P, W + PAST]) for p in range(2)]
        p_t = [sb(f"p_t{p}", [P, W + PAST]) for p in range(2)]
        o_sb = sb("o_sb", [P, 2, HD])
        max_c, max_w, neg_m, total, r_total = (sb(n, [P, 2]) for n in ("max_c", "max_w", "neg_m", "total", "r_total"))
        sums = sb("sums", [P, 2, 2])
        psum = lambda name, cols: ctx.enter_context(nc.psum_tensor("a_" + name, [P, cols], F32))
        ps_w = psum("ps_w", 512)
        ps_c = [psum(f"ps_c{p}", 512) for p in range(2)]
        ps_t = [psum(f"ps_t{h}", 512) for h in range(2)]
        ps_ou = psum("ps_ou", 512)
        ps_o = [ps_ou[:, p * P:(p + 1) * P] for p in range(2)]
        ps_u = ps_ou[:, 2 * P:].rearrange("p (c a v) -> p c a v", c=2, a=2)
        ps_z = psum("ps_z", 512)
        ps_s = psum("ps_s", 512)
        (vp_in, q_hi_done, q_lo_done, k_hi_done, k_lo_done, ckt_hi, ck_in, cv_in, bias_in, bias_set, q_zero, ckt_mm, ckt_sb, s_done, maxc_done, w_done,
         max_done, exp_done, sum_done, rsum_done, t_done, t0_sb, t1_sb, pv_done, o_done, o_sent, cache_out) = (sem(n) for n in (
             "vp_in", "q_hi_done", "q_lo_done", "k_hi_done", "k_lo_done", "ckt_hi", "ck_in", "cv_in", "bias_in", "bias_set", "q_zero", "ckt_mm", "ckt_sb", "s_done",
             "maxc_done", "w_done", "max_done", "exp_done", "sum_done", "rsum_done", "t_done", "t0_sb", "t1_sb", "pv_done",
             "o_done", "o_sent", "cache_out"))
        k_in = [sem(f"k_in{p}") for p in range(2)]
        v_in = [sem(f"v_in{s}") for s in range(2)]
        q_in = [sem(f"q_in{p}") for p in range(2)]
        both = lambda name, shape: [sb(f"{name}{d}", shape) for d in range(2)]
        tri = sb("tri", [P, 2, 2, P])
        mask = sb("mask", [P, 2, P])
        ind = sb("ind", [P, 2])
        up = sb("up", [33, 2, W_GRP])
        aug = both("aug", [33, P])
        qkv = both("qkv", [P, 3 * W_GRP])
        low = both("low", [P, W_GRP])
        nab = both("nab", [P, W_GRP])
        ez = both("ez", [P, W_GRP])
        lz = both("lz", [P, W_GRP])
        la = both("la", [P, W_GRP])
        e_cum, e_neg = (both(n, [P, W_GRP]) for n in ("e_cum", "e_neg"))
        decay = both("decay", [P, 2, 2])
        q_d, k_i = (both(n, [P, W_GRP]) for n in ("q_d", "k_i"))
        e_rest = both("e_rest", [P, 2, W_GRP])
        k_e = both("k_e", [P, 2, W_GRP])
        qd_t = both("qd_t", [P, NH, P])
        kd_t = both("kd_t", [P, 2, P])
        att = both("att", [P, NH, P])
        s_at, s_mid = (both(n, [P, 2, HD]) for n in ("s_at", "s_mid"))
        od_sb = both("od_sb", [P, W_GRP])
        names = ("z_mm", "low_done", "nab_done", "ez_done", "lz_done", "la_done", "c_mm", "exps",
                 "qd_done", "ke_done", "turned", "turned_sb", "u_mm", "att_mm", "att_sb", "mid_done", "new_done", "o_mm", "o_done",
                 "o_sent", "st_out")
        S = [{n: sem(f"{n}{d}") for n in names} for d in DIRS]
        u_sb = sb("u_sb", [P, 2, HD])
        u_kept = sem("u_kept")
        t_in = [sem(f"t_in{d}") for d in DIRS]
        consts, small_in, st_in = sem("consts"), sem("small_in"), sem("st_in")
        block = ctx.enter_context(nc.Block())

        def before(d, i):
            return (0, i) if d else (1, i - 1)

        def piece(c):
            return c * PIECE, PIECE if c < N_GRID // PIECE else N_PROMPT

        def tile_of(d, i):
            if isinstance(i, int) and i >= GRID_T:
                return i if d == 0 else GRID_T + STEPS - 1 - i
            return i if d == 0 else GRID_T - 1 - i

        @block.sync
        def _(sp):
            sp.wait_ge(consts, 1)
            for d, (w, b) in enumerate((("gla_up_f", "gla_bias_f"), ("gla_up_b", "gla_bias_b"))):
                sp.dma_start(up[0:RANK, d, :], io[w].rearrange("a r n -> (a r) n")).then_inc(small_in, 16)
                sp.dma_start(up[32:33, d, :], io[b]).then_inc(small_in, 16)
                sp.dma_start(s_at[d][:, :, :], io["state_gla"][0, 0, d].rearrange("(p h) k v -> (h k) p v", p=2)).then_inc(st_in, 16)

            def load_q(r, p):
                for h in range(2):
                    sp.dma_start(q2[h * HD:(h + 1) * HD, p, h * HD:(h + 1) * HD],
                                 io["qkt"][p, h * HD:(h + 1) * HD, bass.ds(r * GRID_W, GRID_W)]).then_inc(q_in[p], 16)

            def load_tile(d, i):
                tok = tile_of(d, i) * P
                sp.dma_start(aug[d][0:RANK, :], io["a_t"][RANK * d:RANK * (d + 1), bass.ds(tok, P)]).then_inc(t_in[d], 16)
                sp.dma_start(qkv[d][:, :], io["p1"][bass.ds(tok, P), P1_QKD:P1_GD]).then_inc(t_in[d], 16)

            def load_keys(c):
                a, n = piece(c)
                for p in range(2):
                    if c:
                        sp.wait_ge(k_lo_done, 2 * c + p - 1)
                    sp.dma_start(k_raw[p][:, 0:n], io["qkt"][2 + p, :, a:a + n]).then_inc(k_in[p], 16)

            def load_values(rs, s):
                sp.dma_start(v_win[s][:, :, :], io["p1"][bass.ds(rs * GRID_W, W), P1_V:P1_G].rearrange("(m p) c -> p m c", p=P)).then_inc(v_in[s], 16)

            sp.wait_ge(q_zero, 1)
            for p in range(2):
                load_q(0, p)
            load_keys(0)
            flat = io["toep"].rearrange("n q x -> n (q x)")[:, GRID_W - 1:GRID_W - 1 + GRID_W * (P - 1)]
            skew = flat.rearrange("n (q x) -> q n x", x=P - 1)[:, :, 0:GRID_W]
            for h in range(NH):
                sp.dma_start(bias[(h % 2) * 64:(h % 2) * 64 + 64, h // 2], skew[:, h * NDR:(h + 1) * NDR, :]).then_inc(bias_in, 16)
            for s in range(2):
                load_values(0, s)
            sp.wait_ge(consts, 7)
            for d in DIRS:
                load_tile(d, 0)

            for p in range(2):
                sp.wait_ge(q_lo_done, p + 1)
                load_q(1, p)
            sp.sem_inc(o_sent, 16)
            for r, rs, nxt, _, d, i in attention_rows(sp):
                pd, pi = before(d, i)
                ahead(sp, 2 * r + 3, 2 * r + 4, (r + 2) * GRID_W * 4, r * GRID_W * 4, (r - 2) * (GRID_W * P1_W * 4), pi + 1, tile_of(pd, pi + 1) * (P * P1_W * 4), tile_of(pd, pi + 1) * (P * 4))
                more = not isinstance(r, int) or r + 2 < N_TOK // GRID_W
                if more:
                    sp.wait_ge(q_lo_done, 2 * r + 3)
                    load_q(r + 2, 0)
                if isinstance(r, int) and r < 4:
                    load_keys(r + 1)
                if not isinstance(r, int) or 1 <= r <= 2 * STEPS - 2:
                    sp.wait_ge(S[pd]["o_mm"], pi + 1)
                    load_tile(pd, pi + 1)
                if more:
                    sp.wait_ge(q_lo_done, 2 * r + 4)
                    load_q(r + 2, 1)
                sp.wait_ge(o_done, 4 * r + 8)
                if not isinstance(r, int):
                    load_values(r + 2 - WIN_H // 2, d)
                elif r + 2 < ROWS:
                    load_values(min(max(r + 2 - WIN_H // 2, 0), ROWS - WIN_H), d)
                if isinstance(r, int) and r == 3:
                    sp.dma_start(vp[:, :, :], io["p1"][N_GRID:N_TOK, P1_V:P1_G].rearrange("(m p) c -> p m c", p=P)).then_inc(vp_in, 16)
                sp.dma_start(io["ya"][bass.ds(r, 1)].rearrange("a t p d -> (a t) p d"), o_sb[:, :, :]).then_inc(o_sent, 16)
            for name, c0 in (("new_cache_k", W_GRP), ("new_cache_v", P1_V)):
                sp.dma_start(io[name].rearrange("a l h s d -> (a l h) s d"),
                             io["p1"][N_GRID:N_TOK, c0:c0 + W_GRP].rearrange("s (h d) -> h s d", h=NH)).then_inc(cache_out, 16)

            sp.wait_ge(o_sent, 16 * (N_TOK // GRID_W + 1))
            sp.wait_ge(cache_out, 32)

        @block.gpsimd
        def _(pool):
            n = 0

            def step(ins):
                nonlocal n
                ins.then_inc(consts, 1)
                n += 1

            pool.memset(q2[:, :, :], 0.0).then_inc(q_zero, 1)
            step(pool.memset(up[:, :, :], 0.0))
            for d in DIRS:
                step(pool.memset(aug[d][:, :], 0.0))
                step(pool.memset(e_rest[d][:, :, :], 0.0))
                step(pool.memset(qd_t[d][:, :, :], 0.0))
            step(pool.memset(tri[:, :, :, :], 1.0 / TAU))
            step(pool.memset(mask[:, :, :], 1.0))
            step(pool.memset(ind[:, :], 1.0 / TAU))
            pool.wait_ge(consts, n)
            for d in DIRS:
                step(pool.memset(aug[d][32:33, :], 1.0))
            cuts = []
            for d in DIRS:
                sign = 1 if d == 0 else -1
                cuts += [(tri[:, d, 0, :], 0, sign), (tri[:, d, 1, :], -1, -sign), (mask[:, d, :], 0, sign)]
            for view, base, sign in cuts:
                pool.wait_ge(consts, n)
                step(pool.affine_select(out=view, in_=view, compare_op=ALU.is_ge, fill=0.0, base=base,
                                        pattern=[[sign, P]], channel_multiplier=-sign))
                pool.wait_ge(consts, n)
                step(pool.memset(view[0:C, C:P], 0.0))
                step(pool.memset(view[C:P, 0:C], 0.0))
            pool.wait_ge(consts, n)
            step(pool.memset(ind[0:C, 1:2], 0.0))
            step(pool.memset(ind[C:P, 0:1], 0.0))
            assert n == N_CONST
            pool.wait_ge(bias_in, 64)
            n = 0
            for h in range(2):
                for c0, c1, base, step, chan in ((0, GRID_W - WIN_W, WIN_W // 2, 1, -1), (WIN_W, GRID_W, WIN_W // 2 - 1 - WIN_W, -1, 1)):
                    part = bias[h * 64:(h + 1) * 64, :, :, c0:c1].rearrange("q p r x -> q (p r) x")
                    if n:
                        pool.wait_ge(bias_set, n)
                    pool.affine_select(out=part, in_=part, compare_op=ALU.is_ge, fill=NEG, base=base,
                                       pattern=[[0, 2 * NDR], [step, c1 - c0]], channel_multiplier=chan).then_inc(bias_set, 1)
                    n += 1
            for r, _, _, _, d, i in attention_rows(pool):
                k = qkv[d][:, W_GRP:2 * W_GRP]
                pool.wait_ge(S[d]["exps"], i + 1)
                pool.tensor_tensor(k_e[d][:, :, :], k.unsqueeze(1).broadcast_to([P, 2, W_GRP]), e_rest[d][:, :, :], ALU.mult).then_inc(S[d]["ke_done"], 1)

        @block.scalar
        def _(act):
            act.sem_inc(t1_sb, 1)
            for buf, name, landed in ((ck, "cache_k", ck_in), (cv, "cache_v", cv_in)):
                for m in range(CC):
                    act.dma_start(buf[:, m, :, :], io[name][0, 0, :, m * P:(m + 1) * P, :].rearrange("h p d -> p h d")).then_inc(landed, 16)
                for p in range(2):
                    act.wait_ge(k_in[p], 16)
            for d in DIRS:
                act.sem_inc(S[d]["o_sent"], 16)

            def exps(r, rs, p):
                act.wait_ge(max_done, 2 * r + p + 1)
                if rs is None:
                    act.activation(s_sb[p][:, 0:N_PROMPT], ps_c[p][:, 0:N_PROMPT], ACT.Exp, bias=neg_m[:, p:p + 1],
                                   accum_out=total[:, p:p + 1]).then_inc(exp_done, 1)
                else:
                    act.activation(s_sb[p][:, 0:W], s_sb[p][:, 0:W], ACT.Exp, bias=neg_m[:, p:p + 1], accum_out=sums[:, p, 0:1])
                    act.activation(s_sb[p][:, W:], ps_c[p][:, :], ACT.Exp, bias=neg_m[:, p:p + 1],
                                   accum_out=sums[:, p, 1:2]).then_inc(exp_done, 1)

            def high_keys(c):
                a, n = piece(c)
                for p in range(2):
                    act.wait_ge(k_in[p], 16 * c + 16)
                    act.activation(k_hi[:, p, a:a + n], k_raw[p][:, 0:n], ACT.Copy).then_inc(k_hi_done, 1)

            def high_q(r, p):
                act.wait_ge(q_in[p], 32 * r + 32)
                if not isinstance(r, int) or r:
                    act.wait_ge(s_done, 2 * r + p - 1)
                act.activation(q_hi[:, p, :], q2[:, p, :], ACT.Copy).then_inc(q_hi_done, 1)

            act.wait_ge(ckt_mm, 1)
            for p in range(2):
                act.activation(ck_hi[:, p, :], ps_t[p][:, :], ACT.Copy).then_inc(ckt_hi, 1)
            for p in range(2):
                high_q(0, p)
            high_keys(0)
            for p in range(2):
                exps(0, 0, p)
            for p in range(2):
                high_q(1, p)

            def log_decays(d, i):
                act.wait_ge(S[d]["nab_done"], i + 1)
                act.activation(ez[d][:, :], nab[d][:, :], ACT.Exp).then_inc(S[d]["ez_done"], 1)
                act.wait_ge(S[d]["ez_done"], i + 1)
                act.activation(lz[d][:, :], ez[d][:, :], ACT.Ln, bias=1.0).then_inc(S[d]["lz_done"], 1)

            def decays(d, i):
                act.wait_ge(S[d]["c_mm"], i + 1)
                act.activation(e_cum[d][:, :], ps_s[:, 0:W_GRP], ACT.Exp)
                act.activation(e_neg[d][:, :], ps_s[:, 0:W_GRP], ACT.Exp, scale=-1.0)
                for c in range(2):
                    rows = slice(c * C, (c + 1) * C)
                    act.activation(e_rest[d][rows, c, :], ps_s[rows, W_GRP:], ACT.Exp)
                act.activation(decay[d][:, :, :], ps_z[:, W_GRP:W_GRP + 4].rearrange("p (a b) -> p a b", a=2), ACT.Exp).then_inc(S[d]["exps"], 1)

            def keep_turned(d, i):
                act.wait_ge(S[d]["turned"], i + 1)
                turned = ps_s[:, :].rearrange("p (a b) -> p a b", a=4)
                act.activation(kd_t[d][:, :, :], turned[:, 2:4, :], ACT.Copy)
                for odd in range(2):
                    rows = slice(64 * odd, 64 * odd + 64)
                    last = act.activation(qd_t[d][rows, odd::2, :], turned[rows, 0:2, :], ACT.Copy)
                last.then_inc(S[d]["turned_sb"], 1)

            def store_out(d, i):
                act.wait_ge(S[d]["o_done"], i + 1)
                act.dma_start(io["od"][d, bass.ds(tile_of(d, i) * P, P), :], od_sb[d][:, :]).then_inc(S[d]["o_sent"], 16)

            for r, rs, nxt, nrs, d, i in attention_rows(act):
                prev = None if isinstance(r, int) and r == 0 else before(d, i)
                for p in range(2):
                    if rs is not None:
                        act.wait_ge(t_done, 4 * r + 2 * p + 2)
                        act.activation(p_t[p][:, W:], ps_t[1][:, :], ACT.Copy).then_inc(t1_sb, 1)
                    if p == 0 and prev:
                        keep_turned(*prev)
                    if p == 1:
                        decays(d, i)
                    if nxt is not None:
                        exps(r + 1, nrs, p)
                    if p == 0:
                        log_decays(d, i)
                if not isinstance(r, int) or r + 2 < N_TOK // GRID_W:
                    for p in range(2):
                        high_q(r + 2, p)
                if isinstance(r, int) and r < 4:
                    high_keys(r + 1)
                if prev:
                    store_out(*prev)
            keep_turned(1, STEPS - 1)
            store_out(1, STEPS - 1)
            for d in DIRS:
                act.wait_ge(S[d]["o_sent"], 16 * (STEPS + 1))
                act.wait_ge(S[d]["new_done"], 2 * STEPS + 2)
                act.dma_start(io["new_state_gla"][0, 0, d].rearrange("(p h) k v -> (h k) p v", p=2),
                              s_at[d][:, :, :]).then_inc(S[d]["st_out"], 16)
            for d in DIRS:
                act.wait_ge(S[d]["st_out"], 16)

        @block.tensor
        def _(pe):
            pe.wait_ge(ck_in, CC * 16)
            for p in range(2):
                for m in range(CC):
                    last = pe.transpose(ps_t[p][:, m * P:(m + 1) * P], ck[:, m, 2 * p:2 * p + 2, :].rearrange("k h d -> k (h d)"),
                                        keep["ident"][:, :])
            last.then_inc(ckt_mm, 1)
            pe.wait_ge(k_lo_done, 2)

            def scores(r, rs, p):
                pe.wait_ge(q_lo_done, 2 * r + p + 1)
                if not isinstance(r, int) or r or p:
                    pe.wait_ge(max_done, 2 * r + p)
                def three(out, hi, lo):
                    pe.matmul(out, q_hi[:, p, :], hi, start=True, stop=False)
                    pe.matmul(out, q_hi[:, p, :], lo, start=False, stop=False)
                    return pe.matmul(out, q_lo[:, p, :], hi, start=False, stop=True)

                if rs is None:
                    three(ps_c[p][:, 0:N_PROMPT], k_hi[:, p, N_GRID:], k_lo[:, p, N_GRID:]).then_inc(s_done, 1)
                else:
                    window = bass.ds(rs * GRID_W, W)
                    three(ps_w[:, :], k_hi[:, p, window], k_lo[:, p, window])
                    three(ps_c[p][:, :], ck_hi[:, p, :], ck_lo[:, p, :]).then_inc(s_done, 1)

            pe.wait_ge(ckt_sb, 2)
            for p in range(2):
                scores(0, 0, p)

            def turn(r, rs, p):
                pe.wait_ge(exp_done, 2 * r + p + 1)
                pe.wait_ge(t0_sb, 2 * r + p + 1)
                for m in range(N_PROMPT // P if rs is None else CH):
                    last = pe.transpose(ps_t[0][:, m * P:(m + 1) * P], s_sb[p][:, m * P:(m + 1) * P], keep["ident"][:, :])
                last.then_inc(t_done, 2 if rs is None else 1)
                if rs is not None:
                    pe.wait_ge(t1_sb, 2 * r + p + 1)
                    for m in range(CC):
                        last = pe.transpose(ps_t[1][:, m * P:(m + 1) * P], s_sb[p][:, W + m * P:W + (m + 1) * P], keep["ident"][:, :])
                    last.then_inc(t_done, 1)

            def values(r, rs, s, p, prev=None):
                pe.wait_ge(t0_sb, 2 * r + p + 2)
                pe.wait_ge(o_done, 4 * r + 2 * p + 4)
                if prev:
                    pe.wait_ge(S[prev[0]]["mid_done"], 2 * prev[1] + 2)
                if rs is None:
                    todo = [(m, vp[:, m, :]) for m in range(N_PROMPT // P)]
                else:
                    pe.wait_ge(t1_sb, 2 * r + p + 2)
                    todo = [(CH + m, cv[:, m, :, :].rearrange("k h d -> k (h d)")) for m in range(CC)]
                    todo += [(m, v_win[s][:, m, :]) for m in range(CH)]
                for n, (m, v) in enumerate(todo):
                    for h in range(2):
                        rows = slice(h * GRID_W, (h + 1) * GRID_W)
                        last = pe.matmul(ps_o[p][rows, h * HD:(h + 1) * HD], p_t[p][:, m * P + h * GRID_W:m * P + (h + 1) * GRID_W],
                                         v[:, (2 * p + h) * HD:(2 * p + h + 1) * HD], start=(n == 0), stop=(n == len(todo) - 1))
                last.then_inc(pv_done, 1)

            def d_z(d, i):
                pe.wait_ge(t_in[d], 32 * i + 32)
                pe.matmul(ps_z[:, W_GRP:], aug[d][:, :], up[:, d, :], start=True, stop=True).then_inc(S[d]["z_mm"], 1)

            def d_sums(d, i, prev):
                if prev:
                    pe.wait_ge(S[prev[0]]["o_done"], prev[1] + 1)
                pe.wait_ge(S[d]["la_done"], i + 1)
                pe.matmul(ps_s[:, 0:W_GRP], tri[:, d, 0, :], la[d][:, :], start=True, stop=True)
                pe.matmul(ps_s[:, W_GRP:], tri[:, d, 1, :], la[d][:, :], start=True, stop=True)
                for p in range(2):
                    last = pe.matmul(ps_z[:, W_GRP + 2 * p:W_GRP + 2 * p + 2], la[d][:, p * P:(p + 1) * P], ind[:, :], start=True, stop=True)
                last.then_inc(S[d]["c_mm"], 1)

            def d_turn(d, i, row):
                pe.wait_ge(S[d]["qd_done"], i + 1)
                for n, src in enumerate((q_d[d], q_d[d], k_i[d], k_i[d])):
                    last = pe.transpose(ps_s[:, n * P:(n + 1) * P], src[:, (n % 2) * P:(n % 2) * P + P], keep["ident"][:, :])
                last.then_inc(S[d]["turned"], 1)
                pe.wait_ge(S[d]["ke_done"], i + 1)
                pe.wait_ge(o_done, 4 * row + 4)
                for c in range(2):
                    for h in range(NH):
                        last = pe.matmul(ps_u[64 * (h % 2):64 * (h % 2) + 64, c, h // 2, :],
                                         k_e[d][:, c, h * HD:(h + 1) * HD],
                                         qkv[d][:, 2 * W_GRP + h * HD:2 * W_GRP + (h + 1) * HD], start=True, stop=True)
                last.then_inc(S[d]["u_mm"], 1)

            def d_scores(d, i):
                pe.wait_ge(S[d]["turned_sb"], i + 1)
                for h in range(NH):
                    last = pe.matmul(ps_s[:, h * P:(h + 1) * P], kd_t[d][:, h // 2, :], qd_t[d][:, h, :], start=True, stop=True)
                last.then_inc(S[d]["att_mm"], 1)

            def d_out(d, i):
                pe.wait_ge(S[d]["mid_done"], 2 * i + 2)
                pe.wait_ge(S[d]["att_sb"], i + 1)
                for h in range(NH):
                    for n in range(2):
                        c = n if d == 0 else 1 - n
                        pe.matmul(ps_z[c * C:(c + 1) * C, h * HD:(h + 1) * HD], qd_t[d][:, h, c * C:(c + 1) * C],
                                  (s_mid if n else s_at)[d][:, h // 2, :], start=True, stop=False, skip_group_check=True)
                    last = pe.matmul(ps_z[:, h * HD:(h + 1) * HD], att[d][:, h, :],
                                     qkv[d][:, 2 * W_GRP + h * HD:2 * W_GRP + (h + 1) * HD],
                                     start=False, stop=True, skip_group_check=True)
                last.then_inc(S[d]["o_mm"], 1)

            pe.wait_ge(consts, N_CONST)
            pe.wait_ge(small_in, 64)
            pe.wait_ge(st_in, 32)
            pe.wait_ge(cv_in, CC * 16)
            for r, rs, nxt, nrs, d, i in attention_rows(pe):
                if not isinstance(r, int):
                    pe.wait_ge(k_lo_done, 10)
                if rs is None:
                    pe.wait_ge(vp_in, 16)
                else:
                    pe.wait_ge(v_in[d], 16 * i + 16)
                prev = None if isinstance(r, int) and r == 0 else before(d, i)
                turn(r, rs, 0)
                if prev:
                    d_turn(*prev, r)
                if nxt is not None:
                    scores(r + 1, nrs, 0)
                if prev:
                    d_scores(*prev)
                d_z(d, i)
                values(r, rs, d, 0, prev)
                turn(r, rs, 1)
                if prev:
                    pe.wait_ge(S[d]["nab_done"], i + 1)
                    d_out(*prev)
                if nxt is not None:
                    scores(r + 1, nrs, 1)
                d_sums(d, i, prev)
                values(r, rs, d, 1)
            d_turn(1, STEPS - 1, 2 * STEPS)
            d_scores(1, STEPS - 1)
            d_out(1, STEPS - 1)

        @block.vector
        def _(dve):
            dve.wait_ge(ckt_mm, 1)
            for p in range(2):
                dve.wait_ge(ckt_hi, p + 1)
                dve.tensor_tensor(ck_lo[:, p, :], ps_t[p][:, :], ck_hi[:, p, :], ALU.subtract).then_inc(ckt_sb, 1)

            def low_q(r, p):
                dve.wait_ge(q_hi_done, 2 * r + p + 1)
                dve.tensor_tensor(q_lo[:, p, :], q2[:, p, :], q_hi[:, p, :], ALU.subtract).then_inc(q_lo_done, 1)

            def low_keys(c):
                a, n = piece(c)
                for p in range(2):
                    dve.wait_ge(k_hi_done, 2 * c + p + 1)
                    dve.tensor_tensor(k_lo[:, p, a:a + n], k_raw[p][:, 0:n], k_hi[:, p, a:a + n], ALU.subtract).then_inc(k_lo_done, 1)

            for p in range(2):
                low_q(0, p)
            low_keys(0)
            dve.sem_inc(t0_sb, 1)
            dve.sem_inc(o_done, 4)
            dve.wait_ge(bias_set, 4)
            dve.wait_ge(consts, N_CONST)
            dve.wait_ge(st_in, 32)
            for d in DIRS:
                dve.sem_inc(S[d]["new_done"], 2)

            def maxima(r, rs, p):
                dve.wait_ge(s_done, 2 * r + p + 1)
                if rs is None:
                    dve.tensor_reduce(neg_m[:, p:p + 1], ps_c[p][:, 0:N_PROMPT], AX.X, ALU.max, negate=True).then_inc(max_done, 1)
                    return
                dve.tensor_reduce(max_c[:, p:p + 1], ps_c[p][:, :], AX.X, ALU.max).then_inc(maxc_done, 1)
                at = WIN_H // 2 - 1 if not isinstance(rs, int) else rs - r + WIN_H - 1
                dve.tensor_tensor_reduce(out=s_sb[p][:, 0:W].rearrange("k (r x) -> k r x", r=WIN_H), in0=ps_w[:, :].rearrange("k (r x) -> k r x", r=WIN_H), in1=bias[:, p, at:at + WIN_H, :],
                                         scale=1.0, scalar=NEG, op0=ALU.add, op1=ALU.max,
                                         accum_out=max_w[:, p:p + 1]).then_inc(w_done, 1)
                dve.wait_ge(maxc_done, 2 * r + p + 1)
                dve.wait_ge(w_done, 2 * r + p + 1)
                dve.tensor_scalar(neg_m[:, p:p + 1], max_w[:, p:p + 1], max_c[:, p:p + 1], -1.0, ALU.max, ALU.mult).then_inc(max_done, 1)

            for p in range(2):
                maxima(0, 0, p)
            for p in range(2):
                low_q(1, p)

            def state(d, i, n):
                c = n if d == 0 else 1 - n
                if n:
                    dve.wait_ge(S[d]["o_mm"], i + 1)
                    if isinstance(i, int) and i == GRID_T - 1:
                        for p in range(2):
                            dve.memset(s_at[d][:, p, :], 0.0).then_inc(S[d]["new_done"], 1)
                        return
                else:
                    dve.wait_ge(S[d]["u_mm"], i + 1)
                dve.wait_ge(S[d]["mid_done" if n else "new_done"], 2 * i + 2)
                dst, src = (s_at[d], s_mid[d]) if n else (s_mid[d], s_at[d])
                if n == 0:
                    dve.tensor_copy(u_sb[:, :, :], ps_u[:, 1 - c, :, :]).then_inc(u_kept, 1)
                else:
                    dve.wait_ge(u_kept, 2 * i + d + 1)
                for p in range(2):
                    dve.scalar_tensor_tensor(dst[:, p, :], src[:, p, :], decay[d][:, p, c:c + 1], u_sb[:, p, :] if n else ps_u[:, c, p, :],
                                             ALU.mult, ALU.add).then_inc(S[d]["new_done" if n else "mid_done"], 1)

            def mask_scores(d, i):
                dve.wait_ge(S[d]["att_mm"], i + 1)
                dve.tensor_tensor(att[d][:, :, :], ps_s[:, :].rearrange("p (h t) -> p h t", h=NH),
                                  mask[:, d, :].unsqueeze(1).broadcast_to([P, NH, P]), ALU.mult).then_inc(S[d]["att_sb"], 1)

            def copy_out(d, i):
                dve.wait_ge(S[d]["o_mm"], i + 1)
                dve.wait_ge(S[d]["o_sent"], i * 16 + 16)
                dve.tensor_copy(od_sb[d][:, :], ps_z[:, 0:W_GRP]).then_inc(S[d]["o_done"], 1)

            for r, rs, nxt, nrs, d, i in attention_rows(dve):
                prev = None if isinstance(r, int) and r == 0 else before(d, i)
                for p in range(2):
                    u = 2 * r + p
                    dve.wait_ge(exp_done, u + 1)
                    if rs is not None:
                        dve.tensor_tensor(total[:, p:p + 1], sums[:, p, 0:1], sums[:, p, 1:2], ALU.add).then_inc(sum_done, 1)
                        dve.wait_ge(sum_done, u + 1)
                    dve.reciprocal(r_total[:, p:p + 1], total[:, p:p + 1]).then_inc(rsum_done, 1)
                    if p and prev:
                        copy_out(*prev)
                        state(*prev, 1)
                    if p:
                        dve.wait_ge(S[d]["lz_done"], i + 1)
                        dve.tensor_tensor(la[d][:, :], low[d][:, :], lz[d][:, :], ALU.subtract).then_inc(S[d]["la_done"], 1)
                    dve.wait_ge(t_done, 2 * u + 1)
                    cols = N_PROMPT if rs is None else W
                    dve.tensor_copy(p_t[p][:, 0:cols], ps_t[0][:, 0:cols]).then_inc(t0_sb, 1)
                    if prev and p == 0:
                        state(*prev, 0)
                    if nxt is not None:
                        maxima(r + 1, nrs, p)
                    if p == 0:
                        if prev:
                            mask_scores(*prev)
                        dve.wait_ge(S[d]["z_mm"], i + 1)
                        dve.tensor_scalar(low[d][:, :], ps_z[:, W_GRP:], 0.0, None, ALU.min).then_inc(S[d]["low_done"], 1)
                        dve.wait_ge(S[d]["low_done"], i + 1)
                        dve.scalar_tensor_tensor(nab[d][:, :], low[d][:, :], 2.0, ps_z[:, W_GRP:], ALU.mult, ALU.subtract).then_inc(S[d]["nab_done"], 1)
                    else:
                        dve.wait_ge(S[d]["exps"], i + 1)
                        dve.wait_ge(t_in[d], 32 * i + 32)
                        dve.tensor_tensor(k_i[d][:, :], qkv[d][:, W_GRP:2 * W_GRP], e_neg[d][:, :], ALU.mult)
                        dve.scalar_tensor_tensor(q_d[d][:, :], qkv[d][:, 0:W_GRP], HD ** -0.5, e_cum[d][:, :], ALU.mult, ALU.mult).then_inc(S[d]["qd_done"], 1)
                    dve.wait_ge(pv_done, u + 1)
                    dve.wait_ge(rsum_done, u + 1)
                    dve.wait_ge(o_sent, 16 * r + 16)
                    for h in range(2):
                        dve.tensor_scalar(o_sb[h * 64:h * 64 + 64, p, :], ps_o[p][h * 64:h * 64 + 64, h * HD:(h + 1) * HD],
                                          r_total[h * 64:h * 64 + 64, p:p + 1], None, ALU.mult).then_inc(o_done, 1)
                if not isinstance(r, int) or r + 2 < N_TOK // GRID_W:
                    for p in range(2):
                        low_q(r + 2, p)
                if isinstance(r, int) and r < 4:
                    low_keys(r + 1)
            last = (1, STEPS - 1)
            state(*last, 0)
            mask_scores(*last)
            copy_out(*last)
            state(*last, 1)


def fourier_groups(eng):
    with eng.Fori(1, 3) as n:
        for s in range(4):
            yield n * 4 - 4 + s, s


def fourier_stage(nc, io, keep):
    GW = 8
    BANKS = GW // 2
    SLOTS = 4
    with stage(nc) as (ctx, new_sem):
        sb = lambda name, shape, dt=F32: ctx.enter_context(nc.sbuf_tensor("f_" + name, shape, dt))
        sem = lambda name: new_sem("f_" + name)
        first = sb("first", [P, P])
        second = [sb(f"second{s}", [P, GW, 64]) for s in range(SLOTS)]
        gx = [sb(f"gx{s}", [P, GW, W_GRP]) for s in range(SLOTS)]
        yx = [sb(f"yx{s}", [P, GW, W_GRP]) for s in range(SLOTS)]
        whole = sb("whole", [P, 2, 2, N_PROMPT])
        gp = sb("gp", [P, 2, 2, W_GRP])
        yp = sb("yp", [P, 2, W_GRP])
        ps = [ctx.enter_context(nc.psum_tensor(f"f_ps{b}", [P, 2, W_GRP], F32)) for b in range(BANKS)]
        ps_p = ctx.enter_context(nc.psum_tensor("f_psp", [P, 2, W_GRP], F32))
        consts, gp_in = sem("consts"), sem("gp_in")
        slot_in = [[sem(f"in{q}{s}") for s in range(SLOTS)] for q in range(2)]
        mm = [sem(f"mm{q}") for q in range(2)]
        by_act = [sem(f"by_act{q}") for q in range(2)]
        by_dve = [sem(f"by_dve{q}") for q in range(2)]
        sent = [[sem(f"sent{q}{s}") for s in range(SLOTS)] for q in range(2)]
        yp_mm, yp_sb, yp_sent = sem("yp_mm"), sem("yp_sb"), sem("yp_sent")
        block = ctx.enter_context(nc.Block())

        @block.sync
        def _(sp):
            sp.dma_start(first[:, :], io["dft_first"]).then_inc(consts, 16)
            gv = io["g"][:, 0:N_GRID, :].rearrange("r (a b) c -> r a b c", b=64)
            for i, s in fourier_groups(sp):
                ahead(sp, i * BANKS + BANKS, i * (GW * W_GRP * 4))
                sp.wait_ge(mm[0], i * BANKS + BANKS)
                for r in range(2):
                    sp.dma_start(gx[s][64 * r:64 * r + 64, :, :], gv[r, :, bass.ds(i * GW, GW), :]).then_inc(slot_in[0][s], 16)
            for s in range(SLOTS):
                sp.wait_ge(sent[0][s], 48)
            yv = io["y1"].rearrange("(r k) b c -> r b k c", r=2)
            for i, s in fourier_groups(sp):
                ahead(sp, i * BANKS + BANKS, i * (GW * W_GRP * 4 * 64), i * (GW * 64 * 4))
                sp.wait_ge(mm[1], i * BANKS + BANKS)
                for r in range(2):
                    sp.dma_start(gx[s][64 * r:64 * r + 64, :, :], yv[r, :, bass.ds(i * GW, GW), :]).then_inc(slot_in[1][s], 16)
                sp.dma_start(second[s][:, :, :], io["dft_second"][:, bass.ds(i * GW, GW), :]).then_inc(slot_in[1][s], 16)

        @block.gpsimd
        def _(pool):
            for r in range(2):
                pool.dma_start(gp[:, r, :, :], io["g"][r, N_GRID:N_TOK, :].rearrange("(j p) c -> p j c", p=P)).then_inc(gp_in, 16)
                pool.dma_start(whole[:, r, :, :], io["dft_whole"][r].rearrange("(j p) k -> p j k", p=P)).then_inc(gp_in, 16)

        @block.tensor
        def _(pe):
            for q in range(2):
                pe.sem_inc(mm[q], SLOTS * BANKS)
            pe.wait_ge(consts, 16)
            for q in range(2):
                for i, s in fourier_groups(pe):
                    pe.wait_ge(slot_in[q][s], (i - s) * (4 * (2 + q)) + 16 * (2 + q))
                    for n in range(BANKS):
                        pe.wait_ge((by_act, by_dve)[n % 2][q], i * (BANKS // 2) + n // 2 + 1)
                        if q == 0:
                            last = pe.matmul(ps[n][:, :, :], first[:, :], gx[s][:, 2 * n:2 * n + 2, :], start=True, stop=True)
                        else:
                            for k in range(2):
                                last = pe.matmul(ps[n][0:64, k, :], second[s][:, 2 * n + k, :], gx[s][:, 2 * n + k, :], start=True, stop=True)
                        last.then_inc(mm[q], 1)
            pe.wait_ge(gp_in, 64)
            for kc in range(2):
                for r in range(2):
                    for j in range(2):
                        last = pe.matmul(ps_p[:, kc, :], whole[:, r, j, kc * P:(kc + 1) * P], gp[:, r, j, :],
                                         start=(r == 0 and j == 0), stop=(r == 1 and j == 1))
            last.then_inc(yp_mm, 1)

        @block.scalar
        def _(act):
            for q in range(2):
                act.sem_inc(by_act[q], BANKS // 2)
                for s in range(SLOTS):
                    act.sem_inc(sent[q][s], 16)
            for q in range(2):
                rows = slice(0, P if q == 0 else 64)
                for i, s in fourier_groups(act):
                    act.wait_ge(sent[q][s], (i - s) * 4 + 16)
                    for n in range(0, BANKS, 2):
                        act.wait_ge(mm[q], i * BANKS + n + SLOTS * BANKS + 1)
                        act.activation(yx[s][rows, 2 * n:2 * n + 2, :], ps[n][rows, :, :], ACT.Copy).then_inc(by_act[q], 1)
                    act.wait_ge(by_act[q], i * (BANKS // 2) + BANKS)
                    act.wait_ge(by_dve[q], i * (BANKS // 2) + BANKS)
                    if q == 0:
                        act.dma_start(io["y1"][:, bass.ds(i * GW, GW), :], yx[s][:, :, :]).then_inc(sent[q][s], 16)
                    else:
                        act.dma_start(io["yc"][0:N_GRID, :].rearrange("(k2 k1) c -> k2 k1 c", k1=64)[:, bass.ds(i * GW, GW), :],
                                      yx[s][rows, :, :]).then_inc(sent[q][s], 16)
            act.wait_ge(yp_mm, 1)
            act.activation(yp[:, :, :], ps_p[:, :, :], ACT.Copy).then_inc(yp_sb, 1)
            act.wait_ge(yp_sb, 1)
            act.dma_start(io["yc"][N_GRID:N_TOK, :].rearrange("(j p) c -> p j c", p=P), yp[:, :, :]).then_inc(yp_sent, 16)
            act.wait_ge(yp_sent, 16)
            for s in range(SLOTS):
                act.wait_ge(sent[1][s], 48)

        @block.vector
        def _(dve):
            for q in range(2):
                dve.sem_inc(by_dve[q], BANKS // 2)
            for q in range(2):
                rows = slice(0, P if q == 0 else 64)
                for i, s in fourier_groups(dve):
                    dve.wait_ge(sent[q][s], (i - s) * 4 + 16)
                    for n in range(1, BANKS, 2):
                        dve.wait_ge(mm[q], i * BANKS + n + SLOTS * BANKS + 1)
                        dve.tensor_copy(yx[s][rows, 2 * n:2 * n + 2, :], ps[n][rows, :, :]).then_inc(by_dve[q], 1)


def output_stage(nc, io, keep):
    CH = [(0, 128), (64, 192)] + [(n * P, n * P + 64) for n in range(2, K8)]
    PIECES = [(h, m) for h in range(2) for m in range(K8 // 2)]
    LOADS = 11
    with stage(nc) as (ctx, new_sem):
        sb = lambda name, shape, dt=F32: ctx.enter_context(nc.sbuf_tensor("o_" + name, shape, dt))
        sem = lambda name: new_sem("o_" + name)
        two = lambda name, shape, dt=F32: [sb(f"{name}{s}", shape, dt) for s in range(2)]
        w_hi = sb("w_hi", [P, K8, DM], F32R)
        w_lo = sb("w_lo", [P, K8, DM], F32R)
        stage_w = [sb(f"stage_w{s}", [P, 2, 512]) for s in range(4)]
        gate = sb("gate", [P, 2, DM])
        gn = sb("gn", [P, HD])
        gn8 = sb("gn8", [P, HD])
        taps = sb("taps", [P, 3, W_GRP])
        half_pow = sb("half_pow", [P, NH])
        eps = sb("eps", [P, NH])
        x = two("x", [P, DM])
        ya = two("ya", [P, 2, 2, HD])
        g_ad = two("g_ad", [P, 2, W_GRP])
        gbc = two("gbc", [P, 2, W_GRP])
        yc = two("yc", [P, W_GRP])
        od = two("od", [P, 2, W_GRP])
        u = two("u", [P, 3, W_GRP])
        u_w = sb("u_w", [P, 3, W_GRP])
        conv = sb("conv", [P, W_GRP])
        o = sb("o", [P, W_GRP])
        o_sq = sb("o_sq", [P, W_GRP])
        ss = sb("ss", [P, NH])
        ve = sb("ve", [P, NH])
        r = sb("r", [P, NH])
        o_n = sb("o_n", [P, W_GRP])
        gg = sb("gg", [P, W_GRP])
        mix = two("mix", [P, 4, W_GRP])
        y_hi = two("y_hi", [P, K8, P], F32R)
        y_lo = two("y_lo", [P, K8, P], F32R)
        gx = two("gx", [P, DM])
        y = two("y", [P, DM])
        ps_t = [ctx.enter_context(nc.psum_tensor(f"o_ps_t{b}", [P, 4, P], F32)) for b in range(2)]
        ps_y = [[ctx.enter_context(nc.psum_tensor(f"o_ps_y{s}{h}", [P, 512], F32)) for h in range(2)] for s in range(2)]
        w_in = [sem(f"w_in{s}") for s in range(4)]
        w_hi_done, w_lo_done, small_in, taps_in, gn_in, gn_done, pow_set = (
            sem(n) for n in ("w_hi_done", "w_lo_done", "small_in", "taps_in", "gn_in", "gn_done", "pow_set"))
        mix_in = [sem(f"mix_in{s}") for s in range(2)]
        x_in = [sem(f"x_in{s}") for s in range(2)]
        o_sum, sq_done, ss_done, ve_done, r_done, on_done, gg_done, mixed, turned, hi_done, lo_done = (
            sem(n) for n in ("o_sum", "sq_done", "ss_done", "ve_done", "r_done", "on_done", "gg_done", "mixed", "turned", "hi_done", "lo_done"))
        uw_done, conv_done = sem("uw_done"), sem("conv_done")
        mm, gated, added = sem("mm"), sem("gated"), sem("added")
        sent = [sem(f"sent{s}") for s in range(2)]
        block = ctx.enter_context(nc.Block())

        @block.sync
        def _(sp):
            def load_mix(t, s):
                j = kind(t)
                tok = t * P
                for a in range(2):
                    sp.dma_start(ya[s][64 * a:64 * a + 64, :, :, :].rearrange("q h p d -> q h (p d)"),
                                 io["ya"][bass.ds(t * 2 + a, 1)].rearrange("a (h q) p d -> (a q) h (p d)", h=2)).then_inc(mix_in[s], 16)
                sp.dma_start(g_ad[s][:, 0, :], io["p1"][bass.ds(tok, P), P1_G:P1_G + W_GRP]).then_inc(mix_in[s], 16)
                sp.dma_start(g_ad[s][:, 1, :], io["p1"][bass.ds(tok, P), P1_GD:P1_GD + W_GRP]).then_inc(mix_in[s], 16)
                sp.dma_start(gbc[s][:, :, :], io["gates_bc"][bass.ds(tok, P), :].rearrange("t (a c) -> t a c", a=2)).then_inc(mix_in[s], 16)
                sp.dma_start(yc[s][:, :], io["yc"][bass.ds(tok, P), :]).then_inc(mix_in[s], 16)
                for d in range(2):
                    sp.dma_start(od[s][:, d, :], io["od"][d, bass.ds(tok, P), :]).then_inc(mix_in[s], 16)
                for a in range(3):
                    sp.dma_start(u[s][:, a, :], io["conv_u"][bass.ds(tok + (SKIP[j] - 1 + a), P), :]).then_inc(mix_in[s], 16)

            sp.dma_start(gn[:, :], io["gla_norm_g"].broadcast_to([P, HD])).then_inc(gn_in, 16)
            load_mix(0, 0)
            load_mix(1, 1)
            sp.dma_start(taps[:, :, :].rearrange("p a c -> p (a c)"),
                         io["conv_w"].rearrange("a t c -> a (t c)").broadcast_to([P, 3 * W_GRP])).then_inc(taps_in, 16)
            for n, (h, m) in enumerate(PIECES):
                if n >= 4:
                    sp.wait_ge(w_lo_done, n - 3)
                for b in range(2):
                    for a, row in enumerate(CH[2 * m + b]):
                        sp.dma_start(stage_w[n % 4][64 * a:64 * a + 64, b, :],
                                     io["w_out"][0, row:row + 64, 512 * h:512 * h + 512]).then_inc(w_in[n % 4], 16)
            for j in range(2):
                sp.dma_start(gate[:, j, :], io["mod"][j:j + 1, 2 * DM:3 * DM].broadcast_to([P, DM])).then_inc(small_in, 16)
            sp.wait_ge(mixed, 2)
            load_mix(2, 0)
            for t, s, j in tile_pairs(sp, 4):
                ahead(sp, t * 2 + 2, t + 3, t * (P * DM * 4), *((t + 3) * (P * n) for n in (4, 4 * W_GRP, 8 * W_GRP, 4 * P1_W)),
                      (t + 3) * (2 * GRID_W * W_GRP * 4))
                sp.wait_ge(added, t * 2 + 2)
                sp.dma_start(x[s][:, :], token_rows(io, "x_sample", "x_prompt", t, j)).then_inc(x_in[s], 16)
                if not (isinstance(t, int) and t + 3 > LAST):
                    sp.wait_ge(mixed, t + 3)
                    load_mix(t + 3, 1 - s)

        @block.gpsimd
        def _(pool):
            pool.memset(half_pow[:, :], -0.5).then_inc(pow_set, 1)
            pool.memset(eps[:, :], HD * EPS).then_inc(pow_set, 1)
            pool.wait_ge(pow_set, 2)
            pool.sem_inc(mixed, 1)
            pool.wait_ge(gn_done, 1)
            heads = lambda a: a.rearrange("t (h d) -> t h d", d=HD)

            def join(t, s):
                pool.wait_ge(mix_in[s], (t - s) * (LOADS * 8) + LOADS * 16)
                pool.wait_ge(turned, t * 2 + 2)
                pool.tensor_tensor(mix[s][:, 0, :].rearrange("t (h p d) -> t h p d", p=2, h=2), ya[s][:, :, :, :],
                                   g_ad[s][:, 0, :].rearrange("t (p h d) -> t h p d", p=2, h=2), ALU.mult)
                pool.tensor_tensor(mix[s][:, 2, :], gbc[s][:, 1, :], yc[s][:, :], ALU.mult)
                pool.wait_ge(mixed, t + 1)
                pool.tensor_tensor(heads(gg[:, :]), heads(g_ad[s][:, 1, :]), gn8[:, :].unsqueeze(1).broadcast_to([P, NH, HD]),
                                   ALU.mult).then_inc(gg_done, 1)
                pool.wait_ge(ss_done, t + 2)
                pool.tensor_tensor(ve[:, :], ss[:, :], eps[:, :], ALU.add).then_inc(ve_done, 1)
                pool.wait_ge(ve_done, t + 1)
                pool.tensor_tensor(r[:, :], ve[:, :], half_pow[:, :], ALU.pow).then_inc(r_done, 1)
                pool.wait_ge(conv_done, t + 2)
                pool.tensor_tensor(mix[s][:, 1, :], conv[:, :], gbc[s][:, 0, :], ALU.mult)
                pool.wait_ge(on_done, t + 2)
                pool.wait_ge(gg_done, t + 1)
                pool.tensor_tensor(mix[s][:, 3, :], o_n[:, :], gg[:, :], ALU.mult).then_inc(mixed, 1)

            for t in range(2):
                join(t, t)
            for t, s, j in tile_pairs(pool):
                if not (isinstance(t, int) and t + 2 > LAST):
                    join(t + 2, s)

        @block.scalar
        def _(act):
            for s in range(2):
                act.sem_inc(sent[s], 16)
            act.sem_inc(sq_done, 1)
            act.wait_ge(gn_in, 16)
            act.activation(gn8[:, :], gn[:, :], ACT.Copy, scale=8.0).then_inc(gn_done, 1)

            def square(t, s):
                act.wait_ge(o_sum, t + 1)
                act.wait_ge(ss_done, t + 1)
                act.activation(o_sq[:, :], o[:, :], ACT.Square).then_inc(sq_done, 1)

            def high(t, s, _):
                act.wait_ge(mm, t * 2 + 2)
                for b in range(2):
                    act.wait_ge(turned, t * 2 + b + 5)
                    act.activation(y_hi[s][:, 4 * b:4 * b + 4, :], ps_t[b][:, :, :], ACT.Copy).then_inc(hi_done, 1)

            square(0, 0)
            square(1, 1)
            for n, (h, m) in enumerate(PIECES):
                if n == len(PIECES) // 2:
                    high(0, 0, 0)
                act.wait_ge(w_in[n % 4], 64 * (n // 4 + 1))
                act.activation(w_hi[:, 2 * m:2 * m + 2, 512 * h:512 * h + 512], stage_w[n % 4][:, :, :], ACT.Copy).then_inc(w_hi_done, 1)
            for t, s, j in tile_pairs(act):
                prepare_next(high, t, s)
                if not (isinstance(t, int) and t + 2 > LAST):
                    square(t + 2, s)
                act.wait_ge(added, t * 2 + 6)
                act.dma_start(token_rows(io, "y_sample", "y_prompt", t, j), y[s][:, :]).then_inc(sent[s], 16)
            for s in range(2):
                act.wait_ge(sent[s], 16 + 16 * (N_TOK // P // 2))

        @block.tensor
        def _(pe):
            pe.sem_inc(mm, 4)
            pe.sem_inc(turned, 4)

            def turn(t, s, _):
                pe.wait_ge(mixed, t + 2)
                pe.wait_ge(lo_done, t * 2 + 2)
                for b in range(2):
                    for n in range(4):
                        c = 4 * b + n
                        last = pe.transpose(ps_t[b][:, n, :], mix[s][:, c // 2, (c % 2) * P:(c % 2) * P + P], keep["ident"][:, :])
                    last.then_inc(turned, 1)

            turn(0, 0, 0)
            for t, s, j in tile_pairs(pe):
                pe.wait_ge(lo_done, t * 2 + 4)
                for h in range(2):
                    pe.wait_ge(gated, t * 2 + h + 1)
                    pe.wait_ge(w_lo_done, (h + 1) * len(PIECES) // 2)
                    cols = slice(h * 512, h * 512 + 512)
                    product(pe, ps_y[s][h][:, :], lambda k: y_hi[s][:, k, :], lambda k: y_lo[s][:, k, :],
                            lambda k: w_hi[:, k, cols], lambda k: w_lo[:, k, cols]).then_inc(mm, 1)
                    if h == 0:
                        prepare_next(turn, t, s)

        @block.vector
        def _(dve):
            dve.sem_inc(gated, 4)
            dve.sem_inc(on_done, 1)
            dve.sem_inc(ss_done, 1)
            dve.sem_inc(lo_done, 2)
            dve.sem_inc(conv_done, 1)
            dve.sem_inc(added, 4)

            def combine(t, s):
                heads = lambda a: a.rearrange("t (h d) -> t h d", d=HD)
                dve.wait_ge(mix_in[s], (t - s) * (LOADS * 8) + LOADS * 16)
                dve.wait_ge(sq_done, t + 1)
                dve.wait_ge(on_done, t + 1)
                dve.tensor_tensor(o[:, :], od[s][:, 0, :], od[s][:, 1, :], ALU.add).then_inc(o_sum, 1)
                dve.wait_ge(conv_done, t + 1)
                dve.tensor_tensor(u_w[:, :, :], u[s][:, :, :], taps[:, :, :], ALU.mult).then_inc(uw_done, 1)
                dve.wait_ge(sq_done, t + 2)
                dve.tensor_reduce(ss[:, :], heads(o_sq[:, :]), AX.X, ALU.add).then_inc(ss_done, 1)
                dve.wait_ge(mixed, t + 1)
                dve.wait_ge(uw_done, t + 1)
                dve.tensor_reduce(conv[:, :], u_w[:, :, :].rearrange("p a c -> p c a"), AX.X, ALU.add).then_inc(conv_done, 1)
                dve.wait_ge(r_done, t + 1)
                dve.tensor_tensor(heads(o_n[:, :]), heads(o[:, :]), r[:, :].unsqueeze(2).broadcast_to([P, NH, HD]),
                                  ALU.mult).then_inc(on_done, 1)

            def low(t, s, _):
                for b in range(2):
                    dve.wait_ge(hi_done, t * 2 + b + 1)
                    dve.tensor_tensor(y_lo[s][:, 4 * b:4 * b + 4, :], ps_t[b][:, :, :], y_hi[s][:, 4 * b:4 * b + 4, :],
                                      ALU.subtract).then_inc(lo_done, 1)

            dve.wait_ge(taps_in, 16)
            combine(0, 0)
            combine(1, 1)
            for n, (h, m) in enumerate(PIECES):
                if n == len(PIECES) // 2:
                    low(0, 0, 0)
                part = slice(2 * m, 2 * m + 2), slice(512 * h, 512 * h + 512)
                dve.wait_ge(w_hi_done, n + 1)
                dve.tensor_tensor(w_lo[:, part[0], part[1]], stage_w[n % 4][:, :, :], w_hi[:, part[0], part[1]],
                                  ALU.subtract).then_inc(w_lo_done, 1)
            dve.wait_ge(small_in, 32)
            for t, s, j in tile_pairs(dve):
                prepare_next(low, t, s)
                dve.wait_ge(x_in[s], (t - s) * 8 + 16)
                for h in range(2):
                    if h and not (isinstance(t, int) and t + 2 > LAST):
                        combine(t + 2, s)
                    cols = slice(h * 512, h * 512 + 512)
                    dve.wait_ge(mm, t * 2 + h + 5)
                    dve.wait_ge(added, t * 2 + h + 1)
                    dve.tensor_tensor(gx[s][:, cols], ps_y[s][h][:, :], gate[:, j, cols], ALU.mult).then_inc(gated, 1)
                    dve.wait_ge(gated, t * 2 + h + 5)
                    dve.wait_ge(sent[s], (t - s) * 8 + 16)
                    dve.tensor_tensor(y[s][:, cols], gx[s][:, cols], x[s][:, cols], ALU.add).then_inc(added, 1)


def build(nc, io):
    with ExitStack() as ctx:
        sb = lambda name, shape: ctx.enter_context(nc.sbuf_tensor(name, shape, F32))
        keep = {"ident": sb("ident", [P, P])}
        modulation_stage(nc, io, keep)
        projection_stage(nc, io, keep, 0)
        projection_stage(nc, io, keep, 1)
        attention_scan_stage(nc, io, keep)
        fourier_stage(nc, io, keep)
        output_stage(nc, io, keep)


def dft_tables():
    wave = lambda a, b, n: 2 * np.pi * ((np.outer(a, b) % n) / n)
    r = np.arange(64)
    s64, sg = 64 ** -0.5, 8.0
    eye2 = np.eye(2)
    dft64 = np.concatenate([np.kron(eye2, np.cos(wave(r, r, 64)) / sg), np.kron(eye2, -np.sin(wave(r, r, 64)) / sg)], 1)
    c, s = np.cos(wave(r, r, 64)) * s64, np.sin(wave(r, r, 64)) * s64
    first = np.block([[c, -s], [s, c]])
    second = np.zeros((128, 64, 64))
    for k1 in range(64):
        ph = wave(r, k1 + 64 * r, N_GRID)
        second[:64, k1], second[64:, k1] = np.cos(ph) * s64, np.sin(ph) * s64
    n = np.arange(N_PROMPT)
    ph = wave(n, n, N_PROMPT)
    whole = np.stack([np.cos(ph), np.sin(ph)]) * N_PROMPT ** -0.5
    return {"dft64": dft64, "dft_first": first, "dft_second": second, "dft_whole": whole}


NAMES = ["x_prompt", "x_sample", "cache_k", "cache_v", "state_gla", "c", "c_ctx", "norm_g", "w_mod", "b_mod",
         "w_in", "q_norm_g", "k_norm_g", "rpb", "conv_w", "gla_up_f", "gla_bias_f", "gla_up_b", "gla_bias_b",
         "gla_norm_g", "w_out"]
OUTPUTS = [("y_prompt", (1, N_PROMPT, DM)), ("y_sample", (1, N_GRID, DM)), ("new_cache_k", (1, 1, NH, N_PROMPT, HD)),
           ("new_cache_v", (1, 1, NH, N_PROMPT, HD)), ("new_state_gla", (1, 1, 2, NH, HD, HD))]
SCRATCH = [("mod", (2, 3 * DM)), ("p1", (N_TOK, P1_W)), ("a_t", (2 * RANK, N_TOK)), ("qkt", (4, P, N_TOK)), ("conv_u", (N_TOK + 3, W_GRP)),
           ("gates_bc", (N_TOK, 2 * W_GRP)), ("g", (2, N_TOK, W_GRP)), ("ya", (N_TOK // GRID_W, P, 2, HD)), ("toep", (NH * (2 * WIN_H - 1), GRID_W, P)),
           ("y1", (P, 64, W_GRP)), ("yc", (N_TOK, W_GRP)), ("od", (2, N_TOK, W_GRP))]


def kernel(**inputs):
    import concourse.bacc as bacc
    from concourse.bass_utils import run_bass_kernel_spmd

    nc = bacc.Bacc("TRN2", target_bir_lowering=False, num_devices=1)
    arrays, io = {}, {}
    for name in NAMES:
        arrays["in_" + name] = np.ascontiguousarray(inputs[name])
    for name, table in dft_tables().items():
        arrays["in_" + name] = np.ascontiguousarray(table.astype(np.float32))
    for name, a in arrays.items():
        io[name[3:]] = nc.dram_tensor(name, a.shape, F32, kind="ExternalInput").ap()
    for name, shape in OUTPUTS:
        io[name] = nc.dram_tensor("out_" + name, shape, F32, kind="ExternalOutput").ap()
    for name, shape in SCRATCH:
        io[name] = nc.dram_tensor("s_" + name, shape, F32, kind="Internal").ap()
    build(nc, io)
    got = run_bass_kernel_spmd(nc, [arrays], core_ids=[0]).results[0]
    return tuple(got["out_" + name] for name, _ in OUTPUTS)
```
